# Optimizing a Trainium2 kernel written in Bass

```python
import math
import jax
import jax.numpy as jnp
from jax import lax
import numpy as np

D_MODEL = 1024
BATCH = 1
SEQ = 512
DEPTH = 2

GRID_W = 64
CTX_LEN = 256
EPS = 1e-6
N_MOD = 6

HY_WIDTH = 512
HY_ORDER = 2
HY_BANDS = 16
HY_EMB = 1 + 2 * HY_BANDS
HY_FFN = 64
SHORT_K = 3
HY_FAST_DECAY = 0.3
HY_SLOW_DECAY = 1.5
HY_TARGET = 1e-2

MLA_HEADS = 8
QK_NOPE = 64
QK_ROPE = 32
V_DIM = 64
Q_LORA = 384
KV_LORA = 256
ROPE_PAIRS = QK_ROPE // 4
ROPE_BASE = 10000.0
ATTN_SCALE = (QK_NOPE + QK_ROPE) ** -0.5
Q_BLOCK = 128

N_GROUPS = 8
EXP_PER_GROUP = 8
N_EXPERTS = N_GROUPS * EXP_PER_GROUP
TOP_K = 2
D_EXPERT = 256
MOE_BLOCK = 128

HY_COLS = (HY_ORDER + 1) * HY_WIDTH
MLA_END = HY_COLS + Q_LORA + KV_LORA + QK_ROPE
IN_COLS = MLA_END + 2 * D_MODEL

kernel_name = "hyena_mla_hier_moe_dit_trunk"

def rmsnorm(x, g):
    xf = x.astype(jnp.float32)
    y = xf * lax.rsqrt(jnp.mean(xf * xf, axis=-1, keepdims=True) + EPS)
    return (y * g.astype(jnp.float32)).astype(x.dtype)

def modulate(h, g, shift, scale):
    return rmsnorm(h, g) * (1 + scale) + shift

def axial_rope_tables(L):
    rows = L // GRID_W
    r, col = jnp.meshgrid(jnp.arange(rows), jnp.arange(GRID_W), indexing="ij")
    pos = jnp.stack([r.reshape(-1), col.reshape(-1)], axis=-1).astype(jnp.float32)
    inv = ROPE_BASE ** (-jnp.arange(ROPE_PAIRS, dtype=jnp.float32) / ROPE_PAIRS)
    ang = pos[:, :, None] * inv
    return jnp.cos(ang), jnp.sin(ang)

def apply_axial_rope(x, cos, sin):
    shp = x.shape
    xa = x.reshape(shp[:-1] + (2, 2, ROPE_PAIRS))
    x1, x2 = xa[..., 0, :], xa[..., 1, :]
    bshape = (shp[1],) + (1,) * (x.ndim - 3) + (2, ROPE_PAIRS)
    cs = cos.reshape(bshape).astype(x.dtype)
    sn = sin.reshape(bshape).astype(x.dtype)
    return jnp.stack([x1 * cs - x2 * sn, x1 * sn + x2 * cs], axis=-2).reshape(shp)

def short_conv(z, w, b):
    L = z.shape[1]
    pad = SHORT_K // 2
    zp = jnp.pad(z, ((0, 0), (pad, pad), (0, 0)))
    out = b + zp[:, 0:L] * w[0]
    for k in range(1, SHORT_K):
        out = out + zp[:, k:k + L] * w[k]
    return out

def hyena_filters(L, w1, b1, freq, w2, b2, w3):
    f32 = jnp.float32
    t = jnp.linspace(0.0, 1.0, L, dtype=f32)[:, None]
    w = 2.0 * math.pi * jnp.arange(L, dtype=f32)[:, None] / L
    bands = jnp.linspace(1e-4, HY_BANDS - 1, HY_BANDS, dtype=f32)[None, :]
    z = jnp.concatenate([t, jnp.cos(bands * w), -jnp.sin(bands * w)], axis=-1)
    fr = freq.astype(f32)
    h = jnp.sin(fr * (z @ w1.astype(f32) + b1.astype(f32)))
    h = jnp.sin(fr * (h @ w2.astype(f32) + b2.astype(f32)))
    h = (h @ w3.astype(f32)).reshape(L, HY_ORDER, 2, HY_WIDTH)
    deltas = jnp.linspace(math.log(HY_TARGET) / HY_FAST_DECAY, math.log(HY_TARGET) / HY_SLOW_DECAY,
                          HY_WIDTH, dtype=f32)
    h = h * jnp.exp(-t[:, :, None, None] * jnp.abs(deltas))
    h = h * lax.rsqrt(jnp.sum(h * h, axis=0, keepdims=True) + EPS)
    h_fwd, h_bwd = h[:, :, 0], h[:, :, 1]
    circ = jnp.concatenate([h_fwd, jnp.zeros_like(h_fwd[:1]), h_bwd[1:][::-1]], axis=0)
    return jnp.fft.rfft(circ, axis=0)

def long_conv(z, h_freq):
    L = z.shape[1]
    zf = jnp.fft.rfft(z.astype(jnp.float32), n=2 * L, axis=1)
    return jnp.fft.irfft(zf * h_freq, n=2 * L, axis=1)[:, :L].astype(z.dtype)

def hyena_branch(p_hy, sc_w, sc_b, flt, flt_bias):
    L = p_hy.shape[1]
    u = short_conv(p_hy, sc_w, sc_b)
    v, x1, x2 = jnp.split(u, 3, axis=-1)
    h_freq = hyena_filters(L, *flt)
    z = v
    for o, gate in enumerate((x1, x2)):
        z = gate * (long_conv(z, h_freq[:, o]) + flt_bias[o] * z)
    return z

def mla_queries(p_q, q_norm_g, w_uq):
    B, L, _ = p_q.shape
    q = (rmsnorm(p_q, q_norm_g) @ w_uq).reshape(B, L, MLA_HEADS, QK_NOPE + QK_ROPE)
    return q[..., :QK_NOPE], q[..., QK_NOPE:]

def mla_keys_values(p_kv, kv_norm_g, w_ukv):
    B, L, _ = p_kv.shape
    c_kv, k_rope = p_kv[..., :KV_LORA], p_kv[..., KV_LORA:]
    kv = (rmsnorm(c_kv, kv_norm_g) @ w_ukv).reshape(B, L, MLA_HEADS, QK_NOPE + V_DIM)
    return kv[..., :QK_NOPE], kv[..., QK_NOPE:], k_rope

def ctx_attention(qn, qr, kn, kr, v):
    s = jnp.einsum("bqhd,bkhd->bhqk", qn, kn) + jnp.einsum("bqhr,bkr->bhqk", qr, kr)
    p = jax.nn.softmax(s.astype(jnp.float32) * ATTN_SCALE, axis=-1).astype(v.dtype)
    B, C = qn.shape[:2]
    return jnp.einsum("bhqk,bkhd->bqhd", p, v).reshape(B, C, MLA_HEADS * V_DIM)

def latent_attention(qn, qr_rot, qr_raw, kn, kr_rot, v, kn_c, kr_c, v_c):
    B, L = qn.shape[:2]
    nb = L // Q_BLOCK

    def blockify(t):
        return jnp.moveaxis(t.reshape((B, nb, Q_BLOCK) + t.shape[2:]), 1, 0)

    def one_block(args):
        bqn, bqr, bqr0 = args
        s_lat = jnp.einsum("bqhd,bkhd->bhqk", bqn, kn) + jnp.einsum("bqhr,bkr->bhqk", bqr, kr_rot)
        s_ctx = jnp.einsum("bqhd,bkhd->bhqk", bqn, kn_c) + jnp.einsum("bqhr,bkr->bhqk", bqr0, kr_c)
        s = jnp.concatenate([s_lat, s_ctx], axis=-1).astype(jnp.float32) * ATTN_SCALE
        p = jax.nn.softmax(s, axis=-1).astype(v.dtype)
        return (jnp.einsum("bhqk,bkhd->bqhd", p[..., :L], v)
                + jnp.einsum("bhqk,bkhd->bqhd", p[..., L:], v_c))

    out = lax.map(one_block, (blockify(qn), blockify(qr_rot), blockify(qr_raw)))
    return jnp.moveaxis(out, 0, 1).reshape(B, L, MLA_HEADS * V_DIM)

def merge_branches(p_gate, y_hy, y_att, w_hy_o, w_mla_o, w_out):
    g = jax.nn.sigmoid(p_gate)
    return (g[..., :D_MODEL] * (y_hy @ w_hy_o) + g[..., D_MODEL:] * (y_att @ w_mla_o)) @ w_out

def grouped_experts(t, expert, weight, w_gate, w_up, w_down):
    T = t.shape[0]
    A = expert.shape[0]
    token = jnp.repeat(jnp.arange(T, dtype=jnp.int32), TOP_K)
    order = jnp.argsort(expert)
    e_sorted = expert[order]
    counts = jnp.zeros((N_EXPERTS,), jnp.int32).at[expert].add(1)
    padded = (counts + MOE_BLOCK - 1) // MOE_BLOCK * MOE_BLOCK
    start = jnp.cumsum(counts) - counts
    p_end = jnp.cumsum(padded)
    p_start = p_end - padded
    dest = p_start[e_sorted] + jnp.arange(A, dtype=jnp.int32) - start[e_sorted]
    n_blocks = -(-A // MOE_BLOCK) + N_EXPERTS
    slots = n_blocks * MOE_BLOCK
    slot_token = jnp.full((slots,), T, jnp.int32).at[dest].set(token[order])
    slot_weight = jnp.zeros((slots,), weight.dtype).at[dest].set(weight[order])
    block_expert = jnp.minimum(
        jnp.searchsorted(p_end, jnp.arange(n_blocks, dtype=jnp.int32) * MOE_BLOCK, side="right"),
        N_EXPERTS - 1)
    t_pad = jnp.concatenate([t, jnp.zeros((1, t.shape[1]), t.dtype)], axis=0)

    def run_block(args):
        e, tok, wt = args
        xb = t_pad[tok]
        hb = jax.nn.silu(xb @ w_gate[e]) * (xb @ w_up[e])
        return (hb @ w_down[e]) * wt[:, None].astype(t.dtype)

    yb = lax.map(run_block, (block_expert, slot_token.reshape(n_blocks, MOE_BLOCK),
                             slot_weight.reshape(n_blocks, MOE_BLOCK)))
    y = jnp.zeros_like(t_pad).at[slot_token].add(yb.reshape(slots, t.shape[1]))
    return y[:T]

def hier_moe(u, w_rg, b_rg, w_re, b_re, w_gate, w_up, w_down):
    shp = u.shape
    t = u.reshape(-1, D_MODEL)
    T = t.shape[0]
    lg = (t @ w_rg).astype(jnp.float32)
    g_sel = jnp.argmax(lg + b_rg.astype(jnp.float32), axis=-1)
    p_g = jnp.take_along_axis(jax.nn.softmax(lg, axis=-1), g_sel[:, None], axis=-1)
    le = (t @ w_re).astype(jnp.float32).reshape(T, N_GROUPS, EXP_PER_GROUP)
    le_g = jnp.take_along_axis(le, g_sel[:, None, None], axis=1)[:, 0]
    be_g = b_re.astype(jnp.float32).reshape(N_GROUPS, EXP_PER_GROUP)[g_sel]
    _, local = lax.top_k(le_g + be_g, TOP_K)
    w_local = jax.nn.softmax(jnp.take_along_axis(le_g, local, axis=-1), axis=-1)
    expert = (g_sel[:, None] * EXP_PER_GROUP + local).astype(jnp.int32)
    weight = p_g * w_local
    y = grouped_experts(t, expert.reshape(-1), weight.reshape(-1), w_gate, w_up, w_down)
    return y.reshape(shp)

def setup_inputs(seed: int = 0) -> dict:
    key = jax.random.key(seed)
    ks = iter(jax.random.split(key, 40))

    def nrm(shape, scale):
        return jax.random.normal(next(ks), shape, jnp.float32) * scale

    def gain(shape):
        return 1.0 + nrm(shape, 0.05)

    return {
        "x": nrm((BATCH, SEQ, D_MODEL), 1.0),
        "c": nrm((BATCH, D_MODEL), 1.0),
        "ctx": nrm((BATCH, CTX_LEN, D_MODEL), 1.0),
        "c_ctx": nrm((D_MODEL,), 1.0),
        "w_ada": nrm((DEPTH, D_MODEL, N_MOD * D_MODEL), 0.5 * D_MODEL ** -0.5),
        "b_ada": nrm((DEPTH, N_MOD * D_MODEL), 0.02),
        "norm1_g": gain((DEPTH, D_MODEL)),
        "w_in": nrm((DEPTH, D_MODEL, IN_COLS), D_MODEL ** -0.5),
        "q_norm_g": gain((DEPTH, Q_LORA)),
        "kv_norm_g": gain((DEPTH, KV_LORA)),
        "w_uq": nrm((DEPTH, Q_LORA, MLA_HEADS * (QK_NOPE + QK_ROPE)), Q_LORA ** -0.5),
        "w_ukv": nrm((DEPTH, KV_LORA, MLA_HEADS * (QK_NOPE + V_DIM)), KV_LORA ** -0.5),
        "sc_w": nrm((DEPTH, SHORT_K, HY_COLS), SHORT_K ** -0.5),
        "sc_b": nrm((DEPTH, HY_COLS), 0.02),
        "flt_w1": nrm((DEPTH, HY_EMB, HY_FFN), HY_EMB ** -0.5),
        "flt_b1": nrm((DEPTH, HY_FFN), 0.1),
        "flt_freq": gain((DEPTH, HY_FFN)),
        "flt_w2": nrm((DEPTH, HY_FFN, HY_FFN), HY_FFN ** -0.5),
        "flt_b2": nrm((DEPTH, HY_FFN), 0.1),
        "flt_w3": nrm((DEPTH, HY_FFN, HY_ORDER * 2 * HY_WIDTH), HY_FFN ** -0.5),
        "flt_bias": nrm((DEPTH, HY_ORDER, HY_WIDTH), 0.5),
        "w_hy_o": nrm((DEPTH, HY_WIDTH, D_MODEL), HY_WIDTH ** -0.5),
        "w_mla_o": nrm((DEPTH, MLA_HEADS * V_DIM, D_MODEL), (MLA_HEADS * V_DIM) ** -0.5),
        "w_out": nrm((DEPTH, D_MODEL, D_MODEL), D_MODEL ** -0.5),
        "norm2_g": gain((DEPTH, D_MODEL)),
        "w_router_g": nrm((DEPTH, D_MODEL, N_GROUPS), D_MODEL ** -0.5),
        "b_router_g": nrm((DEPTH, N_GROUPS), 0.01),
        "w_router_e": nrm((DEPTH, D_MODEL, N_EXPERTS), D_MODEL ** -0.5),
        "b_router_e": nrm((DEPTH, N_EXPERTS), 0.01),
        "w_gate_e": nrm((DEPTH, N_EXPERTS, D_MODEL, D_EXPERT), D_MODEL ** -0.5),
        "w_up_e": nrm((DEPTH, N_EXPERTS, D_MODEL, D_EXPERT), D_MODEL ** -0.5),
        "w_down_e": nrm((DEPTH, N_EXPERTS, D_EXPERT, D_MODEL), D_EXPERT ** -0.5),
        "final_g": gain((D_MODEL,)),
    }

def reference(x, c, ctx, c_ctx, w_ada, b_ada, norm1_g, w_in, q_norm_g, kv_norm_g, w_uq, w_ukv,
              sc_w, sc_b, flt_w1, flt_b1, flt_freq, flt_w2, flt_b2, flt_w3, flt_bias,
              w_hy_o, w_mla_o, w_out, norm2_g, w_router_g, b_router_g, w_router_e, b_router_e,
              w_gate_e, w_up_e, w_down_e, final_g):
    L = x.shape[1]
    cos, sin = axial_rope_tables(L)
    s_x = jax.nn.silu(c)
    s_c = jax.nn.silu(c_ctx)
    hx, hc = x, ctx
    for l in range(DEPTH):
        last = l == DEPTH - 1
        mx = (s_x @ w_ada[l] + b_ada[l])[:, None, :]
        mc = s_c @ w_ada[l] + b_ada[l]
        sh1x, sc1x, g1x, sh2x, sc2x, g2x = jnp.split(mx, N_MOD, axis=-1)
        sh1c, sc1c, g1c, sh2c, sc2c, g2c = jnp.split(mc, N_MOD, axis=-1)
        flt = (flt_w1[l], flt_b1[l], flt_freq[l], flt_w2[l], flt_b2[l], flt_w3[l])

        ux = modulate(hx, norm1_g[l], sh1x, sc1x)
        uc = modulate(hc, norm1_g[l], sh1c, sc1c)
        px = ux @ w_in[l]
        pc = None if last else uc @ w_in[l]
        pc_mla = uc @ w_in[l][:, HY_COLS:MLA_END] if last else pc[..., HY_COLS:MLA_END]
        kn_c, v_c, kr_c = mla_keys_values(pc_mla[..., Q_LORA:], kv_norm_g[l], w_ukv[l])

        qn_x, qr_x = mla_queries(px[..., HY_COLS:HY_COLS + Q_LORA], q_norm_g[l], w_uq[l])
        kn_x, v_x, kr_x = mla_keys_values(px[..., HY_COLS + Q_LORA:MLA_END], kv_norm_g[l], w_ukv[l])
        att_x = latent_attention(qn_x, apply_axial_rope(qr_x, cos, sin), qr_x,
                                 kn_x, apply_axial_rope(kr_x, cos, sin), v_x, kn_c, kr_c, v_c)
        hy_x = hyena_branch(px[..., :HY_COLS], sc_w[l], sc_b[l], flt, flt_bias[l])
        hx = hx + g1x * merge_branches(px[..., MLA_END:], hy_x, att_x, w_hy_o[l], w_mla_o[l], w_out[l])
        if not last:
            qn_c, qr_c = mla_queries(pc[..., HY_COLS:HY_COLS + Q_LORA], q_norm_g[l], w_uq[l])
            att_c = ctx_attention(qn_c, qr_c, kn_c, kr_c, v_c)
            hy_c = hyena_branch(pc[..., :HY_COLS], sc_w[l], sc_b[l], flt, flt_bias[l])
            hc = hc + g1c * merge_branches(pc[..., MLA_END:], hy_c, att_c, w_hy_o[l], w_mla_o[l], w_out[l])

        moe_w = (w_router_g[l], b_router_g[l], w_router_e[l], b_router_e[l],
                 w_gate_e[l], w_up_e[l], w_down_e[l])
        hx = hx + g2x * hier_moe(modulate(hx, norm2_g[l], sh2x, sc2x), *moe_w)
        if not last:
            hc = hc + g2c * hier_moe(modulate(hc, norm2_g[l], sh2c, sc2c), *moe_w)
    return rmsnorm(hx, final_g)


_drawn_inputs = setup_inputs


def setup_inputs(seed=0):
    import zlib

    import numpy as np

    out = dict(_drawn_inputs(seed))
    spreads = {}
    factors = {'ctx': 5.031,
     'q_norm_g': 8.0,
     'kv_norm_g': 8.0,
     'w_uq': 3.193,
     'norm2_g': 3.059,
     'b_router_g': 8.0,
     'b_router_e': 8.0}
    for name, (base, spread) in spreads.items():
        noise = np.random.default_rng([zlib.crc32(name.encode()), seed]).standard_normal(out[name].shape)
        drawn = base * np.exp(spread * noise) if base else spread * noise
        out[name] = jnp.asarray(drawn.astype(out[name].dtype))
    for name, factor in factors.items():
        out[name] = (out[name] * factor).astype(out[name].dtype)
    return out
```

```python
import math
from contextlib import ExitStack, contextmanager

import concourse.bass as bass
from concourse import mybir
import numpy as np

F32 = mybir.dt.float32
I32 = mybir.dt.int32
ACT = mybir.ActivationFunctionType
ALU = mybir.AluOpType
AX = mybir.AxisListType

P = 128
D = 1024
KC = D // P
SEQ, CTX = 512, 256
TOK = SEQ + CTX
XT, CT = SEQ // P, CTX // P
TT = TOK // P
DEPTH = 2
EPS = 1e-6
N_MOD = 6
GRID_W = 64

HW = 512
HC = HW // P
BANDS, EMB, FFN = 16, 33, 64
HY_COLS = 3 * HW
DECAY_FAST, DECAY_SLOW, DECAY_TARGET = 0.3, 1.5, 1e-2

HEADS, NOPE, ROPE, VD = 8, 64, 32, 64
QK = NOPE + ROPE
QL, KVL = 384, 256
QC, KVC = QL // P, KVL // P
PAIRS = ROPE // 4
SCALE = QK ** -0.5
Q0 = HY_COLS
KR0 = Q0 + QL + KVL
G0 = KR0 + ROPE
IN_COLS = G0 + 2 * D

NG, EG = 8, 8
NE = NG * EG
DE = 256
SLOTS = P
RU = 4

R_G1, R_G2, R_ADA, R_QG, R_KVG, R_SCW, R_SCB = 0, 8, 16, 64, 67, 69, 105
R_ALL = 117
RG_C, RG_CC, RG_F, RG_ALL = 0, 8, 16, 24


def layout_constants():
    out = {"ident": np.eye(P, dtype=np.float32), "ones": np.ones((P, P), np.float32)}
    f = np.float32
    deltas = np.abs(np.linspace(math.log(DECAY_TARGET) / DECAY_FAST, math.log(DECAY_TARGET) / DECAY_SLOW,
                                HW).astype(f))
    for name, n in (("x", SEQ), ("c", CTX)):
        k = np.arange(n)
        ang = np.pi / n * ((k[:, None] * k[None, :]) % (2 * n))
        alt = np.where(k % 2 == 0, 1.0, -1.0)
        fwd_c, fwd_s = np.cos(ang), -np.sin(ang)
        fwd_s[:, 0] = alt
        inv_c, inv_s = np.cos(ang) / n, -np.sin(ang) / n
        inv_c[0] = 0.5 / n
        inv_s[0] = 0.5 * alt / n
        for tag, m in (("fc", fwd_c), ("fs", fwd_s), ("ic", inv_c), ("is", inv_s)):
            out[f"{tag}_{name}"] = m.astype(f)
        t = np.linspace(0.0, 1.0, n).astype(f)[:, None]
        w = (f(2.0 * math.pi) * np.arange(n, dtype=f)[:, None] / f(n)).astype(f)
        bands = np.linspace(1e-4, BANDS - 1, BANDS).astype(f)[None, :]
        bw = (bands * w).astype(f)
        out[f"feat_{name}"] = np.ascontiguousarray(np.concatenate([t, np.cos(bw), -np.sin(bw)], axis=1).T.astype(f))
        out[f"decay_{name}"] = np.exp(-t * deltas[None, :]).astype(f)
    rows = SEQ // GRID_W
    r, col = np.meshgrid(np.arange(rows), np.arange(GRID_W), indexing="ij")
    pos = np.stack([r.reshape(-1), col.reshape(-1)], axis=-1).astype(f)
    inv = (f(10000.0) ** (-np.arange(PAIRS, dtype=f) / f(PAIRS))).astype(f)
    ang = pos[:, :, None] * inv
    cs, sn = np.cos(ang).astype(f), np.sin(ang).astype(f)
    rope = np.zeros((P, SEQ), f)
    for a in range(2):
        for h in range(2):
            at = a * 2 * PAIRS + h * PAIRS
            rope[NOPE + at:NOPE + at + PAIRS] = cs[:, a].T
            rope[QK + at:QK + at + PAIRS] = (sn if h else -sn)[:, a].T
    out["rope"] = rope
    out["triu"] = np.triu(np.ones((P, P), f), 1)
    iota = np.zeros((P, 96), f)
    iota[:, 0:64] = np.arange(64)
    iota[:, 64:88] = np.arange(24)
    iota[:, 88] = np.arange(P)
    out["iota"] = iota
    return out


@contextmanager
def stage(nc, name, signals, buffers=()):
    with ExitStack() as ctx:
        mine = {n: ctx.enter_context(nc.sbuf_tensor(f"{name}_{n}", shape, dt[0] if dt else F32))
                for n, shape, *dt in buffers}
        sems = {n: nc.alloc_semaphore(f"{name}_{n}") for n in signals}
        with nc.Block() as block:
            yield block, {**mine, **sems}
        nc.clear_and_free_semaphores(list(sems.values()))
        nc.all_engine_barrier()


class Chain:

    def __init__(self, eng, sem, start=0):
        self.eng, self.sem, self.n = eng, sem, start

    def __call__(self, ins):
        self.n = self.n + 1
        ins.then_inc(self.sem, 1)
        self.eng.wait_ge(self.sem, self.n)


def refined_rsqrt(nc, link, root, var, tmp):
    link(nc.vector.reciprocal(root, root))
    link(nc.vector.tensor_tensor(tmp, root, root, ALU.mult))
    link(nc.vector.scalar_tensor_tensor(tmp, tmp, -0.5, var, ALU.mult, ALU.mult))
    link(nc.vector.scalar_tensor_tensor(root, tmp, 1.5, root, ALU.add, ALU.mult))


def spans(with_ctx):
    return ((0, 0, SEQ), (1, SEQ, CTX)) if with_ctx else ((0, 0, SEQ),)


def load_stage(nc, m, x, ctx, rows_l, rows_g, consts):
    with stage(nc, "load", ["tokens_in", "rows_in", "consts_in", "pe_done", "evac", "silu_done"],
               [("tok", [P, TT, D]), ("rows", [P, DEPTH + 1, P])]) as (block, s):
        @block.sync
        def _(sp):
            sp.dma_start(m.ident[:], consts["ident"]).then_inc(s["consts_in"], 16)
            sp.dma_start(m.ones[:], consts["ones"]).then_inc(s["consts_in"], 16)
            for l in range(DEPTH):
                for at, n, src in rows_l[l]:
                    sp.dma_start(s["rows"][at:at + n, l], src).then_inc(s["rows_in"], 16)
            for at, n, src in rows_g:
                sp.dma_start(s["rows"][at:at + n, DEPTH], src).then_inc(s["rows_in"], 16)
            for t in range(TT):
                src = x[0, t * P:(t + 1) * P] if t < XT else ctx[0, (t - XT) * P:(t - XT + 1) * P]
                sp.dma_start(s["tok"][:, t], src).then_inc(s["tokens_in"], 16)

        @block.tensor
        def _(pe):
            pe.wait_ge(s["consts_in"], 32)
            pe.wait_ge(s["rows_in"], 16 * (sum(len(r) for r in rows_l) + len(rows_g)))
            for l in range(DEPTH + 1):
                n = R_ALL if l < DEPTH else RG_ALL
                last = nc.tensor.transpose(m.ps[:, 7, l * P:l * P + n], s["rows"][0:n, l], m.ident[0:n, 0:n])
            last.then_inc(s["pe_done"], 1)
            pe.wait_ge(s["tokens_in"], 16 * TT)
            for t in range(TT):
                for half in range(2):
                    n = 2 * t + half
                    if n >= 4:
                        pe.wait_ge(s["evac"], n - 3)
                    for c in range(4):
                        k = half * 4 + c
                        last = nc.tensor.transpose(m.ps[:, n % 4, c * P:(c + 1) * P], s["tok"][:, t, k * P:(k + 1) * P],
                                                   m.ident[:])
                    last.then_inc(s["pe_done"], 1)

        @block.vector
        def _(dve):
            for n in range(2 * TT):
                t, half = n // 2, n % 2
                dve.wait_ge(s["pe_done"], n + 2)
                nc.vector.tensor_copy(m.resid[:, half * 4:half * 4 + 4, t * P:(t + 1) * P],
                                      m.ps[:, n % 4].rearrange("p (c t) -> p c t", c=4)).then_inc(s["evac"], 1)

        @block.scalar
        def _(act):
            act.wait_ge(s["pe_done"], 1)
            for l in range(DEPTH):
                nc.scalar.activation(m.cols[:, l, 0:R_ALL], m.ps[:, 7, l * P:l * P + R_ALL], ACT.Copy)
            nc.scalar.activation(m.gcols[:, 0:RG_ALL], m.ps[:, 7, DEPTH * P:DEPTH * P + RG_ALL],
                                 ACT.Copy).then_inc(s["silu_done"], 1)
            nc.scalar.activation(m.sil[:], m.ps[:, 7, DEPTH * P:DEPTH * P + 2 * KC].rearrange("p (s c) -> p c s", s=2),
                                 ACT.Silu)


def ada_stage(nc, m, w_ada):
    RING, COLS, BLOCKS = 3, 512, N_MOD * D // 512
    per = COLS // P
    with stage(nc, "ada", ["w0", "w1", "w2", "w_used", "pe_done", "chain"],
               [("w", [P, RING, KC, COLS])]) as (block, s):
        loaded = [s["w0"], s["w1"], s["w2"]]
        src = w_ada.rearrange("l (c p) n -> l p c n", p=P)

        @block.sync
        def _(sp):
            for l in range(DEPTH):
                with sp.Fori(0, BLOCKS // RING) as i:
                    for b in range(RING):
                        sp.wait_ge(s["w_used"], i * RING + (l * BLOCKS + b + 1))
                        sp.dma_start(s["w"][:, b], src[l, :, :, bass.ds((i * RING + b) * COLS, COLS)]).then_inc(loaded[b], 16)

        @block.tensor
        def _(pe):
            pe.sem_inc(s["w_used"], RING)
            for l in range(DEPTH):
                with pe.Fori(0, BLOCKS // RING) as i:
                    for b in range(RING):
                        pe.wait_ge(loaded[b], i * 16 + 16 * (l * (BLOCKS // RING) + 1))
                        for j in range(per):
                            for c in range(KC):
                                last = nc.tensor.matmul(m.ps[:, l, bass.ds((i * RING + b) * (2 * per) + 2 * j, 2)],
                                                        s["w"][:, b, c, j * P:(j + 1) * P], m.sil[:, c],
                                                        start=c == 0, stop=c == KC - 1)
                        last.then_inc(s["w_used"], 1)
            last = nc.tensor.matmul(m.ps[:, 2, 0:2], m.ident[:], m.sil[:, 0], start=True, stop=True)
            last.then_inc(s["pe_done"], 1)

        @block.vector
        def _(dve):
            dve.wait_ge(s["pe_done"], 1)
            link = Chain(dve, s["chain"])
            for l in range(DEPTH):
                got = m.ps[:, l, 0:2 * N_MOD * KC].rearrange("p (j s) -> p s j", s=2)
                for t in range(2):
                    last = nc.vector.tensor_tensor(m.mod[:, l, t], got[:, t], m.cols[:, l, R_ADA:R_ADA + N_MOD * KC],
                                                   ALU.add)
            link(last)
            for l in range(DEPTH):
                for t in range(2):
                    for k, (part, row) in enumerate(((1, R_G1), (4, R_G2))):
                        nc.vector.scalar_tensor_tensor(m.gain[:, l, t, k], m.mod[:, l, t, part * KC:(part + 1) * KC],
                                                       1.0, m.cols[:, l, row:row + KC], ALU.add, ALU.mult)


def norm_stage(nc, m, name, out, streams, gains, shifts):
    n_tok = sum(n for _, _, n in streams)
    with stage(nc, name, ["sq_done", "sum_done", "chain", "root_done", "scaled"],
               [("sq", [P, 2, TOK]), ("rstd", [P, TOK]), ("var", [P, TOK])]) as (block, s):
        r, var = s["rstd"][:, 0:n_tok], s["var"][:, 0:n_tok]

        @block.scalar
        def _(act):
            for c in range(KC):
                if c >= 2:
                    act.wait_ge(s["sum_done"], c - 1)
                nc.scalar.activation(s["sq"][:, c % 2, 0:n_tok], m.resid[:, c, 0:n_tok], ACT.Square).then_inc(s["sq_done"], 1)
            act.wait_ge(s["chain"], 1)
            nc.scalar.activation(r, var, ACT.Sqrt).then_inc(s["root_done"], 1)
            for c in range(KC):
                act.wait_ge(s["scaled"], c + 1)
                for t, at, n in streams:
                    o = out[:, c, at:at + n]
                    if shifts is None:
                        nc.scalar.activation(o, o, ACT.Identity, scale=gains(t, c))
                    else:
                        nc.scalar.activation(o, o, ACT.Identity, scale=gains(t, c), bias=shifts(t, c))

        @block.tensor
        def _(pe):
            for c in range(KC):
                pe.wait_ge(s["sq_done"], c + 1)
                for t, at, n in streams:
                    last = nc.tensor.matmul(m.ps[:, t, 0:n], m.ones[:], s["sq"][:, c % 2, at:at + n],
                                            start=c == 0, stop=c == KC - 1)
                last.then_inc(s["sum_done"], 1)

        @block.vector
        def _(dve):
            link = Chain(dve, s["chain"])
            dve.wait_ge(s["sum_done"], KC)
            for t, at, n in streams:
                last = nc.vector.tensor_scalar(s["var"][:, at:at + n], m.ps[:, t, 0:n], 1.0 / D, EPS, ALU.mult, ALU.add)
            link(last)
            dve.wait_ge(s["root_done"], 1)
            refined_rsqrt(nc, link, r, var, s["sq"][:, 0, 0:n_tok])
            for c in range(KC):
                nc.vector.tensor_tensor(out[:, c, 0:n_tok], m.resid[:, c, 0:n_tok], r, ALU.mult).then_inc(s["scaled"], 1)


def hyena_in_stage(nc, m, l, w_in, streams):
    n_tok = sum(n for _, _, n in streams)
    tiles = n_tok // P
    NT = 3 * HC
    PAD = TOK + 4
    first = {0: 1, 1: SEQ + 3}
    with stage(nc, f"hyin{l}", ["w0", "w1", "w_used", "mm_done", "p_done", "mid_done", "conv_done", "zeroed", "taps",
                                "tr_done", "tr_evac"],
               [("w", [P, 2, KC, HW]), ("p", [P, 2, PAD]), ("conv", [P, 2, TOK])]) as (block, s):
        loaded = [s["w0"], s["w1"]]
        src = w_in[l].rearrange("(c p) n -> p c n", p=P)

        def col(row, i):
            return m.cols[:, l, row + i:row + i + 1]

        @block.sync
        def _(sp):
            for g in range(3):
                if g == 2:
                    sp.wait_ge(s["mm_done"], HC)
                sp.dma_start(s["w"][:, g % 2], src[:, :, g * HW:(g + 1) * HW]).then_inc(loaded[g % 2], 16)

        @block.tensor
        def _(pe):
            def transposes(i):
                pe.wait_ge(s["conv_done"], i + 1)
                if i >= 1:
                    pe.wait_ge(s["tr_evac"], 2 * i)
                for j in range(tiles):
                    last = nc.tensor.transpose(m.ps[:, 4 + j // 4, (j % 4) * P:(j % 4 + 1) * P],
                                               s["conv"][:, i % 2, j * P:(j + 1) * P], m.ident[:])
                last.then_inc(s["tr_done"], 1)

            for i in range(NT):
                if i % HC == 0:
                    g = i // HC
                    pe.wait_ge(loaded[g % 2], 16 * (g // 2 + 1))
                if i >= 2:
                    pe.wait_ge(s["p_done"], i - 1)
                    pe.wait_ge(s["mid_done"], i - 1)
                for t, at, n in streams:
                    for c in range(KC):
                        last = nc.tensor.matmul(m.ps[:, 2 * (i % 2) + t, 0:n], s["w"][:, (i // HC) % 2, c, (i % HC) * P:(i % HC + 1) * P],
                                                m.u[:, c, at:at + n], start=c == 0, stop=c == KC - 1)
                last.then_inc(s["mm_done"], 1)
                if 1 <= i <= 2 * HC:
                    transposes(i - 1)

        @block.scalar
        def _(act):
            act.wait_ge(s["zeroed"], 1)
            for i in range(NT):
                act.wait_ge(s["mm_done"], i + 1)
                if i >= 2:
                    act.wait_ge(s["conv_done"], i - 1)
                for t, at, n in streams:
                    last = nc.scalar.activation(s["p"][:, i % 2, first[t]:first[t] + n], m.ps[:, 2 * (i % 2) + t, 0:n], ACT.Copy)
                last.then_inc(s["p_done"], 1)
                dst = s["conv"][:, i % 2] if i < 2 * HC else m.x2[:, i - 2 * HC]
                if 2 <= i < 2 * HC:
                    act.wait_ge(s["tr_done"], i - 1)
                for t, at, n in streams:
                    last = nc.scalar.activation(dst[:, at:at + n], m.ps[:, 2 * (i % 2) + t, 0:n], ACT.Identity,
                                                scale=col(R_SCW + NT, i), bias=col(R_SCB, i))
                last.then_inc(s["mid_done"], 1)
                if 2 <= i <= 2 * HC + 1:
                    k = i - 2
                    act.wait_ge(s["tr_done"], k + 1)
                    dst = m.v if k < HC else m.x1
                    for half in range(2):
                        a, b = 4 * half, min(4 * half + 4, tiles)
                        if a < b:
                            ins = nc.scalar.activation(dst[:, a:b, (k % HC) * P:(k % HC + 1) * P],
                                                       m.ps[:, 4 + half, 0:(b - a) * P].rearrange("p (j c) -> p j c", c=P),
                                                       ACT.Copy)
                            ins.then_inc(s["tr_evac"], 1 if tiles > 4 else 2)

        @block.vector
        def _(dve):
            nc.vector.memset(s["p"][:], 0.0).then_inc(s["zeroed"], 1)
            for i in range(NT):
                dst = s["conv"][:, i % 2] if i < 2 * HC else m.x2[:, i - 2 * HC]
                dve.wait_ge(s["mid_done"], i + 1)
                dve.wait_ge(s["p_done"], i + 1)
                for k, tap in enumerate((0, 2)):
                    for t, at, n in streams:
                        f = first[t] + tap - 1
                        last = nc.vector.scalar_tensor_tensor(dst[:, at:at + n], s["p"][:, i % 2, f:f + n],
                                                              col(R_SCW + tap * NT, i), dst[:, at:at + n],
                                                              ALU.mult, ALU.add)
                    if k == 0:
                        last.then_inc(s["taps"], 1)
                        dve.wait_ge(s["taps"], i + 1)
                last.then_inc(s["conv_done"], 1)


TWO_PI = 2.0 * math.pi
TWO_PI_HI = 6.28125
ROUND = 1.5 * 2.0 ** 23
PI_BELOW = 3.1415925


def conv_stage(nc, m, l, t, flt, consts):
    n, at, tag = (SEQ, 0, "x") if t == 0 else (CTX, SEQ, "c")
    J = n // P
    tok0 = at // P
    w1, b1, freq, w2, b2, w3, fbias = flt
    sems = ["mats_in", "small_in", "mm", "dve", "sines", "f_done", "sq_done", "h3_done", "sum_done", "var_done",
            "root_done", "fd_done", "unit_done", "h_done", "t_done", "y_done", "inv_done", "inv_evac", "t_used", "c0_done"]
    bufs = [("fc", [P, J, n]), ("fs", [P, J, n]), ("ic", [P, J, n]), ("is_", [P, J, n]), ("decay", [P, J, HW]),
            ("feat", [EMB, n]), ("w1", [EMB, FFN]), ("w2", [FFN, FFN]), ("w3", [FFN, 4 * HW]), ("vec", [FFN, 3]),
            ("bias", [1, 2, HW]), ("a", [FFN, n]), ("k", [FFN, n]), ("h", [FFN, n]),
            ("f", [P, 2, J, HW]),
            ("hr", [P, J, HW]), ("hi", [P, J, HW]), ("hc0", [P, HW]), ("t", [P, 4, HW])]
    with stage(nc, f"conv{l}{tag}", sems, bufs) as (block, s):
        sq, var, rn = s["t"][:, 0:2], s["t"][:, 2:4], s["hi"][:, 0:2]

        @block.sync
        def _(sp):
            for dst, src in ((s["feat"][:], consts[f"feat_{tag}"]), (s["w1"][:], w1), (s["w2"][:], w2), (s["w3"][:], w3),
                             (s["vec"][:, 0:1], b1[:, None]), (s["vec"][:, 1:2], freq[:, None]), (s["vec"][:, 2:3], b2[:, None]),
                             (s["bias"][0:1], fbias[None])):
                sp.dma_start(dst, src).then_inc(s["small_in"], 16)
            for dst, name in ((s["decay"], "decay"), (s["fc"], "fc"), (s["fs"], "fs"), (s["ic"], "ic"), (s["is_"], "is")):
                sp.dma_start(dst[:], consts[f"{name}_{tag}"].rearrange("(j p) k -> p j k", p=P)).then_inc(s["mats_in"], 16)

        def slot_free(eng, k):
            if k >= 2:
                o, r = divmod(k - 2, 2 * J)
                if r < J:
                    eng.wait_ge(s["h_done"], o * J + r + 1)
                else:
                    eng.wait_ge(s["t_done"], o * J + r - J + 1)

        @block.tensor
        def _(pe):
            mm, unit, h3 = 0, 0, 0
            pe.wait_ge(s["small_in"], 16 * 8)
            nc.tensor.matmul(m.ps[0:FFN, 0, 0:n], s["w1"][:], s["feat"][:], start=True, stop=True).then_inc(s["mm"], 1)
            pe.wait_ge(s["sines"], 1)
            nc.tensor.matmul(m.ps[0:FFN, 1, 0:n], s["w2"][:], s["h"][:], start=True, stop=True).then_inc(s["mm"], 1)
            pe.wait_ge(s["sines"], 2)
            for o in range(2):
                if o:
                    pe.wait_ge(s["inv_evac"], J)
                for q in range(2 * J):
                    e, j = divmod(q, J)
                    if q >= 2:
                        pe.wait_ge(s["f_done"], 2 * J * o + q - 1)
                    nc.tensor.matmul(m.ps[:, q % 2], s["h"][:, j * P:(j + 1) * P], s["w3"][:, (2 * o + e) * HW:(2 * o + e + 1) * HW],
                                     start=True, stop=True).then_inc(s["h3_done"], 1)
                    if q >= 1:
                        e, j = divmod(q - 1, J)
                        pe.wait_ge(s["sq_done"], 2 * J * o + q)
                        nc.tensor.matmul(m.ps[:, 2 + e], m.ones[:], sq[:, (q - 1) % 2], start=j == 0,
                                         stop=j == J - 1).then_inc(s["sum_done"], 1)
                pe.wait_ge(s["sq_done"], 2 * J * (o + 1))
                nc.tensor.matmul(m.ps[:, 3], m.ones[:], sq[:, 1], start=J == 1, stop=True).then_inc(s["sum_done"], 1)
                if o == 0:
                    pe.wait_ge(s["mats_in"], 16 * 5)
                pe.wait_ge(s["fd_done"], 2 * o + 2)
                for j in range(J):
                    slot_free(pe, unit)
                    b = 4 + 2 * (unit % 2)
                    for i in range(J):
                        nc.tensor.matmul(m.ps[:, b], s["fc"][:, i, j * P:(j + 1) * P], s["f"][:, 0, i], start=i == 0, stop=False)
                    nc.tensor.matmul(m.ps[:, b], m.ones[0:1], s["bias"][0:1, o], start=False, stop=True)
                    for i in range(J):
                        last = nc.tensor.matmul(m.ps[:, b + 1], s["fs"][:, i, j * P:(j + 1) * P], s["f"][:, 1, i],
                                                start=i == 0, stop=i == J - 1)
                    last.then_inc(s["unit_done"], 1)
                    unit += 1
                for i in range(J):
                    nc.tensor.matmul(m.ps[0:1, 0], s["fs"][:, i, 0:1], s["f"][:, 0, i], start=i == 0, stop=False)
                nc.tensor.matmul(m.ps[0:1, 0], m.ones[0:1, 0:1], s["bias"][0:1, o], start=False, stop=True).then_inc(s["mm"], 1)
                z = m.v if o == 0 else m.x1
                for j in range(J):
                    slot_free(pe, unit)
                    b = 4 + 2 * (unit % 2)
                    for mat, bank in ((s["fc"], b), (s["fs"], b + 1)):
                        for i in range(J):
                            last = nc.tensor.matmul(m.ps[:, bank], mat[:, i, j * P:(j + 1) * P], z[:, tok0 + i],
                                                    start=i == 0, stop=i == J - 1)
                    last.then_inc(s["unit_done"], 1)
                    unit += 1
                pe.wait_ge(s["c0_done"], o + 1)
                pe.wait_ge(s["y_done"], 2 * J * (o + 1))
                for q in range(J if o == 0 else HC):
                    if q >= 2:
                        pe.wait_ge(s["inv_evac"], J * o + q - 1)
                    for j in range(J):
                        for e, mat in ((0, s["ic"]), (1, s["is_"])):
                            first, stop = j == 0 and e == 0, j == J - 1 and e == 1
                            if o == 0:
                                last = nc.tensor.matmul(m.ps[:, q % 2], mat[:, j, q * P:(q + 1) * P], s["f"][:, e, j],
                                                        start=first, stop=stop)
                            else:
                                last = nc.tensor.matmul(m.ps[:, q % 2, 0:n], s["f"][:, e, j, q * P:(q + 1) * P], mat[:, j],
                                                        start=first, stop=stop)
                    last.then_inc(s["inv_done"], 1)

        @block.scalar
        def _(act):
            for k in range(2):
                act.wait_ge(s["dve"], 6 * (k + 1))
                nc.scalar.activation(s["h"][:], s["a"][:], ACT.Sin).then_inc(s["sines"], 1)
            for o in range(2):
                for q in range(2 * J):
                    e, j = divmod(q, J)
                    act.wait_ge(s["f_done"], 2 * J * o + q + 1)
                    if q >= 2:
                        act.wait_ge(s["sum_done"], 2 * J * o + q - 1)
                    nc.scalar.activation(sq[:, q % 2], s["f"][:, e, j], ACT.Square).then_inc(s["sq_done"], 1)
                act.wait_ge(s["var_done"], o + 1)
                nc.scalar.activation(rn, var, ACT.Sqrt).then_inc(s["root_done"], 1)
                for j in range(J):
                    unit = 2 * J * o + j
                    act.wait_ge(s["unit_done"], unit + 1)
                    if o:
                        act.wait_ge(s["t_done"], J)
                    b = 4 + 2 * (unit % 2)
                    nc.scalar.activation(s["hr"][:, j], m.ps[:, b], ACT.Copy)
                    if j == 0:
                        nc.scalar.activation(s["hc0"][:], m.ps[:, b], ACT.Copy)
                    nc.scalar.activation(s["hi"][:, j], m.ps[:, b + 1], ACT.Copy).then_inc(s["h_done"], 1)
                act.wait_ge(s["h_done"], J * (o + 1))
                act.wait_ge(s["mm"], 3 + o)
                nc.scalar.activation(s["hc0"][0:1], m.ps[0:1, 0], ACT.Copy)
                nc.scalar.mul(s["hi"][0:1, 0], s["hi"][0:1, 0], 0.0).then_inc(s["c0_done"], 1)

        @block.vector
        def _(dve):
            link = Chain(dve, s["dve"])
            for k in range(2):
                dve.wait_ge(s["mm"], k + 1)
                if k == 0:
                    dve.wait_ge(s["small_in"], 16 * 8)
                link(nc.vector.tensor_scalar(s["a"][:], m.ps[0:FFN, k, 0:n], s["vec"][:, 2 * k:2 * k + 1], s["vec"][:, 1:2],
                                             ALU.add, ALU.mult))
                link(nc.vector.tensor_scalar(s["k"][:], s["a"][:], 1.0 / TWO_PI, ROUND, ALU.mult, ALU.add))
                link(nc.vector.tensor_scalar_sub(s["k"][:], s["k"][:], ROUND))
                link(nc.vector.scalar_tensor_tensor(s["a"][:], s["k"][:], -TWO_PI_HI, s["a"][:], ALU.mult, ALU.add))
                link(nc.vector.scalar_tensor_tensor(s["a"][:], s["k"][:], -(TWO_PI - TWO_PI_HI), s["a"][:], ALU.mult, ALU.add))
                link(nc.vector.tensor_scalar(s["a"][:], s["a"][:], PI_BELOW, -PI_BELOW, ALU.min, ALU.max))
                if k == 0:
                    dve.wait_ge(s["sines"], 1)
            dve.wait_ge(s["mats_in"], 16 * 5)
            for o in range(2):
                if o:
                    dve.wait_ge(s["inv_done"], J)
                for q in range(2 * J):
                    e, j = divmod(q, J)
                    dve.wait_ge(s["h3_done"], 2 * J * o + q + 1)
                    nc.vector.tensor_tensor(s["f"][:, e, j], m.ps[:, q % 2], s["decay"][:, j], ALU.mult).then_inc(s["f_done"], 1)
                dve.wait_ge(s["sum_done"], 2 * J * (o + 1))
                nc.vector.tensor_scalar_add(var, m.ps[:, 2:4], EPS).then_inc(s["var_done"], 1)
                dve.wait_ge(s["root_done"], o + 1)
                refined_rsqrt(nc, link, rn, var, sq)
                for e in range(2):
                    for j in range(J):
                        last = nc.vector.tensor_tensor(s["f"][:, e, j], s["f"][:, e, j], rn[:, e], ALU.mult)
                link(last)
                link(nc.vector.memset(s["f"][0:1, 1, 0], 0.0))
                nc.vector.tensor_tensor(s["f"][:, 0], s["f"][:, 0], s["f"][:, 1], ALU.add).then_inc(s["fd_done"], 1)
                dve.wait_ge(s["fd_done"], 2 * o + 1)
                nc.vector.scalar_tensor_tensor(s["f"][:, 1], s["f"][:, 1], -2.0, s["f"][:, 0], ALU.mult, ALU.add).then_inc(s["fd_done"], 1)
                dve.wait_ge(s["c0_done"], o + 1)
                for j in range(J):
                    unit = 2 * J * o + J + j
                    b = 4 + 2 * (unit % 2)
                    dve.wait_ge(s["unit_done"], unit + 1)
                    if J * o + j >= 1:
                        dve.wait_ge(s["y_done"], 2 * (J * o + j))
                    zr, zi = m.ps[:, b], m.ps[:, b + 1]
                    nc.vector.tensor_tensor(s["t"][:, 0], zr, s["hr"][:, j], ALU.mult)
                    nc.vector.tensor_tensor(s["t"][:, 1], zi, s["hi"][:, j], ALU.mult)
                    nc.vector.tensor_tensor(s["t"][:, 2], zr, s["hi"][:, j], ALU.mult)
                    nc.vector.tensor_tensor(s["t"][:, 3], zi, s["hc0"][:] if j == 0 else s["hr"][:, j], ALU.mult).then_inc(s["t_done"], 1)
                for q in range(J if o == 0 else HC):
                    dve.wait_ge(s["inv_done"], J * o + q + 1)
                    if o == 0:
                        x = m.x1[:, tok0 + q]
                        nc.vector.tensor_tensor(x, m.ps[:, q % 2], x, ALU.mult).then_inc(s["inv_evac"], 1)
                    else:
                        nc.vector.tensor_tensor(m.yh[:, q, at:at + n], m.ps[:, q % 2, 0:n], m.x2[:, q, at:at + n],
                                                ALU.mult).then_inc(s["inv_evac"], 1)

        @block.gpsimd
        def _(pool):
            for k in range(2 * J):
                o, j = divmod(k, J)
                pool.wait_ge(s["t_done"], k + 1)
                nc.gpsimd.tensor_tensor(s["f"][:, 0, j], s["t"][:, 0], s["t"][:, 1], ALU.subtract).then_inc(s["y_done"], 1)
                nc.gpsimd.tensor_tensor(s["f"][:, 1, j], s["t"][:, 2], s["t"][:, 3], ALU.add).then_inc(s["y_done"], 1)


def qkv_stage(nc, m, l, w_in, w_ukv, consts, streams_q):
    both = spans(True)
    NU = QC + KVC + 1
    src = w_in[l].rearrange("(c p) n -> p c n", p=P)
    with stage(nc, f"qkv{l}", ["w_in", "wkr_in", "wv_in", "rope_in", "zeroed", "swapped", "mm_done", "raw_done", "sq_done",
                               "sum_done", "dve", "root_done", "rope_done", "norm_done", "v_done", "v_evac"],
               [("w", [P, KC, QL + KVL]), ("wkr", [P, KC, P]), ("wv", [P, KVC, HEADS, VD]), ("raw", [P, QC + KVC, TOK]),
                ("sq", [P, 2, TOK]), ("r", [P, 2, TOK]), ("var", [P, 2, TOK]), ("t", [P, 2, SEQ]), ("g", [P, QC])]) as (block, s):
        def streams(i):
            return streams_q if i < QC else both

        @block.sync
        def _(sp):
            sp.dma_start(s["w"][:], src[:, :, Q0:KR0]).then_inc(s["w_in"], 16)
            sp.wait_ge(s["zeroed"], 1)
            sp.dma_start(s["wkr"][:, :, NOPE:QK], src[:, :, KR0:G0]).then_inc(s["wkr_in"], 16)
            sp.dma_start(m.rope[:], consts["rope"]).then_inc(s["rope_in"], 16)
            for c in range(KVC):
                v_cols = w_ukv[l, c * P:(c + 1) * P].rearrange("p (h k) -> p h k", h=HEADS)[:, :, NOPE:NOPE + VD]
                sp.dma_start(s["wv"][:, c], v_cols).then_inc(s["wv_in"], 16)

        @block.gpsimd
        def _(pool):
            nc.gpsimd.memset(s["wkr"][:], 0.0).then_inc(s["zeroed"], 1)
            pool.wait_ge(s["wkr_in"], 16)
            raw = s["wkr"][:, :, NOPE:QK].rearrange("p c (a h k) -> p c a h k", a=2, h=2)
            swap = s["wkr"][:, :, QK:P].rearrange("p c (a h k) -> p c a h k", a=2, h=2)
            for h in range(2):
                for a in range(2):
                    nc.gpsimd.tensor_copy(swap[:, :, a, h], raw[:, :, a, 1 - h]).then_inc(s["swapped"], 1)

        @block.tensor
        def _(pe):
            def sums(i):
                pe.wait_ge(s["sq_done"], i + 1)
                k, c, last_c = (0, i, QC - 1) if i < QC else (1, i - QC, KVC - 1)
                for t, at, n in streams(i):
                    last = nc.tensor.matmul(m.ps[:, 4 + 2 * k + t, 0:n], m.ones[:], s["sq"][:, i % 2, at:at + n],
                                            start=c == 0, stop=c == last_c)
                last.then_inc(s["sum_done"], 1)

            pe.wait_ge(s["w_in"], 16)
            for i in range(NU):
                if i >= 2:
                    pe.wait_ge(s["sq_done"], i - 1)
                    pe.wait_ge(s["raw_done"], i - 1)
                if i == NU - 1:
                    pe.wait_ge(s["swapped"], 4)
                for t, at, n in streams(i):
                    for c in range(KC):
                        lhs = s["w"][:, c, i * P:(i + 1) * P] if i < NU - 1 else s["wkr"][:, c]
                        last = nc.tensor.matmul(m.ps[:, 2 * (i % 2) + t, 0:n], lhs, m.u[:, c, at:at + n],
                                                start=c == 0, stop=c == KC - 1)
                last.then_inc(s["mm_done"], 1)
                if i >= 1:
                    sums(i - 1)
            pe.wait_ge(s["wv_in"], 16 * KVC)
            pe.wait_ge(s["norm_done"], QC + KVC)
            for j in range(TT):
                if j >= 2:
                    pe.wait_ge(s["v_evac"], j - 1)
                for c in range(KVC):
                    last = nc.tensor.matmul(m.ps[:, j % 2], m.kvn[:, c, j * P:(j + 1) * P], s["wv"][:, c],
                                            start=c == 0, stop=c == KVC - 1)
                last.then_inc(s["v_done"], 1)

        @block.scalar
        def _(act):
            nc.scalar.mul(s["g"][:], m.cols[:, l, R_QG:R_QG + QC], SCALE)
            for i in range(NU - 1):
                act.wait_ge(s["mm_done"], i + 1)
                for t, at, n in streams(i):
                    last = nc.scalar.activation(s["raw"][:, i, at:at + n], m.ps[:, 2 * (i % 2) + t, 0:n], ACT.Copy)
                last.then_inc(s["raw_done"], 1)
                if i >= 2:
                    act.wait_ge(s["sum_done"], i - 1)
                for t, at, n in streams(i):
                    last = nc.scalar.activation(s["sq"][:, i % 2, at:at + n], m.ps[:, 2 * (i % 2) + t, 0:n], ACT.Square)
                last.then_inc(s["sq_done"], 1)
            act.wait_ge(s["dve"], 1)
            nc.scalar.activation(s["r"][:], s["var"][:], ACT.Sqrt).then_inc(s["root_done"], 1)
            for j in range(TT):
                act.wait_ge(s["v_done"], j + 1)
                nc.scalar.activation(m.vt[:, j], m.ps[:, j % 2], ACT.Copy).then_inc(s["v_evac"], 1)

        @block.vector
        def _(dve):
            link = Chain(dve, s["dve"])
            last = None
            if len(streams_q) == 1:
                nc.vector.memset(s["var"][:, 0, SEQ:TOK], 1.0)
            dve.wait_ge(s["sum_done"], QC + KVC)
            for k, width in ((0, QL), (1, KVL)):
                for t, at, n in (streams_q, both)[k]:
                    last = nc.vector.tensor_scalar(s["var"][:, k, at:at + n], m.ps[:, 4 + 2 * k + t, 0:n], 1.0 / width, EPS,
                                                   ALU.mult, ALU.add)
            link(last)
            dve.wait_ge(s["root_done"], 1)
            refined_rsqrt(nc, link, s["r"][:], s["var"][:], s["sq"][:])
            for i in range(QC + KVC):
                n = sum(n for _, _, n in streams(i))
                k, out, g = (0, m.qn[:, i, 0:n], s["g"][:, i:i + 1]) if i < QC else \
                    (1, m.kvn[:, i - QC, 0:n], m.cols[:, l, R_KVG + i - QC:R_KVG + i - QC + 1])
                nc.vector.scalar_tensor_tensor(out, s["raw"][:, i, 0:n], g, s["r"][:, k, 0:n], ALU.mult,
                                               ALU.mult).then_inc(s["norm_done"], 1)
            b = 2 * ((NU - 1) % 2)
            dve.wait_ge(s["mm_done"], NU)
            dve.wait_ge(s["rope_in"], 16)
            nc.vector.tensor_tensor(s["t"][NOPE:QK, 0], m.ps[NOPE:QK, b], m.rope[NOPE:QK], ALU.mult)
            link(nc.vector.tensor_tensor(s["t"][NOPE:QK, 1], m.ps[QK:P, b], m.rope[QK:P], ALU.mult))
            for h in range(2):
                nc.vector.tensor_tensor(m.key[NOPE:QK, h, 0:SEQ], s["t"][NOPE:QK, 0], s["t"][NOPE:QK, 1], ALU.add)
                nc.vector.tensor_copy(m.key[NOPE:QK, h, SEQ:TOK], m.ps[NOPE:QK, b + 1, 0:CTX])


def attention_stage(nc, m, l, w_uq, w_ukv, streams_q):
    n_q = sum(n for _, _, n in streams_q)
    units = [(j, 0, TOK) for j in range(XT)] + [(XT + j, SEQ, CTX) for j in range((n_q - SEQ) // P)]
    NU = 2 * len(units)
    NT = n_q // P
    ctx_q = len(streams_q) > 1
    wq_src = w_uq[l].rearrange("(c p) (h k) -> p c h k", p=P, k=QK)
    wk_src = w_ukv[l].rearrange("(c p) (h k) -> p c h k", p=P, k=NOPE + VD)
    work = [(h, *u) for h in range(2) for u in units]
    with stage(nc, f"attn{l}", ["w0", "w1", "swapped", "turns", "proj_done", "q_done", "dve", "rot_done", "qk_done",
                                "s_done", "max_done", "exp_done", "tr_done", "ta_done", "tv_done", "pv_done", "o_done",
                                "back", "back_evac"],
               [("wq", [P, 2, QC, P]), ("wk", [P, 2, KVC, NOPE]), ("t", [P, 2, SEQ]), ("qrot", [P, 2, SEQ]),
                ("q", [P, 2, TOK]), ("p", [P, 2, TOK]), ("pt", [P, 2, TT, P]), ("nm", [P, 2]), ("sum", [P, 4]),
                ("rs", [P, 2]), ("otok", [P, TT, HEADS * VD])]) as (block, s):
        loaded = [s["w0"], s["w1"]]

        def act_share(nk):
            return 4 if nk == TOK else nk // P // 2

        def proj_bank(h):
            return 4 if h == 0 else 0

        @block.sync
        def _(sp):
            with sp.Fori(0, HEADS // 2) as i:
                for h in range(2):
                    sp.wait_ge(s["proj_done"], i * 4 + (2 * h + 2))
                    sp.dma_start(s["wq"][:, h, :, 0:QK], wq_src[:, :, i * 2 + h]).then_inc(loaded[h], 16)
                    sp.dma_start(s["wk"][:, h], wk_src[:, :, i * 2 + h, 0:NOPE]).then_inc(loaded[h], 16)

        @block.gpsimd
        def _(pool):
            with pool.Fori(0, HEADS // 2) as i:
                for h in range(2):
                    pool.wait_ge(loaded[h], i * 32 + 32)
                    pool.sem_inc(s["turns"], 1)
                    raw = s["wq"][:, h, :, NOPE:QK].rearrange("p c (a h k) -> p c a h k", a=2, h=2)
                    swap = s["wq"][:, h, :, QK:P].rearrange("p c (a h k) -> p c a h k", a=2, h=2)
                    for b in range(2):
                        for a in range(2):
                            nc.gpsimd.tensor_copy(swap[:, :, a, b], raw[:, :, a, 1 - b]).then_inc(s["swapped"], 1)

        @block.tensor
        def _(pe):
            pe.sem_inc(s["proj_done"], 4)
            pe.sem_inc(s["tr_done"], 2)
            pe.sem_inc(s["pv_done"], 2)

            def project(i, h):
                pe.wait_ge(loaded[h], i * 32 + 32)
                pe.wait_ge(s["swapped"], i * 8 + (4 * h + 4))
                b = proj_bank(h)
                for bank, off, n, at, wide in ((b, 0, SEQ, 0, True), (b + 1, 0, SEQ, 0, False),
                                               (b + 2, 0, CTX, SEQ, True), (b + 2, CTX, CTX, SEQ, False)):
                    if wide and at and not ctx_q:
                        continue
                    w, z, k = (s["wq"], m.qn, QC) if wide else (s["wk"], m.kvn, KVC)
                    out = m.ps[0:P if wide else NOPE, bank, off:off + n]
                    for c in range(k):
                        last = nc.tensor.matmul(out, w[:, h, c], z[:, c, at:at + n], start=c == 0, stop=c == k - 1)
                    if wide and not at:
                        last.then_inc(s["proj_done"], 1)
                last.then_inc(s["proj_done"], 1)

            def scores(i, u):
                h, j, k0, nk = work[u]
                pe.wait_ge(s["exp_done"], i * NU + (u + 1))
                b = 2 * (u % 2)
                if j < XT:
                    nc.tensor.matmul(m.ps[:, b], s["qrot"][0:QK, h, j * P:(j + 1) * P], m.key[0:QK, h, 0:SEQ], start=True, stop=True)
                off = 1 if j < XT else 0
                nc.tensor.matmul(m.ps[:, b + off, 0:CTX], s["q"][0:QK, h, j * P:(j + 1) * P], m.key[0:QK, h, SEQ:TOK],
                                 start=True, stop=True).then_inc(s["s_done"], 1)

            def transposes(i, u):
                _, _, _, nk = work[u]
                pe.wait_ge(s["exp_done"], i * NU + (u + 3))
                pe.wait_ge(s["ta_done"], i * NU + (u + 1))
                pe.wait_ge(s["tv_done"], i * NU + (u + 1))
                na = act_share(nk)
                for k in range(nk // P):
                    kb = k if k < na else k - na
                    last = nc.tensor.transpose(m.ps[:, 4 if k < na else 5, kb * P:(kb + 1) * P],
                                               s["p"][:, u % 2, k * P:(k + 1) * P], m.ident[:])
                last.then_inc(s["tr_done"], 1)

            def values(i, u):
                h, j, k0, nk = work[u]
                pe.wait_ge(s["ta_done"], i * NU + (u + 2))
                pe.wait_ge(s["tv_done"], i * NU + (u + 2))
                pe.wait_ge(s["o_done"], i * NU + (u + 1))
                for k in range(nk // P):
                    last = nc.tensor.matmul(m.ps[:, 6 + u % 2, 0:VD], s["pt"][:, u % 2, k],
                                            m.vt[:, k0 // P + k, bass.ds((i * 2 + h) * VD, VD)], start=k == 0, stop=k == nk // P - 1)
                last.then_inc(s["pv_done"], 1)

            with pe.Fori(0, HEADS // 2) as i:
                pe.wait_ge(s["exp_done"], i * NU + 2)
                pe.wait_ge(s["ta_done"], i * NU + 1)
                pe.wait_ge(s["tv_done"], i * NU + 1)
                pe.wait_ge(s["o_done"], i * NU + 2)
                for h in range(2):
                    project(i, h)
                pe.wait_ge(s["q_done"], i * 2 + 2)
                pe.wait_ge(s["qk_done"], i * 2 + 2)
                for u in range(NU + 2):
                    if u < NU:
                        scores(i, u)
                    if 1 <= u <= NU:
                        transposes(i, u - 1)
                    if u >= 2:
                        values(i, u - 2)
            pe.wait_ge(s["o_done"], HEADS // 2 * NU + 2)
            for j in range(NT):
                if j >= 2:
                    pe.wait_ge(s["back_evac"], j - 1)
                for c in range(HC):
                    last = nc.tensor.transpose(m.ps[:, j % 2, c * P:(c + 1) * P], s["otok"][:, j, c * P:(c + 1) * P], m.ident[:])
                last.then_inc(s["back"], 1)

        @block.scalar
        def _(act):
            act.sem_inc(s["exp_done"], 2)
            act.sem_inc(s["ta_done"], 1)

            def copy_projected(i, h):
                b = proj_bank(h)
                act.wait_ge(s["proj_done"], i * 4 + (2 * h + 6))
                if h == 0:
                    act.wait_ge(s["pv_done"], i * NU + 2)
                nc.scalar.activation(m.key[0:NOPE, h, 0:SEQ], m.ps[0:NOPE, b + 1], ACT.Copy)
                if ctx_q:
                    nc.scalar.activation(s["q"][0:QK, h, SEQ:TOK], m.ps[0:QK, b + 2, 0:CTX], ACT.Copy)
                nc.scalar.activation(m.key[0:NOPE, h, SEQ:TOK], m.ps[0:NOPE, b + 2, CTX:2 * CTX], ACT.Copy)
                act.wait_ge(s["rot_done"], i * 2 + (h + 1))
                nc.scalar.activation(s["q"][0:QK, h, 0:SEQ], m.ps[0:QK, b], ACT.Copy).then_inc(s["qk_done"], 1)

            def exponential(i, u):
                h, j, k0, nk = work[u]
                act.wait_ge(s["max_done"], i * NU + (u + 1))
                act.wait_ge(s["tr_done"], i * NU + (u + 1))
                b = 2 * (u % 2)
                nc.scalar.activation(s["p"][:, u % 2, 0:nk], m.ps[:, b:b + 2].rearrange("p b k -> p (b k)")[:, 0:nk], ACT.Exp,
                                     bias=s["nm"][:, u % 2:u % 2 + 1], accum_out=s["sum"][:, u % 4:u % 4 + 1]).then_inc(s["exp_done"], 1)

            def copy_transposed(i, u):
                _, _, _, nk = work[u]
                act.wait_ge(s["tr_done"], i * NU + (u + 3))
                act.wait_ge(s["pv_done"], i * NU + (u + 1))
                n = act_share(nk)
                nc.scalar.activation(s["pt"][:, u % 2, 0:n], m.ps[:, 4, 0:n * P].rearrange("p (k q) -> p k q", q=P),
                                     ACT.Copy).then_inc(s["ta_done"], 1)

            with act.Fori(0, HEADS // 2) as i:
                for h in range(2):
                    copy_projected(i, h)
                for u in range(NU + 1):
                    if u < NU:
                        exponential(i, u)
                    if u >= 1:
                        copy_transposed(i, u - 1)

        @block.vector
        def _(dve):
            dve.sem_inc(s["tv_done"], 1)
            dve.sem_inc(s["o_done"], 2)

            def rotate(i, h):
                b = proj_bank(h)
                dve.wait_ge(s["proj_done"], i * 4 + (2 * h + 5))
                if h == 0:
                    dve.wait_ge(s["pv_done"], i * NU + 2)
                nc.vector.tensor_tensor(s["t"][NOPE:QK, 0], m.ps[NOPE:QK, b], m.rope[NOPE:QK], ALU.mult)
                nc.vector.tensor_tensor(s["t"][NOPE:QK, 1], m.ps[QK:P, b], m.rope[QK:P], ALU.mult)
                nc.vector.tensor_copy(s["qrot"][0:NOPE, h], m.ps[0:NOPE, b]).then_inc(s["rot_done"], 1)
                dve.wait_ge(s["rot_done"], i * 2 + (h + 1))
                nc.vector.tensor_tensor(s["qrot"][NOPE:QK, h], s["t"][NOPE:QK, 0], s["t"][NOPE:QK, 1], ALU.add).then_inc(s["q_done"], 1)
                dve.wait_ge(s["q_done"], i * 2 + (h + 1))

            def maximum(i, u):
                h, j, k0, nk = work[u]
                dve.wait_ge(s["s_done"], i * NU + (u + 1))
                dve.wait_ge(s["exp_done"], i * NU + (u + 1))
                b = 2 * (u % 2)
                nc.vector.tensor_reduce(s["nm"][:, u % 2:u % 2 + 1], m.ps[:, b:b + 2].rearrange("p b k -> p (b k)")[:, 0:nk],
                                        axis=AX.X, op=ALU.max, negate=True).then_inc(s["max_done"], 1)

            def copy_transposed(i, u):
                _, _, _, nk = work[u]
                dve.wait_ge(s["tr_done"], i * NU + (u + 3))
                dve.wait_ge(s["pv_done"], i * NU + (u + 1))
                na, n = act_share(nk), nk // P - act_share(nk)
                nc.vector.tensor_copy(s["pt"][:, u % 2, na:na + n],
                                      m.ps[:, 5, 0:n * P].rearrange("p (k q) -> p k q", q=P)).then_inc(s["tv_done"], 1)

            def output(i, u):
                h, j, k0, nk = work[u]
                r = s["rs"][:, u % 2:u % 2 + 1]
                dve.wait_ge(s["o_done"], i * NU + (u + 1))
                nc.vector.reciprocal(r, s["sum"][:, u % 4:u % 4 + 1]).then_inc(s["dve"], 1)
                dve.wait_ge(s["dve"], i * NU + (u + 1))
                dve.wait_ge(s["pv_done"], i * NU + (u + 3))
                nc.vector.tensor_scalar_mul(s["otok"][:, j, bass.ds((i * 2 + h) * VD, VD)], m.ps[:, 6 + u % 2, 0:VD],
                                            r).then_inc(s["o_done"], 1)

            with dve.Fori(0, HEADS // 2) as i:
                for h in range(2):
                    rotate(i, h)
                for u in range(NU + 2):
                    if u < NU:
                        maximum(i, u)
                    if 1 <= u <= NU:
                        copy_transposed(i, u - 1)
                    if u >= 2:
                        output(i, u - 2)
            for j in range(NT):
                dve.wait_ge(s["back"], j + 1)
                nc.vector.tensor_copy(m.ya[:, :, j * P:(j + 1) * P],
                                      m.ps[:, j % 2].rearrange("p (c t) -> p c t", c=HC)).then_inc(s["back_evac"], 1)


def merge_stage(nc, m, l, w_in, w_hy_o, w_mla_o, streams):
    NS = len(streams)
    KW = 2 * KC + 2 * HC
    w_src = w_in[l].rearrange("(c p) n -> p c n", p=P)
    hy_src = w_hy_o[l].rearrange("(c p) n -> p c n", p=P)
    mla_src = w_mla_o[l].rearrange("(c p) n -> p c n", p=P)
    with stage(nc, f"merge{l}", ["w0", "w1", "mm_done", "sig_done", "prod_done", "mix_done"],
               [("w", [P, 2, KW, P]), ("sig", [P, 2, 2, SEQ]), ("t", [P, 2, 2, SEQ])]) as (block, s):
        loaded = [s["w0"], s["w1"]]

        @block.sync
        def _(sp):
            with sp.Fori(0, KC // 2) as i:
                for b in range(2):
                    sp.wait_ge(s["mm_done"], i * (2 * NS) + (b + 1) * NS)
                    for at, n, src, col in ((0, KC, w_src, G0), (KC, KC, w_src, G0 + D), (2 * KC, HC, hy_src, 0),
                                            (2 * KC + HC, HC, mla_src, 0)):
                        sp.dma_start(s["w"][:, b, at:at + n], src[:, :, bass.ds(i * (2 * P) + (b * P + col), P)]).then_inc(loaded[b], 16)

        @block.tensor
        def _(pe):
            pe.sem_inc(s["mm_done"], 2 * NS)
            with pe.Fori(0, KC // 2) as i:
                for b in range(2):
                    pe.wait_ge(loaded[b], i * 64 + 64)
                    for t, at, n in streams:
                        k = b * NS + t
                        pe.wait_ge(s["prod_done"], i * (2 * NS) + (k + 1))
                        q = 4 * (k % 2)
                        for bank, w_at, z, kn in ((q, 0, m.u, KC), (q + 1, KC, m.u, KC), (q + 2, 2 * KC, m.yh, HC),
                                                  (q + 3, 2 * KC + HC, m.ya, HC)):
                            for c in range(kn):
                                last = nc.tensor.matmul(m.ps[:, bank, 0:n], s["w"][:, b, w_at + c], z[:, c, at:at + n],
                                                        start=c == 0, stop=c == kn - 1)
                        last.then_inc(s["mm_done"], 1)

        @block.scalar
        def _(act):
            with act.Fori(0, KC // 2) as i:
                for b in range(2):
                    for t, at, n in streams:
                        k = b * NS + t
                        act.wait_ge(s["mm_done"], i * (2 * NS) + (k + 1 + 2 * NS))
                        act.wait_ge(s["prod_done"], i * (2 * NS) + (k + 1))
                        nc.scalar.activation(s["sig"][:, k % 2, :, 0:n], m.ps[:, 4 * (k % 2):4 * (k % 2) + 2, 0:n],
                                             ACT.Sigmoid).then_inc(s["sig_done"], 1)

        @block.vector
        def _(dve):
            dve.sem_inc(s["prod_done"], 2)
            with dve.Fori(0, KC // 2) as i:
                for b in range(2):
                    for t, at, n in streams:
                        k = b * NS + t
                        dve.wait_ge(s["sig_done"], i * (2 * NS) + (k + 1))
                        dve.wait_ge(s["mix_done"], i * (2 * NS) + (k + 1))
                        nc.vector.tensor_tensor(s["t"][:, k % 2, :, 0:n], m.ps[:, 4 * (k % 2) + 2:4 * (k % 2) + 4, 0:n],
                                                s["sig"][:, k % 2, :, 0:n], ALU.mult).then_inc(s["prod_done"], 1)

        @block.gpsimd
        def _(pool):
            pool.sem_inc(s["mix_done"], 2)
            with pool.Fori(0, KC // 2) as i:
                for b in range(2):
                    for t, at, n in streams:
                        k = b * NS + t
                        pool.wait_ge(s["prod_done"], i * (2 * NS) + (k + 3))
                        nc.gpsimd.tensor_tensor(m.mix[:, bass.ds(i * 2 + b, 1), at:at + n].rearrange("p a n -> p (a n)"),
                                                s["t"][:, k % 2, 0, 0:n], s["t"][:, k % 2, 1, 0:n], ALU.add).then_inc(s["mix_done"], 1)


def out_stage(nc, m, l, w_out, streams):
    src = w_out[l].rearrange("(c p) n -> p c n", p=P)
    with stage(nc, f"out{l}", ["w0", "w1", "w_used", "mm_done", "evac"], [("w", [P, 2, KC, 4 * P])]) as (block, s):
        loaded = [s["w0"], s["w1"]]

        @block.sync
        def _(sp):
            for g in range(2):
                sp.dma_start(s["w"][:, g], src[:, :, g * 4 * P:(g + 1) * 4 * P]).then_inc(loaded[g], 16)

        @block.tensor
        def _(pe):
            for k in range(KC):
                if k % 4 == 0:
                    pe.wait_ge(loaded[k // 4], 16)
                if k >= 2:
                    pe.wait_ge(s["evac"], k - 1)
                for t, at, n in streams:
                    for c in range(KC):
                        last = nc.tensor.matmul(m.ps[:, 2 * (k % 2) + t, 0:n], s["w"][:, k // 4, c, (k % 4) * P:(k % 4 + 1) * P],
                                                m.mix[:, c, at:at + n], start=c == 0, stop=c == KC - 1)
                last.then_inc(s["mm_done"], 1)

        @block.vector
        def _(dve):
            for k in range(KC):
                dve.wait_ge(s["mm_done"], k + 1)
                for t, at, n in streams:
                    r = m.resid[:, k, at:at + n]
                    last = nc.vector.scalar_tensor_tensor(r, m.ps[:, 2 * (k % 2) + t, 0:n], m.mod[:, l, t, 2 * KC + k:2 * KC + k + 1],
                                                          r, ALU.mult, ALU.add)
                last.then_inc(s["evac"], 1)


class Memory:
    pass


def chip_memory(nc, ctx):
    def sb(name, shape, dtype=F32):
        return ctx.enter_context(nc.sbuf_tensor(name, shape, dtype))

    m = Memory()
    m.resid = sb("resid", [P, KC, TOK])
    m.ident = sb("ident", [P, P])
    m.ones = sb("ones", [P, P])
    m.cols = sb("cols", [P, DEPTH, R_ALL])
    m.gcols = sb("gcols", [P, RG_ALL])
    m.sil = sb("sil", [P, KC, 2])
    m.mod = sb("mod", [P, DEPTH, 2, N_MOD * KC])
    m.gain = sb("gain", [P, DEPTH, 2, 2, KC])
    m.weight = sb("weight", [P, 2, TT])
    m.table = sb("table", [P, NE + overflow_blocks(TOK)], I32)
    m.over = sb("over", [P, 1 + overflow_blocks(TOK)], I32)
    m.ps = ctx.enter_context(nc.psum_tensor("ps", [P, 8, 512], F32))
    return m


def mixers(nc, m, l, a, consts):
    last = l == DEPTH - 1
    streams = spans(not last)

    def buffer(scope, name, shape):
        return scope.enter_context(nc.sbuf_tensor(f"{name}{l}", shape, F32))

    with ExitStack() as whole:
        m.u = buffer(whole, "u", [P, KC, TOK])
        norm_stage(nc, m, f"norm1_{l}", m.u, spans(True), lambda t, c: m.gain[:, l, t, 0, c:c + 1],
                   lambda t, c: m.mod[:, l, t, c:c + 1])
        m.yh = buffer(whole, "yh", [P, HC, TOK])
        with ExitStack() as part:
            m.v = buffer(part, "v", [P, TT, HW])
            m.x1 = buffer(part, "x1", [P, TT, HW])
            m.x2 = buffer(part, "x2", [P, HC, TOK])
            hyena_in_stage(nc, m, l, a["w_in"], streams)
            flt = [a[k][l] for k in ("flt_w1", "flt_b1", "flt_freq", "flt_w2", "flt_b2", "flt_w3", "flt_bias")]
            for t, _, _ in streams:
                conv_stage(nc, m, l, t, flt, consts)
        m.ya = buffer(whole, "ya", [P, HC, TOK])
        with ExitStack() as part:
            m.qn = buffer(part, "qn", [P, QC, TOK])
            m.kvn = buffer(part, "kvn", [P, KVC, TOK])
            m.key = buffer(part, "key", [P, 2, TOK])
            m.vt = buffer(part, "vt", [P, TT, HEADS * VD])
            m.rope = buffer(part, "rope", [P, SEQ])
            qkv_stage(nc, m, l, a["w_in"], a["w_ukv"], consts, streams)
            attention_stage(nc, m, l, a["w_uq"], a["w_ukv"], streams)
        m.mix = buffer(whole, "mix", [P, KC, TOK])
        merge_stage(nc, m, l, a["w_in"], a["w_hy_o"], a["w_mla_o"], streams)
        out_stage(nc, m, l, a["w_out"], streams)


def table_rows(a):
    def rows(v):
        return v.rearrange("(r p) -> r p", p=P)

    per_layer = [((R_G1, KC, rows(a["norm1_g"][l])), (R_G2, KC, rows(a["norm2_g"][l])), (R_ADA, N_MOD * KC, rows(a["b_ada"][l])),
                  (R_QG, QC, rows(a["q_norm_g"][l])), (R_KVG, KVC, rows(a["kv_norm_g"][l])),
                  (R_SCW, 9 * HC, a["sc_w"][l].rearrange("k (r p) -> (k r) p", p=P)), (R_SCB, 3 * HC, rows(a["sc_b"][l])))
                 for l in range(DEPTH)]
    return per_layer, ((RG_C, KC, rows(a["c"][0])), (RG_CC, KC, rows(a["c_ctx"])), (RG_F, KC, rows(a["final_g"])))


A_ALL = 2 * TOK
NO_ROW = A_ALL


def overflow_blocks(n_tok):
    return 2 * n_tok // SLOTS


def router_stage(nc, m, l, a, consts, streams, dram):
    n_tok = sum(n for _, _, n in streams)
    NT = n_tok // P
    NOV = overflow_blocks(n_tok)
    NB = NE + NOV
    QM = (n_tok - 1) // SLOTS
    R = NG + NE
    LOW = -3.0e38
    sems = ["consts_in", "wr_in", "bias_in", "tr_done", "lg_done", "tr_evac_a", "tr_evac_v", "lg_evac", "u_out0", "u_out1", "dve",
            "exps", "hot_done", "rank_done", "filled", "fill_out", "dest_done", "sc_out", "table_in"]
    bufs = [("wr", [P, KC, R]), ("bias", [P, R]), ("lg", [P, NT, R]), ("utok", [P, 2, D]), ("triu", [P, P]), ("iota", [P, 96]),
            ("gb", [P, NT, NG]), ("c", [P, NT, NG]), ("hot_g", [P, NT, NG]), ("e", [P, NT, NG]), ("leg", [P, NT, EG]),
            ("beg", [P, NT, EG]), ("val", [P, NT, EG]), ("hot1", [P, NT, EG]), ("hot2", [P, NT, EG]), ("big", [P, NT, NE]),
            ("sel", [P, 2, NT, NE]), ("both", [P, NT, NE]), ("rank", [P, NT, NE]), ("cnt", [P, NE]), ("ovf", [P, NE]),
            ("incl", [P, NE]), ("base", [P, NE]), ("one", [P, NE]), ("r", [P, 16, NT]), ("ex", [P, 2, NT]),
            ("q", [P, 2, NT]), ("pos", [P, 2, NT]), ("eid", [P, 2, NT]), ("ob", [P, 2, NT]), ("z", [P, 2, NT]), ("dest", [P, 2, NT]),
            ("dest_i", [P, 2, NT], I32), ("num", [P, 2, NT]), ("num_i", [P, 2, NT], I32), ("fill", [P, NB], I32),
            ("cmp", [P, NOV, NE]), ("oe", [P, NOV])]
    table = dram["table"][l]
    with stage(nc, f"route{l}", sems, bufs) as (block, s):
        u_out = [s["u_out0"], s["u_out1"]]

        @block.sync
        def _(sp):
            sp.dma_start(s["wr"][:, :, 0:NG], a["w_router_g"][l].rearrange("(c p) n -> p c n", p=P)).then_inc(s["wr_in"], 16)
            sp.dma_start(s["wr"][:, :, NG:R], a["w_router_e"][l].rearrange("(c p) n -> p c n", p=P)).then_inc(s["wr_in"], 16)
            sp.dma_start(s["bias"][:, 0:NG], a["b_router_g"][l].partition_broadcast(P)).then_inc(s["bias_in"], 16)
            sp.dma_start(s["bias"][:, NG:R], a["b_router_e"][l].partition_broadcast(P)).then_inc(s["bias_in"], 16)
            sp.dma_start(s["triu"][:], consts["triu"]).then_inc(s["consts_in"], 16)
            sp.dma_start(s["iota"][:], consts["iota"]).then_inc(s["consts_in"], 16)
            sp.wait_ge(s["filled"], 1)
            sp.dma_start(table.rearrange("(s b) o -> s (b o)", b=NB), s["fill"][:]).then_inc(s["fill_out"], 16)
            for j in range(NT):
                sp.wait_ge(s["tr_evac_a"], j + 1)
                sp.wait_ge(s["tr_evac_v"], j + 1)
                for k in range(2):
                    sp.dma_start(dram["u"][k * TOK + j * P:k * TOK + (j + 1) * P], s["utok"][:, j % 2]).then_inc(u_out[j % 2], 16)
            sp.wait_ge(s["sc_out"], 16 * 2 * NT)
            sp.dma_start(m.table[:, 0:NB], table.rearrange("(s b) o -> s (b o)", b=NB)).then_inc(s["table_in"], 16)
            for k in range(2):
                sp.wait_ge(u_out[k], 16 * NT)
            sp.wait_ge(s["table_in"], 16)

        @block.gpsimd
        def _(pool):
            nc.gpsimd.memset(s["fill"][:], NO_ROW).then_inc(s["filled"], 1)
            pool.wait_ge(s["fill_out"], 16)
            pool.wait_ge(s["dest_done"], 2)
            for k in range(2):
                for j in range(NT):
                    nc.gpsimd.indirect_dma_start(out=table, out_offset=bass.IndirectOffsetOnAxis(ap=s["dest_i"][:, k, j:j + 1], axis=0),
                                                 in_=s["num_i"][:, k, j:j + 1], in_offset=None,
                                                 bounds_check=SLOTS * NB - 1, oob_is_err=False).then_inc(s["sc_out"], 16)
            pool.wait_ge(s["sc_out"], 16 * 2 * NT)

        @block.tensor
        def _(pe):
            pe.wait_ge(s["wr_in"], 32)
            for j in range(NT):
                if j >= 2:
                    pe.wait_ge(s["tr_evac_a"], j - 1)
                    pe.wait_ge(s["tr_evac_v"], j - 1)
                b = 2 * (j % 2)
                for c in range(KC):
                    last = nc.tensor.transpose(m.ps[:, b + c // 4, (c % 4) * P:(c % 4 + 1) * P], m.u[:, c, j * P:(j + 1) * P], m.ident[:])
                last.then_inc(s["tr_done"], 1)
                if j >= 2:
                    pe.wait_ge(s["lg_evac"], j - 1)
                for c in range(KC):
                    last = nc.tensor.matmul(m.ps[:, 4 + j % 2, 0:R], m.u[:, c, j * P:(j + 1) * P], s["wr"][:, c], start=c == 0, stop=c == KC - 1)
                last.then_inc(s["lg_done"], 1)
            pe.wait_ge(s["consts_in"], 32)
            pe.wait_ge(s["hot_done"], 1)
            for j in range(NT):
                for i in range(j + 1):
                    nc.tensor.matmul(m.ps[:, 6, j * NE:(j + 1) * NE], m.ones[:] if i < j else s["triu"][:], s["both"][:, i],
                                     start=i == 0, stop=i == j)
            for i in range(NT):
                last = nc.tensor.matmul(m.ps[:, 7, 0:NE], m.ones[:], s["both"][:, i], start=i == 0, stop=i == NT - 1)
            last.then_inc(s["rank_done"], 1)

        @block.scalar
        def _(act):
            for j in range(NT):
                act.wait_ge(s["tr_done"], j + 1)
                if j >= 2:
                    act.wait_ge(u_out[j % 2], 32 * (j // 2))
                nc.scalar.activation(s["utok"][:, j % 2, 0:512], m.ps[:, 2 * (j % 2)], ACT.Copy).then_inc(s["tr_evac_a"], 1)
            act.wait_ge(s["exps"], 1)
            nc.scalar.activation(s["e"][:], s["e"][:], ACT.Exp).then_inc(s["exps"], 1)
            act.wait_ge(s["exps"], 3)
            nc.scalar.activation(s["ex"][:], s["ex"][:], ACT.Exp).then_inc(s["exps"], 1)

        @block.vector
        def _(dve):
            link = Chain(dve, s["dve"])
            for j in range(NT):
                dve.wait_ge(s["tr_done"], j + 1)
                if j >= 2:
                    dve.wait_ge(u_out[j % 2], 32 * (j // 2))
                nc.vector.tensor_copy(s["utok"][:, j % 2, 512:D], m.ps[:, 2 * (j % 2) + 1]).then_inc(s["tr_evac_v"], 1)
                dve.wait_ge(s["lg_done"], j + 1)
                nc.vector.tensor_copy(s["lg"][:, j], m.ps[:, 4 + j % 2, 0:R]).then_inc(s["lg_evac"], 1)
            dve.wait_ge(s["lg_evac"], NT)
            dve.wait_ge(s["bias_in"], 32)
            dve.wait_ge(s["consts_in"], 32)

            def over(ap, *shape):
                return ap.broadcast_to([P, *shape])

            def row(k):
                return s["r"][:, k]

            iota8 = over(s["iota"][:, None, 0:NG], NT, NG)

            def first_max(val, hot, k):
                link(nc.vector.tensor_reduce(row(k), val, axis=AX.X, op=ALU.max))
                link(nc.vector.tensor_tensor(s["c"][:], val, over(row(k)[:, :, None], NT, NG), ALU.is_equal))
                link(nc.vector.scalar_tensor_tensor(s["c"][:], s["c"][:], -64.0, iota8, ALU.mult, ALU.add))
                link(nc.vector.tensor_reduce(row(k), s["c"][:], axis=AX.X, op=ALU.min))
                link(nc.vector.tensor_tensor(hot, s["c"][:], over(row(k)[:, :, None], NT, NG), ALU.is_equal))

            def picked(out, val, hot):
                link(nc.vector.tensor_tensor(s["c"][:], val, hot, ALU.mult))
                link(nc.vector.tensor_reduce(out, s["c"][:], axis=AX.X, op=ALU.add))

            lg_g = s["lg"][:, :, 0:NG]
            link(nc.vector.tensor_tensor(s["gb"][:], lg_g, over(s["bias"][:, None, 0:NG], NT, NG), ALU.add))
            first_max(s["gb"][:], s["hot_g"][:], 0)
            link(nc.vector.tensor_reduce(row(1), lg_g, axis=AX.X, op=ALU.max))
            nc.vector.tensor_tensor(s["e"][:], lg_g, over(row(1)[:, :, None], NT, NG), ALU.subtract).then_inc(s["exps"], 1)
            dve.wait_ge(s["exps"], 2)
            link(nc.vector.tensor_reduce(row(2), s["e"][:], axis=AX.X, op=ALU.add))
            picked(row(3), s["e"][:], s["hot_g"][:])
            hot_over = over(s["hot_g"][:, :, :, None], NT, NG, EG)
            big4 = s["big"][:].rearrange("p t (g j) -> p t g j", g=NG)
            for src, dst in ((s["lg"][:, :, NG:R].rearrange("p t (g j) -> p t g j", g=NG), s["leg"]),
                             (over(s["bias"][:, NG:R].rearrange("p (t g j) -> p t g j", t=1, g=NG), NT, NG, EG), s["beg"])):
                link(nc.vector.tensor_tensor(big4, src, hot_over, ALU.mult))
                link(nc.vector.tensor_reduce(dst[:], s["big"][:].rearrange("p t (g j) -> p t j g", g=NG), axis=AX.X, op=ALU.add))
            link(nc.vector.tensor_tensor(s["val"][:], s["leg"][:], s["beg"][:], ALU.add))
            first_max(s["val"][:], s["hot1"][:], 4)
            link(nc.vector.scalar_tensor_tensor(s["val"][:], s["hot1"][:], LOW, s["val"][:], ALU.mult, ALU.add))
            first_max(s["val"][:], s["hot2"][:], 5)
            picked(s["ex"][:, 0], s["leg"][:], s["hot1"][:])
            picked(s["ex"][:, 1], s["leg"][:], s["hot2"][:])
            link(nc.vector.tensor_tensor(row(6), s["ex"][:, 0], s["ex"][:, 1], ALU.max))
            nc.vector.tensor_tensor(s["ex"][:], s["ex"][:], over(row(6)[:, None, :], 2, NT), ALU.subtract).then_inc(s["exps"], 1)
            for k, hot in enumerate((s["hot1"], s["hot2"])):
                last = nc.vector.tensor_tensor(s["sel"][:, k].rearrange("p t (g j) -> p t g j", g=NG), hot_over,
                                               over(hot[:, :, None, :], NT, NG, EG), ALU.mult)
            link(last)
            nc.vector.tensor_tensor(s["both"][:], s["sel"][:, 0], s["sel"][:, 1], ALU.add).then_inc(s["hot_done"], 1)
            dve.wait_ge(s["exps"], 4)
            link(nc.vector.tensor_tensor(row(7), s["ex"][:, 0], s["ex"][:, 1], ALU.add))
            link(nc.vector.tensor_tensor(row(7), row(7), row(2), ALU.mult))
            link(nc.vector.reciprocal(row(8), row(7)))
            link(nc.vector.tensor_tensor(row(8), row(8), row(3), ALU.mult))
            nc.vector.tensor_tensor(m.weight[:, :, 0:NT], s["ex"][:], over(row(8)[:, None, :], 2, NT), ALU.mult)
            dve.wait_ge(s["rank_done"], 1)
            nc.vector.tensor_copy(s["rank"][:], m.ps[:, 6, 0:NT * NE].rearrange("p (t e) -> p t e", e=NE))
            nc.vector.memset(s["one"][:], 1.0)
            link(nc.vector.tensor_copy(s["cnt"][:], m.ps[:, 7, 0:NE]))
            link(nc.vector.tensor_scalar(s["ovf"][:], s["cnt"][:], float(SLOTS), None, ALU.is_gt))
            for q in range(2, QM + 1):
                link(nc.vector.scalar_tensor_tensor(s["ovf"][:], s["cnt"][:], float(q * SLOTS), s["ovf"][:], ALU.is_gt, ALU.add))
            link(nc.vector.tensor_tensor_scan(s["incl"][:], s["one"][:], s["ovf"][:], 0.0, ALU.mult, ALU.add))
            link(nc.vector.tensor_tensor(s["base"][:], s["incl"][:], s["ovf"][:], ALU.subtract))
            for k in range(2):
                for vals, out in ((s["rank"][:], s["pos"]), (over(s["iota"][:, None, 0:NE], NT, NE), s["eid"]), (over(s["base"][:, None, :], NT, NE), s["ob"])):
                    link(nc.vector.tensor_tensor(s["big"][:], s["sel"][:, k], vals, ALU.mult))
                    link(nc.vector.tensor_reduce(out[:, k], s["big"][:], axis=AX.X, op=ALU.add))
            link(nc.vector.tensor_scalar(s["q"][:], s["pos"][:], float(SLOTS), None, ALU.is_ge))
            link(nc.vector.tensor_copy(s["z"][:], s["q"][:]))
            for q in range(2, QM + 1):
                link(nc.vector.scalar_tensor_tensor(s["q"][:], s["pos"][:], float(q * SLOTS), s["q"][:], ALU.is_ge, ALU.add))
            link(nc.vector.scalar_tensor_tensor(s["ob"][:], s["ob"][:], float(NE - 1), s["q"][:], ALU.add, ALU.add))
            link(nc.vector.tensor_tensor(s["ob"][:], s["ob"][:], s["eid"][:], ALU.subtract))
            link(nc.vector.tensor_tensor(s["ob"][:], s["ob"][:], s["z"][:], ALU.mult))
            link(nc.vector.tensor_tensor(s["ob"][:], s["ob"][:], s["eid"][:], ALU.add))
            link(nc.vector.scalar_tensor_tensor(s["pos"][:], s["q"][:], -float(SLOTS), s["pos"][:], ALU.mult, ALU.add))
            link(nc.vector.scalar_tensor_tensor(s["dest"][:], s["pos"][:], float(NB), s["ob"][:], ALU.mult, ALU.add))
            nc.vector.tensor_copy(s["dest_i"][:], s["dest"][:]).then_inc(s["dest_done"], 1)
            for k in range(2):
                for j in range(NT):
                    last = nc.vector.tensor_scalar_add(s["num"][:, k, j:j + 1], s["iota"][:, 88:89], float(k * TOK + j * P))
            link(last)
            nc.vector.tensor_copy(s["num_i"][:], s["num"][:]).then_inc(s["dest_done"], 1)
            link(nc.vector.tensor_tensor(s["cmp"][:], over(s["incl"][:, None, :], NOV, NE),
                                         over(s["iota"][:, 64:64 + NOV][:, :, None], NOV, NE), ALU.is_le))
            link(nc.vector.tensor_reduce(s["oe"][:], s["cmp"][:], axis=AX.X, op=ALU.add))
            link(nc.vector.tensor_scalar(s["oe"][:], s["oe"][:], float(NE - 1), None, ALU.min))
            nc.vector.tensor_copy(m.over[:, 1:1 + NOV], s["oe"][:])
            nc.vector.tensor_copy(m.over[:, 0:1], s["incl"][:, NE - 1:NE])


def moe_stage(nc, m, l, a, dram):
    W_RING = RU
    sems = ["w0", "w1", "w2", "w3", "g0", "g1", "g2", "g3", "s0", "s1", "zeroed", "gu_done", "xt_done", "ht_done", "down_done",
            "silu_done", "xa", "ya", "h_done", "xb", "hb", "yb"]
    bufs = [("wgu", [P, W_RING, 2, KC, DE]), ("wd", [P, W_RING, 2, D]), ("xg", [P, 4, D]), ("xt", [P, 2, KC, P]),
            ("sg", [P, 2, DE]), ("h", [P, 2, DE]), ("ht", [P, 2, 2, P]), ("y", [P, 2, D])]
    with stage(nc, f"moe{l}", sems, bufs) as (block, s):
        loaded, gathered, scattered = [s["w0"], s["w1"], s["w2"], s["w3"]], [s["g0"], s["g1"], s["g2"], s["g3"]], [s["s0"], s["s1"]]

        def wait(eng, sem, n):
            if not isinstance(n, int) or n > 0:
                eng.wait_ge(sem, n)

        def rounds(eng, body):
            for b in range(RU):
                body(b, b, b)
            with eng.Fori(1, NE // RU - 1) as i:
                for b in range(RU):
                    body(i * RU + b, b, i)
            for b in range(RU):
                body(NE - RU + b, b, NE // RU - 1)

        def turn(j, r):
            return j // RU if isinstance(j, int) else r

        @block.sync
        def _(sp):
            def load(j, b, r):
                r = turn(j, r)
                wait(sp, s["down_done"], j - (W_RING - 1))
                at = j if isinstance(j, int) else None
                e = bass.ds(j, 1)
                for k, w in enumerate((a["w_gate_e"], a["w_up_e"])):
                    sp.dma_start(s["wgu"][:, b, k], w[l, e].rearrange("o (p c) n -> p (o c) n", p=P)).then_inc(loaded[b], 16)
                sp.dma_start(s["wd"][:, b], a["w_down_e"][l, e].rearrange("o (p c) n -> p (o c) n", p=P)).then_inc(loaded[b], 16)

            rounds(sp, load)

        @block.gpsimd
        def _(pool):
            nc.gpsimd.memset(s["xg"][:], 0.0).then_inc(s["zeroed"], 1)
            pool.wait_ge(s["zeroed"], 1)

            def gather(j):
                if j >= 4:
                    pool.wait_ge(s["xt_done"], j - 3)
                nc.gpsimd.indirect_dma_start(out=s["xg"][:, j % 4], out_offset=None, in_=dram["u"],
                                             in_offset=bass.IndirectOffsetOnAxis(ap=m.table[:, j:j + 1], axis=0),
                                             bounds_check=A_ALL - 1, oob_is_err=False).then_inc(gathered[j % 4], 16)

            def scatter(j):
                pool.wait_ge(s["ya"], j + 1)
                pool.wait_ge(s["yb"], j + 1)
                nc.gpsimd.indirect_dma_start(out=dram["y"], out_offset=bass.IndirectOffsetOnAxis(ap=m.table[:, j:j + 1], axis=0),
                                             in_=s["y"][:, j % 2], in_offset=None,
                                             bounds_check=A_ALL - 1, oob_is_err=False).then_inc(scattered[j % 2], 16)

            for j in range(NE + 3):
                if j < NE:
                    gather(j)
                if j >= 3:
                    scatter(j - 3)
            for b in range(2):
                pool.wait_ge(scattered[b], 16 * (NE // 2))

        @block.tensor
        def _(pe):
            def x_transposes(j, b, r):
                wait(pe, gathered[b], 16 * (r + 1) if isinstance(r, int) else r * 16 + 16)
                wait(pe, s["xa"], j)
                wait(pe, s["xb"], j)
                for c in range(KC):
                    last = nc.tensor.transpose(m.ps[:, 2 + c // 4, (c % 4) * P:(c % 4 + 1) * P],
                                               s["xg"][:, b].rearrange("p (q c) -> p c q", c=KC)[:, c], m.ident[:])
                last.then_inc(s["xt_done"], 1)

            def down(j, b):
                wait(pe, s["hb"], j + 1)
                wait(pe, s["ya"], j)
                wait(pe, s["yb"], j)
                for half in range(2):
                    for c in range(2):
                        last = nc.tensor.matmul(m.ps[:, 5 + half], s["ht"][:, b % 2, c], s["wd"][:, b, c, half * 512:(half + 1) * 512],
                                                start=c == 0, stop=c == 1)
                last.then_inc(s["down_done"], 1)

            def body(j, b, r):
                r = turn(j, r)
                wait(pe, loaded[b], r * 48 + 48)
                wait(pe, s["xa"], j + 1)
                wait(pe, s["xb"], j + 1)
                wait(pe, s["h_done"], j - 1)
                for c in range(KC):
                    last = nc.tensor.matmul(m.ps[:, b % 2], s["xt"][:, b % 2, c], s["wgu"][:, b, :, c], start=c == 0, stop=c == KC - 1)
                last.then_inc(s["gu_done"], 1)
                if not isinstance(j, int) or j + 1 < NE:
                    x_transposes(j + 1, (b + 1) % RU, r + (b + 1) // RU)
                if not isinstance(j, int) or j >= 1:
                    down(j - 1, (b - 1) % RU)
                wait(pe, s["h_done"], j + 1)
                wait(pe, s["hb"], j)
                for c in range(2):
                    last = nc.tensor.transpose(m.ps[:, 4, c * P:(c + 1) * P], s["h"][:, b % 2].rearrange("p (q c) -> p c q", c=2)[:, c], m.ident[:])
                last.then_inc(s["ht_done"], 1)

            x_transposes(0, 0, 0)
            rounds(pe, body)
            down(NE - 1, RU - 1)

        def evac_x(act, sem, op, half):
            def run(j, b):
                wait(act, s["xt_done"], j + 1)
                wait(act, s["gu_done"], j - 1)
                op(s["xt"][:, b % 2, 4 * half:4 * half + 4], m.ps[:, 2 + half].rearrange("p (c q) -> p c q", c=4)).then_inc(sem, 1)
            return run

        def evac_y(act, sem, op, half):
            def run(j, b):
                wait(act, s["down_done"], j + 1)
                if isinstance(j, int):
                    wait(act, scattered[b % 2], 16 * (j // 2))
                else:
                    act.wait_ge(scattered[b % 2], (j - (b % 2)) * 8)
                op(s["y"][:, b % 2, half * 512:(half + 1) * 512], m.ps[:, 5 + half]).then_inc(sem, 1)
            return run

        @block.scalar
        def _(act):
            def copy(out, in_):
                return nc.scalar.activation(out, in_, ACT.Copy)

            x_half, y_half = evac_x(act, s["xa"], copy, 0), evac_y(act, s["ya"], copy, 0)

            def body(j, b, r):
                wait(act, s["gu_done"], j + 1)
                wait(act, s["h_done"], j - 1)
                nc.scalar.activation(s["sg"][:, b % 2], m.ps[:, b % 2, 0:DE], ACT.Silu).then_inc(s["silu_done"], 1)
                if not isinstance(j, int) or j + 1 < NE:
                    x_half(j + 1, b + 1)
                if not isinstance(j, int) or j >= 1:
                    y_half(j - 1, (b - 1) % RU)

            x_half(0, 0)
            rounds(act, body)
            y_half(NE - 1, RU - 1)

        @block.vector
        def _(dve):
            x_half, y_half = evac_x(dve, s["xb"], nc.vector.tensor_copy, 1), evac_y(dve, s["yb"], nc.vector.tensor_copy, 1)

            def body(j, b, r):
                wait(dve, s["silu_done"], j + 1)
                wait(dve, s["ht_done"], j - 1)
                nc.vector.tensor_tensor(s["h"][:, b % 2], m.ps[:, b % 2, DE:2 * DE], s["sg"][:, b % 2], ALU.mult).then_inc(s["h_done"], 1)
                if not isinstance(j, int) or j + 1 < NE:
                    x_half(j + 1, b + 1)
                if not isinstance(j, int) or j >= 1:
                    y_half(j - 1, (b - 1) % RU)
                wait(dve, s["ht_done"], j + 1)
                wait(dve, s["down_done"], j - 1)
                nc.vector.tensor_copy(s["ht"][:, b % 2], m.ps[:, 4, 0:2 * P].rearrange("p (c q) -> p c q", c=2)).then_inc(s["hb"], 1)

            x_half(0, 0)
            rounds(dve, body)
            y_half(NE - 1, RU - 1)


def overflow_stage(nc, m, l, a, dram, n_tok):
    NOV = overflow_blocks(n_tok)
    sems = ["w_in", "idx_done", "g_in", "sc_out", "pe_done", "x_evac", "silu_done", "h_done", "ht_evac", "y_evac", "zeroed", "turns", "block_done"]
    bufs = [("wgu", [P, 2, KC, DE]), ("wd", [P, 2, D]), ("xg", [P, D]), ("xt", [P, KC, P]), ("sg", [P, DE]), ("h", [P, DE]),
            ("ht", [P, 2, P]), ("y", [P, D]), ("idx", [P, 1], I32)]
    with stage(nc, f"over{l}", sems, bufs) as (block, s):
        def blocks(eng, body):
            n = eng.value_load(m.over[0:1, 0:1], min_val=0, max_val=NOV)
            with eng.Fori(0, NOV) as i:
                with eng.If(i < n):
                    body(i)

        @block.sync
        def _(sp):
            sp.sem_inc(s["pe_done"], 4)

            def body(i):
                e = sp.value_load(m.over[0:1, bass.ds(i + 1, 1)], min_val=0, max_val=NE - 1)
                sp.wait_ge(s["pe_done"], i * 4 + 4)
                at = bass.ds(e, 1)
                for k, w in enumerate((a["w_gate_e"], a["w_up_e"])):
                    sp.dma_start(s["wgu"][:, k], w[l, at].rearrange("o (p c) n -> p (o c) n", p=P)).then_inc(s["w_in"], 16)
                sp.dma_start(s["wd"][:], a["w_down_e"][l, at].rearrange("o (p c) n -> p (o c) n", p=P)).then_inc(s["w_in"], 16)

            blocks(sp, body)

        @block.gpsimd
        def _(pool):
            nc.gpsimd.memset(s["xg"][:], 0.0).then_inc(s["zeroed"], 1)
            pool.wait_ge(s["zeroed"], 1)

            def body(i):
                at = bass.IndirectOffsetOnAxis(ap=s["idx"][:, 0:1], axis=0)
                pool.wait_ge(s["idx_done"], i + 1)
                pool.sem_inc(s["turns"], 1)
                nc.gpsimd.indirect_dma_start(out=s["xg"][:], out_offset=None, in_=dram["u"], in_offset=at,
                                             bounds_check=A_ALL - 1, oob_is_err=False).then_inc(s["g_in"], 16)
                pool.wait_ge(s["y_evac"], i + 1)
                pool.sem_inc(s["turns"], 1)
                nc.gpsimd.indirect_dma_start(out=dram["y"], out_offset=at, in_=s["y"][:], in_offset=None,
                                             bounds_check=A_ALL - 1, oob_is_err=False).then_inc(s["sc_out"], 16)
                pool.wait_ge(s["sc_out"], i * 16 + 16)
                pool.sem_inc(s["block_done"], 1)

            pool.sem_inc(s["block_done"], 1)
            blocks(pool, body)

        @block.tensor
        def _(pe):
            def body(i):
                pe.wait_ge(s["g_in"], i * 16 + 16)
                for c in range(KC):
                    last = nc.tensor.transpose(m.ps[:, c // 4, (c % 4) * P:(c % 4 + 1) * P], s["xg"][:].rearrange("p (q c) -> p c q", c=KC)[:, c], m.ident[:])
                last.then_inc(s["pe_done"], 1)
                pe.wait_ge(s["w_in"], i * 48 + 48)
                pe.wait_ge(s["x_evac"], i + 1)
                for c in range(KC):
                    last = nc.tensor.matmul(m.ps[:, 2], s["xt"][:, c], s["wgu"][:, :, c], start=c == 0, stop=c == KC - 1)
                last.then_inc(s["pe_done"], 1)
                pe.wait_ge(s["h_done"], i + 1)
                for c in range(2):
                    last = nc.tensor.transpose(m.ps[:, 3, c * P:(c + 1) * P], s["h"][:].rearrange("p (q c) -> p c q", c=2)[:, c], m.ident[:])
                last.then_inc(s["pe_done"], 1)
                pe.wait_ge(s["ht_evac"], i + 1)
                for half in range(2):
                    for c in range(2):
                        last = nc.tensor.matmul(m.ps[:, 4 + half], s["ht"][:, c], s["wd"][:, c, half * 512:(half + 1) * 512],
                                                start=c == 0, stop=c == 1)
                last.then_inc(s["pe_done"], 1)

            blocks(pe, body)

        @block.scalar
        def _(act):
            def body(i):
                act.wait_ge(s["pe_done"], i * 4 + 6)
                nc.scalar.activation(s["sg"][:], m.ps[:, 2, 0:DE], ACT.Silu).then_inc(s["silu_done"], 1)

            blocks(act, body)

        @block.vector
        def _(dve):
            def body(i):
                dve.wait_ge(s["block_done"], i + 1)
                nc.vector.tensor_scalar(s["idx"][:], m.table[:, bass.ds(i + NE, 1)], 0.0, None, ALU.add).then_inc(s["idx_done"], 1)
                dve.wait_ge(s["pe_done"], i * 4 + 5)
                nc.vector.tensor_copy(s["xt"][:], m.ps[:, 0:2].rearrange("p b (c q) -> p (b c) q", c=4)).then_inc(s["x_evac"], 1)
                dve.wait_ge(s["silu_done"], i + 1)
                nc.vector.tensor_tensor(s["h"][:], m.ps[:, 2, DE:2 * DE], s["sg"][:], ALU.mult).then_inc(s["h_done"], 1)
                dve.wait_ge(s["pe_done"], i * 4 + 7)
                nc.vector.tensor_copy(s["ht"][:], m.ps[:, 3, 0:2 * P].rearrange("p (c q) -> p c q", c=2)).then_inc(s["ht_evac"], 1)
                dve.wait_ge(s["pe_done"], i * 4 + 8)
                nc.vector.tensor_copy(s["y"][:], m.ps[:, 4:6].rearrange("p b k -> p (b k)")).then_inc(s["y_evac"], 1)

            blocks(dve, body)


def combine_stage(nc, m, l, dram, streams):
    work = [(t, at // P + j) for t, at, n in streams for j in range(n // P)]
    with stage(nc, f"comb{l}", ["y0", "y1", "y2", "y3", "half_done", "sum_done", "tr_done", "evac"],
               [("y", [P, 4, 2, D]), ("c", [P, 2, D])]) as (block, s):
        loaded = [s["y0"], s["y1"], s["y2"], s["y3"]]

        @block.sync
        def _(sp):
            for j, (t, tile) in enumerate(work):
                if j >= 4:
                    sp.wait_ge(s["sum_done"], j - 3)
                for k in range(2):
                    at = k * TOK + tile * P
                    sp.dma_start(s["y"][:, j % 4, k], dram["y"][at:at + P]).then_inc(loaded[j % 4], 16)

        @block.scalar
        def _(act):
            for j, (t, tile) in enumerate(work):
                act.wait_ge(loaded[j % 4], 32 * (j // 4 + 1))
                if j >= 2:
                    act.wait_ge(s["tr_done"], j - 1)
                nc.scalar.mul(s["c"][:, j % 2], s["y"][:, j % 4, 0], m.weight[:, 0, tile:tile + 1]).then_inc(s["half_done"], 1)

        @block.tensor
        def _(pe):
            for j, (t, tile) in enumerate(work):
                pe.wait_ge(s["sum_done"], j + 1)
                if j >= 2:
                    pe.wait_ge(s["evac"], j - 1)
                for c in range(KC):
                    last = nc.tensor.transpose(m.ps[:, 2 * (j % 2) + c // 4, (c % 4) * P:(c % 4 + 1) * P], s["c"][:, j % 2, c * P:(c + 1) * P], m.ident[:])
                last.then_inc(s["tr_done"], 1)

        @block.vector
        def _(dve):
            def add(j):
                t, tile = work[j]
                dve.wait_ge(s["tr_done"], j + 1)
                for c in range(KC):
                    r = m.resid[:, c, tile * P:(tile + 1) * P]
                    last = nc.vector.scalar_tensor_tensor(r, m.ps[:, 2 * (j % 2) + c // 4, (c % 4) * P:(c % 4 + 1) * P],
                                                          m.mod[:, l, t, 5 * KC + c:5 * KC + c + 1], r, ALU.mult, ALU.add)
                last.then_inc(s["evac"], 1)

            for j, (t, tile) in enumerate(work):
                dve.wait_ge(s["half_done"], j + 1)
                nc.vector.scalar_tensor_tensor(s["c"][:, j % 2], s["y"][:, j % 4, 1], m.weight[:, 1, tile:tile + 1], s["c"][:, j % 2],
                                               ALU.mult, ALU.add).then_inc(s["sum_done"], 1)
                if j >= 1:
                    add(j - 1)
            add(len(work) - 1)


def store_stage(nc, m, out):
    with stage(nc, "store", ["tr_done", "evac", "out0", "out1"], [("o", [P, 2, D])]) as (block, s):
        @block.tensor
        def _(pe):
            for j in range(XT):
                if j >= 2:
                    pe.wait_ge(s["evac"], j - 1)
                for c in range(KC):
                    last = nc.tensor.transpose(m.ps[:, 2 * (j % 2) + c // 4, (c % 4) * P:(c % 4 + 1) * P], m.u[:, c, j * P:(j + 1) * P], m.ident[:])
                last.then_inc(s["tr_done"], 1)

        @block.vector
        def _(dve):
            for j in range(XT):
                dve.wait_ge(s["tr_done"], j + 1)
                if j >= 2:
                    dve.wait_ge((s["out0"], s["out1"])[j % 2], 16 * (j // 2))
                nc.vector.tensor_copy(s["o"][:, j % 2], m.ps[:, 2 * (j % 2):2 * (j % 2) + 2].rearrange("p b k -> p (b k)")).then_inc(s["evac"], 1)

        @block.sync
        def _(sp):
            for j in range(XT):
                sp.wait_ge(s["evac"], j + 1)
                sp.dma_start(out[0, j * P:(j + 1) * P], s["o"][:, j % 2]).then_inc((s["out0"], s["out1"])[j % 2], 16)
            for k in range(2):
                sp.wait_ge((s["out0"], s["out1"])[k], 16 * (XT // 2))


def experts(nc, m, l, a, consts, dram):
    streams = spans(l < DEPTH - 1)
    n_tok = sum(n for _, _, n in streams)
    with nc.sbuf_tensor(f"u2_{l}", [P, KC, TOK], F32) as u:
        m.u = u
        norm_stage(nc, m, f"norm2_{l}", m.u, streams, lambda t, c: m.gain[:, l, t, 1, c:c + 1],
                   lambda t, c: m.mod[:, l, t, 3 * KC + c:3 * KC + c + 1])
        router_stage(nc, m, l, a, consts, streams, dram)
    moe_stage(nc, m, l, a, dram)
    overflow_stage(nc, m, l, a, dram, n_tok)
    combine_stage(nc, m, l, dram, streams)


def trunk(nc, a, consts, out):
    with ExitStack() as ctx:
        m = chip_memory(nc, ctx)
        dram = {"u": nc.dram_tensor("rows_in", [A_ALL, D], F32).ap(), "y": nc.dram_tensor("rows_out", [A_ALL, D], F32).ap(),
                "table": [nc.dram_tensor(f"slots{l}", [SLOTS * (NE + overflow_blocks(TOK if l < DEPTH - 1 else SEQ)), 1],
                                         I32).ap() for l in range(DEPTH)]}
        per_layer, shared = table_rows(a)
        load_stage(nc, m, a["x"], a["ctx"], per_layer, shared, consts)
        ada_stage(nc, m, a["w_ada"])
        for l in range(DEPTH):
            mixers(nc, m, l, a, consts)
            experts(nc, m, l, a, consts, dram)
        with nc.sbuf_tensor("u_out", [P, KC, TOK], F32) as u:
            m.u = u
            norm_stage(nc, m, "norm_out", m.u, spans(False), lambda t, c: m.gcols[:, RG_F + c:RG_F + c + 1], None)
            store_stage(nc, m, out)


NAMES = ["x", "c", "ctx", "c_ctx", "w_ada", "b_ada", "norm1_g", "w_in", "q_norm_g", "kv_norm_g", "w_uq", "w_ukv", "sc_w", "sc_b",
         "flt_w1", "flt_b1", "flt_freq", "flt_w2", "flt_b2", "flt_w3", "flt_bias", "w_hy_o", "w_mla_o", "w_out", "norm2_g",
         "w_router_g", "b_router_g", "w_router_e", "b_router_e", "w_gate_e", "w_up_e", "w_down_e", "final_g"]


def kernel(**inputs):
    import concourse.bacc as bacc
    from concourse.bass_utils import run_bass_kernel_spmd

    nc = bacc.Bacc("TRN2", target_bir_lowering=False, num_devices=1)
    arrays, a, consts = {}, {}, {}
    for name in NAMES:
        arrays[f"in_{name}"] = np.ascontiguousarray(inputs[name])
        a[name] = nc.dram_tensor(f"in_{name}", arrays[f"in_{name}"].shape, F32, kind="ExternalInput").ap()
    for name, value in layout_constants().items():
        arrays[f"const_{name}"] = value
        consts[name] = nc.dram_tensor(f"const_{name}", value.shape, F32, kind="ExternalInput").ap()
    out = nc.dram_tensor("out", (1, SEQ, D), F32, kind="ExternalOutput").ap()
    trunk(nc, a, consts, out)
    r = run_bass_kernel_spmd(nc, [arrays], core_ids=[0])
    return r.results[0]["out"]
```

```python
import math
from contextlib import ExitStack, contextmanager

import concourse.bass as bass
from concourse import mybir
import numpy as np

F32 = mybir.dt.float32
I32 = mybir.dt.int32
ACT = mybir.ActivationFunctionType
ALU = mybir.AluOpType
AX = mybir.AxisListType

P = 128
D = 1024
KC = D // P
SEQ, CTX = 512, 256
TOK = SEQ + CTX
XT, CT = SEQ // P, CTX // P
TT = TOK // P
DEPTH = 2
EPS = 1e-6
N_MOD = 6
GRID_W = 64

HW = 512
HC = HW // P
BANDS, EMB, FFN = 16, 33, 64
HY_COLS = 3 * HW
DECAY_FAST, DECAY_SLOW, DECAY_TARGET = 0.3, 1.5, 1e-2

HEADS, NOPE, ROPE, VD = 8, 64, 32, 64
QK = NOPE + ROPE
QL, KVL = 384, 256
QC, KVC = QL // P, KVL // P
PAIRS = ROPE // 4
SCALE = QK ** -0.5
Q0 = HY_COLS
KR0 = Q0 + QL + KVL
G0 = KR0 + ROPE
IN_COLS = G0 + 2 * D

NG, EG = 8, 8
NE = NG * EG
DE = 256
SLOTS = 64
RU = 4

R_G1, R_G2, R_ADA, R_QG, R_KVG, R_SCW, R_SCB = 0, 8, 16, 64, 67, 69, 105
R_ALL = 117
RG_C, RG_CC, RG_F, RG_ALL = 0, 8, 16, 24


def layout_constants():
    out = {"ident": np.eye(P, dtype=np.float32), "ones": np.ones((P, P), np.float32)}
    f = np.float32
    deltas = np.abs(np.linspace(math.log(DECAY_TARGET) / DECAY_FAST, math.log(DECAY_TARGET) / DECAY_SLOW,
                                HW).astype(f))
    for name, n in (("x", SEQ), ("c", CTX)):
        k = np.arange(n)
        ang = np.pi / n * ((k[:, None] * k[None, :]) % (2 * n))
        alt = np.where(k % 2 == 0, 1.0, -1.0)
        fwd_c, fwd_s = np.cos(ang), -np.sin(ang)
        fwd_s[:, 0] = alt
        inv_c, inv_s = np.cos(ang) / n, -np.sin(ang) / n
        inv_c[0] = 0.5 / n
        inv_s[0] = 0.5 * alt / n
        for tag, m in (("fc", fwd_c), ("fs", fwd_s), ("ic", inv_c), ("is", inv_s)):
            out[f"{tag}_{name}"] = m.astype(f)
        t = np.linspace(0.0, 1.0, n).astype(f)[:, None]
        w = (f(2.0 * math.pi) * np.arange(n, dtype=f)[:, None] / f(n)).astype(f)
        bands = np.linspace(1e-4, BANDS - 1, BANDS).astype(f)[None, :]
        bw = (bands * w).astype(f)
        out[f"feat_{name}"] = np.ascontiguousarray(np.concatenate([t, np.cos(bw), -np.sin(bw)], axis=1).T.astype(f))
        out[f"decay_{name}"] = np.exp(-t * deltas[None, :]).astype(f)
    rows = SEQ // GRID_W
    r, col = np.meshgrid(np.arange(rows), np.arange(GRID_W), indexing="ij")
    pos = np.stack([r.reshape(-1), col.reshape(-1)], axis=-1).astype(f)
    inv = (f(10000.0) ** (-np.arange(PAIRS, dtype=f) / f(PAIRS))).astype(f)
    ang = pos[:, :, None] * inv
    cs, sn = np.cos(ang).astype(f), np.sin(ang).astype(f)
    rope = np.zeros((P, SEQ), f)
    for a in range(2):
        for h in range(2):
            at = a * 2 * PAIRS + h * PAIRS
            rope[NOPE + at:NOPE + at + PAIRS] = cs[:, a].T
            rope[QK + at:QK + at + PAIRS] = (sn if h else -sn)[:, a].T
    out["rope"] = rope
    out["triu"] = np.triu(np.ones((P, P), f), 1)
    iota = np.zeros((P, 96), f)
    iota[:, 0:64] = np.arange(64)
    iota[:, 64:88] = np.arange(24)
    iota[:, 88] = np.arange(P)
    out["iota"] = iota
    return out


@contextmanager
def stage(nc, name, signals, buffers=()):
    with ExitStack() as ctx:
        mine = {n: ctx.enter_context(nc.sbuf_tensor(f"{name}_{n}", shape, dt[0] if dt else F32))
                for n, shape, *dt in buffers}
        sems = {n: nc.alloc_semaphore(f"{name}_{n}") for n in signals}
        with nc.Block() as block:
            yield block, {**mine, **sems}
        nc.clear_and_free_semaphores(list(sems.values()))
        nc.all_engine_barrier()


class Chain:

    def __init__(self, eng, sem, start=0):
        self.eng, self.sem, self.n = eng, sem, start

    def __call__(self, ins):
        self.n = self.n + 1
        ins.then_inc(self.sem, 1)
        self.eng.wait_ge(self.sem, self.n)


def refined_rsqrt(nc, link, root, var, tmp):
    link(nc.vector.reciprocal(root, root))
    link(nc.vector.tensor_tensor(tmp, root, root, ALU.mult))
    link(nc.vector.scalar_tensor_tensor(tmp, tmp, -0.5, var, ALU.mult, ALU.mult))
    link(nc.vector.scalar_tensor_tensor(root, tmp, 1.5, root, ALU.add, ALU.mult))


def spans(with_ctx):
    return ((0, 0, SEQ), (1, SEQ, CTX)) if with_ctx else ((0, 0, SEQ),)


def load_stage(nc, m, x, ctx, rows_l, rows_g, consts):
    with stage(nc, "load", ["tokens_in", "rows_in", "consts_in", "pe_done", "evac", "silu_done", "sil_zeroed"],
               [("tok", [P, TT, D]), ("rows", [P, DEPTH + 1, P])]) as (block, s):
        @block.sync
        def _(sp):
            sp.dma_start(m.ident[:], consts["ident"]).then_inc(s["consts_in"], 16)
            sp.dma_start(m.ones[:], consts["ones"]).then_inc(s["consts_in"], 16)
            for l in range(DEPTH):
                for at, n, src in rows_l[l]:
                    sp.dma_start(s["rows"][at:at + n, l], src).then_inc(s["rows_in"], 16)
            for at, n, src in rows_g:
                sp.dma_start(s["rows"][at:at + n, DEPTH], src).then_inc(s["rows_in"], 16)
            for t in range(TT):
                src = x[0, t * P:(t + 1) * P] if t < XT else ctx[0, (t - XT) * P:(t - XT + 1) * P]
                sp.dma_start(s["tok"][:, t], src).then_inc(s["tokens_in"], 16)

        @block.tensor
        def _(pe):
            pe.wait_ge(s["consts_in"], 32)
            pe.wait_ge(s["rows_in"], 16 * (sum(len(r) for r in rows_l) + len(rows_g)))
            for l in range(DEPTH + 1):
                n = R_ALL if l < DEPTH else RG_ALL
                last = nc.tensor.transpose(m.ps[:, 7, l * P:l * P + n], s["rows"][0:n, l], m.ident[0:n, 0:n])
            last.then_inc(s["pe_done"], 1)
            pe.wait_ge(s["tokens_in"], 16 * TT)
            for t in range(TT):
                for half in range(2):
                    n = 2 * t + half
                    if n >= 4:
                        pe.wait_ge(s["evac"], n - 3)
                    for c in range(4):
                        k = half * 4 + c
                        last = nc.tensor.transpose(m.ps[:, n % 4, c * P:(c + 1) * P], s["tok"][:, t, k * P:(k + 1) * P],
                                                   m.ident[:])
                    last.then_inc(s["pe_done"], 1)

        @block.vector
        def _(dve):
            nc.vector.memset(m.sil[:], 0.0).then_inc(s["sil_zeroed"], 1)
            for n in range(2 * TT):
                t, half = n // 2, n % 2
                dve.wait_ge(s["pe_done"], n + 2)
                nc.vector.tensor_copy(m.resid[:, half * 4:half * 4 + 4, t * P:(t + 1) * P],
                                      m.ps[:, n % 4].rearrange("p (c t) -> p c t", c=4)).then_inc(s["evac"], 1)

        @block.scalar
        def _(act):
            act.wait_ge(s["pe_done"], 1)
            for l in range(DEPTH):
                nc.scalar.activation(m.cols[:, l, 0:R_ALL], m.ps[:, 7, l * P:l * P + R_ALL], ACT.Copy)
            nc.scalar.activation(m.gcols[:, 0:RG_ALL], m.ps[:, 7, DEPTH * P:DEPTH * P + RG_ALL],
                                 ACT.Copy).then_inc(s["silu_done"], 1)
            act.wait_ge(s["sil_zeroed"], 1)
            nc.scalar.activation(m.sil[:, :, 0:2], m.ps[:, 7, DEPTH * P:DEPTH * P + 2 * KC].rearrange("p (s c) -> p c s", s=2),
                                 ACT.Silu)


TWO_PI = 2.0 * math.pi
TWO_PI_HI = 6.28125
ROUND = 1.5 * 2.0 ** 23
PI_BELOW = 3.1415925


def transfer_planes(t):
    return 2 * ((SEQ, CTX)[t] // P) + 1


def prepare_stage(nc, m, a, consts, dram):
    RING, COLS = 3, 512
    per = COLS // P
    BLOCKS = N_MOD * D // COLS
    sets = [(l, t) for l in range(DEPTH) for t, _, _ in spans(l < DEPTH - 1)]
    items = [(i, l, t, o) for i, (l, t) in enumerate(sets) for o in range(2)]
    NI = len(items)
    EACH = DEPTH * BLOCKS // NI
    tiles = [(SEQ, CTX)[t] // P for _, _, t, _ in items]
    before = [sum(tiles[:k]) for k in range(NI + 1)]
    sems = ["ada0_in", "ada1_in", "ada2_in", "small_in", "mats_in", "mlp_done", "sines", "dve", "h3_done", "f_done", "sq_done", "sum_done",
            "var_done", "root_done", "fd_done", "unit_done", "nyq_done", "h_done", "fix_done", "h0_out", "h1_out", "h2_out", "c0_out",
            "rows_done", "rows_evac", "cols_done", "mod_done"]
    bufs = [("w", [P, RING, KC, COLS]), ("fc0", [P, XT, SEQ]), ("fs0", [P, XT, SEQ]), ("fc1", [P, CT, CTX]), ("fs1", [P, CT, CTX]),
            ("decay0", [P, XT, HW]), ("decay1", [P, CT, HW]), ("feat0", [EMB, SEQ]), ("feat1", [EMB, CTX]),
            ("w1", [EMB, DEPTH, FFN]), ("w2", [P, FFN]), ("w3", [P, 4 * HW]), ("vec", [P, 3]),
            ("bias", [1, DEPTH, 2, HW]), ("a", [P, TOK]), ("k", [P, TOK]), ("h", [P, TOK]), ("rows", [P, 2, COLS]), ("sel", [P, 2]),
            ("f", [P, 2, 2, XT, HW]), ("sq", [P, 2, HW]), ("var", [P, 2, HW]), ("rn", [P, 2, HW]), ("out", [P, 3, 2, HW]),
            ("c0", [P, HW])]
    with stage(nc, "prep", sems, bufs) as (block, s):
        loaded, hd = [s["ada0_in"], s["ada1_in"], s["ada2_in"]], [s["h0_out"], s["h1_out"], s["h2_out"]]
        f, sq, var, rn, out = s["f"], s["sq"], s["var"], s["rn"], s["out"]
        SMALL = DEPTH * 7 + 2
        of_layer = [slice(l * FFN, (l + 1) * FFN) for l in range(DEPTH)]
        ada_src = a["w_ada"].rearrange("l (c p) n -> l p c n", p=P)

        def ada_wait(eng, g):
            if g >= 0:
                eng.wait_ge(s["mod_done"], g + 1)

        @block.sync
        def _(sp):
            for t, tag in ((0, "x"), (1, "c")):
                sp.dma_start(s[f"feat{t}"][:], consts[f"feat_{tag}"]).then_inc(s["small_in"], 16)
            for l in range(DEPTH):
                at = of_layer[l]
                for dst, src in ((s["w1"][:, l], a["flt_w1"][l]), (s["w2"][at], a["flt_w2"][l]), (s["w3"][at], a["flt_w3"][l]),
                                 (s["vec"][at, 0:1], a["flt_b1"][l][:, None]), (s["vec"][at, 1:2], a["flt_freq"][l][:, None]),
                                 (s["vec"][at, 2:3], a["flt_b2"][l][:, None]), (s["bias"][0:1, l], a["flt_bias"][l][None])):
                    sp.dma_start(dst, src).then_inc(s["small_in"], 16)
            for t, tag in ((0, "x"), (1, "c")):
                for name in ("decay", "fc", "fs"):
                    sp.dma_start(s[f"{name}{t}"][:], consts[f"{name}_{tag}"].rearrange("(j p) k -> p j k", p=P)).then_inc(s["mats_in"], 16)
            for g in range(DEPTH * BLOCKS):
                if g >= RING:
                    sp.wait_ge(s["rows_done"], g - RING + 1)
                sp.dma_start(s["w"][:, g % RING], ada_src[g // BLOCKS, :, :, (g % BLOCKS) * COLS:(g % BLOCKS + 1) * COLS]
                             ).then_inc(loaded[g % RING], 16)

        @block.tensor
        def _(pe):
            def ada(g):
                pe.wait_ge(loaded[g % RING], 16 * (g // RING + 1))
                ada_wait(pe, g - 2)
                for c in range(KC // 4):
                    for q in range(4):
                        k = q * KC // 4 + c
                        last = nc.tensor.matmul(m.ps[32 * q:32 * q + 32, g % 2], m.sil[:, k], s["w"][:, g % RING, k],
                                                start=c == 0, stop=c == KC // 4 - 1)
                last.then_inc(s["rows_done"], 1)

            def ada_columns(g):
                pe.wait_ge(s["rows_evac"], g + 1)
                for j in range(per):
                    last = nc.tensor.matmul(m.ps[:, g % 2, 2 * j:2 * j + 2], s["rows"][:, g % 2, j * P:(j + 1) * P], s["sel"][:],
                                            start=True, stop=True)
                last.then_inc(s["cols_done"], 1)

            def adas(first, n):
                for g in range(first, first + n):
                    ada(g)
                    if g > first:
                        ada_columns(g - 1)
                ada_columns(first + n - 1)

            def taps(k):
                i, l, t, o = items[k]
                J = tiles[k]
                ada_wait(pe, EACH * (k - 1) - 1)
                for q in range(2 * J + 1):
                    if q < 2 * J:
                        e, j = divmod(q, J)
                        if q >= 2:
                            pe.wait_ge(s["f_done"], 2 * before[k] + q - 1)
                        nc.tensor.matmul(m.ps[:, q % 2], s["h"][of_layer[l], t * SEQ + j * P:t * SEQ + (j + 1) * P],
                                         s["w3"][of_layer[l], (2 * o + e) * HW:(2 * o + e + 1) * HW],
                                         start=True, stop=True).then_inc(s["h3_done"], 1)
                    if q >= 1:
                        e, j = divmod(q - 1, J)
                        pe.wait_ge(s["sq_done"], 2 * before[k] + q)
                        if q == 1 and k:
                            pe.wait_ge(s["var_done"], k)
                            pe.wait_ge(s["fix_done"], k - 1) if k > 1 else None
                        nc.tensor.matmul(m.ps[:, 2 + e], m.ones[:], sq[:, (q - 1) % 2], start=j == 0,
                                         stop=j == J - 1).then_inc(s["sum_done"], 1)

            def transform(k):
                i, l, t, o = items[k]
                J, fc, fs = tiles[k], s[f"fc{t}"], s[f"fs{t}"]
                pe.wait_ge(s["fd_done"], 2 * k + 2)
                for j in range(J):
                    unit = before[k] + j
                    if unit >= 2:
                        pe.wait_ge(s["h_done"], unit - 1)
                    b = 4 + 2 * (unit % 2)
                    for x in range(J):
                        nc.tensor.matmul(m.ps[:, b], fc[:, x, j * P:(j + 1) * P], f[:, k % 2, 0, x], start=x == 0, stop=x == J - 1)
                    for x in range(J):
                        last = nc.tensor.matmul(m.ps[:, b + 1], fs[:, x, j * P:(j + 1) * P], f[:, k % 2, 1, x], start=x == 0, stop=x == J - 1)
                    last.then_inc(s["unit_done"], 1)
                    if j == 0:
                        if k + 1 < NI:
                            pe.wait_ge(s["var_done"], k + 2)
                        for x in range(J):
                            last = nc.tensor.matmul(m.ps[0:1, 2], fs[:, x, 0:1], f[:, k % 2, 0, x], start=x == 0, stop=x == J - 1)
                        last.then_inc(s["nyq_done"], 1)

            pe.wait_ge(s["small_in"], 16 * SMALL)
            for k in range(2):
                if k:
                    pe.wait_ge(s["sines"], 1)
                for l in range(DEPTH):
                    for t, at, n in spans(True):
                        last = nc.tensor.matmul(m.ps[of_layer[l], 4 + 2 * k + t, 0:n], s["w2"][of_layer[l]] if k else s["w1"][:, l],
                                                s["h"][of_layer[l], at:at + n] if k else s[f"feat{t}"][:], start=True, stop=True)
                last.then_inc(s["mlp_done"], 1)
            pe.wait_ge(s["sines"], 2)
            taps(0)
            for k in range(NI):
                if k + 1 < NI:
                    taps(k + 1)
                adas(EACH * k, 2)
                transform(k)
                adas(EACH * k + 2, EACH - 2)

        @block.scalar
        def _(act):
            def squares(k):
                J = tiles[k]
                for q in range(2 * J):
                    e, j = divmod(q, J)
                    act.wait_ge(s["f_done"], 2 * before[k] + q + 1)
                    if 2 * before[k] + q >= 2:
                        act.wait_ge(s["sum_done"], 2 * before[k] + q - 1)
                    nc.scalar.activation(sq[:, q % 2], f[:, k % 2, e, j], ACT.Square).then_inc(s["sq_done"], 1)

            def root(k):
                act.wait_ge(s["var_done"], k + 1)
                nc.scalar.activation(rn[:], var[:], ACT.Sqrt).then_inc(s["root_done"], 1)

            def store(k):
                i, l, t, o = items[k]
                J = tiles[k]
                for j in range(J):
                    unit = before[k] + j
                    b, r = 4 + 2 * (unit % 2), unit % 3
                    act.wait_ge(s["unit_done"], unit + 1)
                    if unit >= 3:
                        act.wait_ge(hd[r], 16 * (unit // 3))
                    if j == 0:
                        if k:
                            act.wait_ge(s["c0_out"], 16 * k)
                        nc.scalar.activation(s["c0"][:], m.ps[:, b], ACT.Copy)
                    nc.scalar.activation(out[:, r, 0], m.ps[:, b], ACT.Copy)
                    nc.scalar.activation(out[:, r, 1], m.ps[:, b + 1], ACT.Copy).then_inc(s["h_done"], 1)
                    act.wait_ge(s["h_done"], unit + 1)
                    if j == 0:
                        act.wait_ge(s["nyq_done"], k + 1)
                        nc.scalar.activation(s["c0"][0:1], m.ps[0:1, 2], ACT.Copy)
                        nc.scalar.mul(out[0:1, r, 1], out[0:1, r, 1], 0.0).then_inc(s["fix_done"], 1)
                        act.wait_ge(s["fix_done"], k + 1)
                        act.dma_start(dram["h"][l][t][o, :, 2 * J], s["c0"][:]).then_inc(s["c0_out"], 16)
                    act.dma_start(dram["h"][l][t][o, :, 2 * j:2 * j + 2], out[:, r]).then_inc(hd[r], 16)

            def evacuate(g):
                act.wait_ge(s["rows_done"], g + 1)
                if g >= 2:
                    act.wait_ge(s["cols_done"], g - 1)
                nc.scalar.activation(s["rows"][:, g % 2], m.ps[:, g % 2], ACT.Copy).then_inc(s["rows_evac"], 1)

            for k in range(2):
                act.wait_ge(s["dve"], 6 * (k + 1))
                if k:
                    act.wait_ge(s["mlp_done"], 2)
                nc.scalar.activation(s["h"][:], s["a"][:], ACT.Sin).then_inc(s["sines"], 1)
            squares(0)
            root(0)
            for k in range(NI):
                if k + 1 < NI:
                    squares(k + 1)
                evacuate(EACH * k)
                evacuate(EACH * k + 1)
                if k + 1 < NI:
                    root(k + 1)
                store(k)
                for g in range(2, EACH):
                    evacuate(EACH * k + g)
            for r in range(3):
                act.wait_ge(hd[r], 16 * len(range(r, before[NI], 3)))
            act.wait_ge(s["c0_out"], 16 * NI)

        @block.vector
        def _(dve):
            link = Chain(dve, s["dve"])

            def mod(g):
                l, blk = divmod(g, BLOCKS)
                dve.wait_ge(s["cols_done"], g + 1)
                got = m.ps[:, g % 2, 0:2 * per].rearrange("p (j s) -> p s j", s=2)
                at = blk * per
                for t in range(2):
                    last = nc.vector.tensor_tensor(m.mod[:, l, t, at:at + per], got[:, t], m.cols[:, l, R_ADA + at:R_ADA + at + per], ALU.add)
                last.then_inc(s["mod_done"], 1)

            def decayed(k):
                i, l, t, o = items[k]
                J = tiles[k]
                if k >= 2:
                    dve.wait_ge(s["unit_done"], before[k - 1])
                    dve.wait_ge(s["nyq_done"], k - 1)
                for q in range(2 * J):
                    e, j = divmod(q, J)
                    dve.wait_ge(s["h3_done"], 2 * before[k] + q + 1)
                    nc.vector.tensor_tensor(f[:, k % 2, e, j], m.ps[:, q % 2], s[f"decay{t}"][:, j], ALU.mult).then_inc(s["f_done"], 1)

            def normalised(k):
                _, l, _, o = items[k]
                J = tiles[k]
                g = f[:, k % 2]
                dve.wait_ge(s["sum_done"], 2 * before[k + 1])
                nc.vector.tensor_scalar_add(var[:], m.ps[:, 2:4], EPS).then_inc(s["var_done"], 1)
                dve.wait_ge(s["root_done"], k + 1)
                refined_rsqrt(nc, link, rn[:], var[:], sq[:])
                for e in range(2):
                    for j in range(J):
                        last = nc.vector.tensor_tensor(g[:, e, j], g[:, e, j], rn[:, e], ALU.mult)
                link(last)
                link(nc.vector.memset(g[0:1, 1, 0], 0.0))
                link(nc.vector.tensor_tensor(g[0:1, 0, 0], g[0:1, 0, 0], s["bias"][0:1, l, o], ALU.add))
                nc.vector.tensor_tensor(g[:, 0, 0:J], g[:, 0, 0:J], g[:, 1, 0:J], ALU.add).then_inc(s["fd_done"], 1)
                dve.wait_ge(s["fd_done"], 2 * k + 1)
                nc.vector.scalar_tensor_tensor(g[:, 1, 0:J], g[:, 1, 0:J], -2.0, g[:, 0, 0:J], ALU.mult, ALU.add).then_inc(s["fd_done"], 1)

            dve.wait_ge(s["small_in"], 16 * SMALL)
            nc.vector.tensor_reduce(s["sel"][:], m.ident.rearrange("p (q r) -> p r q", q=4)[:, 0:2], AX.X, ALU.add)
            x, kk = s["a"][:], s["k"][:]
            for k in range(2):
                dve.wait_ge(s["mlp_done"], k + 1)
                link(nc.vector.tensor_scalar(x, m.ps[:, 4 + 2 * k:6 + 2 * k].rearrange("p b n -> p (b n)")[:, 0:TOK],
                                             s["vec"][:, 2 * k:2 * k + 1], s["vec"][:, 1:2], ALU.add, ALU.mult))
                link(nc.vector.tensor_scalar(kk, x, 1.0 / TWO_PI, ROUND, ALU.mult, ALU.add))
                link(nc.vector.tensor_scalar_sub(kk, kk, ROUND))
                link(nc.vector.scalar_tensor_tensor(x, kk, -TWO_PI_HI, x, ALU.mult, ALU.add))
                link(nc.vector.scalar_tensor_tensor(x, kk, -(TWO_PI - TWO_PI_HI), x, ALU.mult, ALU.add))
                link(nc.vector.tensor_scalar(x, x, PI_BELOW, -PI_BELOW, ALU.min, ALU.max))
                dve.wait_ge(s["sines"], k + 1)
            dve.wait_ge(s["mats_in"], 16 * 6)
            decayed(0)
            normalised(0)
            for k in range(NI):
                if k + 1 < NI:
                    decayed(k + 1)
                mod(EACH * k)
                mod(EACH * k + 1)
                if k + 1 < NI:
                    normalised(k + 1)
                for g in range(2, EACH):
                    mod(EACH * k + g)
            dve.wait_ge(s["mod_done"], DEPTH * BLOCKS)
            for l in range(DEPTH):
                for t in range(2):
                    for k, (part, row) in enumerate(((1, R_G1), (4, R_G2))):
                        nc.vector.scalar_tensor_tensor(m.gain[:, l, t, k], m.mod[:, l, t, part * KC:(part + 1) * KC],
                                                       1.0, m.cols[:, l, row:row + KC], ALU.add, ALU.mult)


def norm_stage(nc, m, name, out, streams, gains, shifts, prefetch=None):
    n_tok = sum(n for _, _, n in streams)
    with stage(nc, name, ["sq_done", "sum_done", "chain", "root_done", "scaled"],
               [("sq", [P, 2, TOK]), ("rstd", [P, TOK]), ("var", [P, TOK])]) as (block, s):
        if prefetch:
            block.sync(prefetch)
        r, var = s["rstd"][:, 0:n_tok], s["var"][:, 0:n_tok]

        @block.scalar
        def _(act):
            for c in range(KC):
                if c >= 2:
                    act.wait_ge(s["sum_done"], c - 1)
                nc.scalar.activation(s["sq"][:, c % 2, 0:n_tok], m.resid[:, c, 0:n_tok], ACT.Square).then_inc(s["sq_done"], 1)
            act.wait_ge(s["chain"], 1)
            nc.scalar.activation(r, var, ACT.Sqrt).then_inc(s["root_done"], 1)
            for c in range(KC):
                act.wait_ge(s["scaled"], c + 1)
                for t, at, n in streams:
                    o = out[:, c, at:at + n]
                    if shifts is None:
                        nc.scalar.activation(o, o, ACT.Identity, scale=gains(t, c))
                    else:
                        nc.scalar.activation(o, o, ACT.Identity, scale=gains(t, c), bias=shifts(t, c))

        @block.tensor
        def _(pe):
            for c in range(KC):
                pe.wait_ge(s["sq_done"], c + 1)
                for t, at, n in streams:
                    last = nc.tensor.matmul(m.ps[:, t, 0:n], m.ones[:], s["sq"][:, c % 2, at:at + n],
                                            start=c == 0, stop=c == KC - 1)
                last.then_inc(s["sum_done"], 1)

        @block.vector
        def _(dve):
            link = Chain(dve, s["chain"])
            dve.wait_ge(s["sum_done"], KC)
            for t, at, n in streams:
                last = nc.vector.tensor_scalar(s["var"][:, at:at + n], m.ps[:, t, 0:n], 1.0 / D, EPS, ALU.mult, ALU.add)
            link(last)
            dve.wait_ge(s["root_done"], 1)
            refined_rsqrt(nc, link, r, var, s["sq"][:, 0, 0:n_tok])
            for c in range(KC):
                nc.vector.tensor_tensor(out[:, c, 0:n_tok], m.resid[:, c, 0:n_tok], r, ALU.mult).then_inc(s["scaled"], 1)


def hyena_in_stage(nc, m, l, w_in, streams):
    n_tok = sum(n for _, _, n in streams)
    tiles = n_tok // P
    NT = 3 * HC
    PAD = TOK + 4
    first = {0: 1, 1: SEQ + 3}
    with stage(nc, f"hyin{l}", ["w0", "w1", "w_used", "mm_done", "p_done", "mid_done", "conv_done", "zeroed", "taps",
                                "tr_done", "tr_evac"],
               [("w", [P, 2, KC, HW]), ("p", [P, 2, PAD]), ("conv", [P, 2, TOK])]) as (block, s):
        loaded = [s["w0"], s["w1"]]
        src = w_in[l].rearrange("(c p) n -> p c n", p=P)

        def col(row, i):
            return m.cols[:, l, row + i:row + i + 1]

        @block.sync
        def _(sp):
            for g in range(3):
                if g == 2:
                    sp.wait_ge(s["mm_done"], HC)
                sp.dma_start(s["w"][:, g % 2], src[:, :, g * HW:(g + 1) * HW]).then_inc(loaded[g % 2], 16)

        @block.tensor
        def _(pe):
            def transposes(i):
                pe.wait_ge(s["conv_done"], i + 1)
                if i >= 1:
                    pe.wait_ge(s["tr_evac"], 2 * i)
                for j in range(tiles):
                    last = nc.tensor.transpose(m.ps[:, 4 + j // 4, (j % 4) * P:(j % 4 + 1) * P],
                                               s["conv"][:, i % 2, j * P:(j + 1) * P], m.ident[:])
                last.then_inc(s["tr_done"], 1)

            for i in range(NT):
                if i % HC == 0:
                    g = i // HC
                    pe.wait_ge(loaded[g % 2], 16 * (g // 2 + 1))
                if i >= 2:
                    pe.wait_ge(s["p_done"], i - 1)
                    pe.wait_ge(s["mid_done"], i - 1)
                for t, at, n in streams:
                    for c in range(KC):
                        last = nc.tensor.matmul(m.ps[:, 2 * (i % 2) + t, 0:n], s["w"][:, (i // HC) % 2, c, (i % HC) * P:(i % HC + 1) * P],
                                                m.u[:, c, at:at + n], start=c == 0, stop=c == KC - 1)
                last.then_inc(s["mm_done"], 1)
                if 1 <= i <= 2 * HC:
                    transposes(i - 1)

        @block.scalar
        def _(act):
            act.wait_ge(s["zeroed"], 1)
            for i in range(NT):
                act.wait_ge(s["mm_done"], i + 1)
                if i >= 2:
                    act.wait_ge(s["conv_done"], i - 1)
                for t, at, n in streams:
                    last = nc.scalar.activation(s["p"][:, i % 2, first[t]:first[t] + n], m.ps[:, 2 * (i % 2) + t, 0:n], ACT.Copy)
                last.then_inc(s["p_done"], 1)
                dst = s["conv"][:, i % 2] if i < 2 * HC else m.x2[:, i - 2 * HC]
                if 2 <= i < 2 * HC:
                    act.wait_ge(s["tr_done"], i - 1)
                for t, at, n in streams:
                    last = nc.scalar.activation(dst[:, at:at + n], m.ps[:, 2 * (i % 2) + t, 0:n], ACT.Identity,
                                                scale=col(R_SCW + NT, i), bias=col(R_SCB, i))
                last.then_inc(s["mid_done"], 1)
                if 2 <= i <= 2 * HC + 1:
                    k = i - 2
                    act.wait_ge(s["tr_done"], k + 1)
                    dst = m.v if k < HC else m.x1
                    for half in range(2):
                        a, b = 4 * half, min(4 * half + 4, tiles)
                        if a < b:
                            ins = nc.scalar.activation(dst[:, a:b, (k % HC) * P:(k % HC + 1) * P],
                                                       m.ps[:, 4 + half, 0:(b - a) * P].rearrange("p (j c) -> p j c", c=P),
                                                       ACT.Copy)
                            ins.then_inc(s["tr_evac"], 1 if tiles > 4 else 2)

        @block.vector
        def _(dve):
            nc.vector.memset(s["p"][:], 0.0).then_inc(s["zeroed"], 1)
            for i in range(NT):
                dst = s["conv"][:, i % 2] if i < 2 * HC else m.x2[:, i - 2 * HC]
                dve.wait_ge(s["mid_done"], i + 1)
                dve.wait_ge(s["p_done"], i + 1)
                for k, tap in enumerate((0, 2)):
                    for t, at, n in streams:
                        f = first[t] + tap - 1
                        last = nc.vector.scalar_tensor_tensor(dst[:, at:at + n], s["p"][:, i % 2, f:f + n],
                                                              col(R_SCW + tap * NT, i), dst[:, at:at + n],
                                                              ALU.mult, ALU.add)
                    if k == 0:
                        last.then_inc(s["taps"], 1)
                        dve.wait_ge(s["taps"], i + 1)
                last.then_inc(s["conv_done"], 1)


def conv_stage(nc, m, l, t, consts, dram):
    n, at, tag = (SEQ, 0, "x") if t == 0 else (CTX, SEQ, "c")
    J = n // P
    tok0 = at // P
    planes = transfer_planes(t)
    sems = ["fc_in", "fs_in", "inv_in", "h0_in", "h1_in", "unit_done", "t_done", "y_done", "inv_done", "inv_evac"]
    bufs = [("fc", [P, J, n]), ("fs", [P, J, n]), ("ic", [P, J, n]), ("is", [P, J, n]), ("h", [P, 2, planes, HW]),
            ("y", [P, 2, J, HW]), ("t", [P, 2, 4, HW])]
    with stage(nc, f"conv{l}{tag}", sems, bufs) as (block, s):
        y, h, prod = s["y"], s["h"], s["t"]
        h_in = [s["h0_in"], s["h1_in"]]

        @block.sync
        def _(sp):
            def matrix(name, sem):
                sp.dma_start(s[name][:], consts[f"{name}_{tag}"].rearrange("(j p) k -> p j k", p=P)).then_inc(sem, 16)

            matrix("fc", s["fc_in"])
            matrix("fs", s["fs_in"])
            sp.dma_start(h[:, 0], dram["h"][l][t][0]).then_inc(h_in[0], 16)
            matrix("ic", s["inv_in"])
            matrix("is", s["inv_in"])
            sp.dma_start(h[:, 1], dram["h"][l][t][1]).then_inc(h_in[1], 16)

        @block.tensor
        def _(pe):
            for o in range(2):
                z = m.v if o == 0 else m.x1
                if o:
                    pe.wait_ge(s["inv_evac"], J)
                for j in range(J):
                    unit = o * J + j
                    b = 4 + 2 * (unit % 2)
                    if unit >= 2:
                        pe.wait_ge(s["t_done"], unit - 1)
                    for mat, bank, sem in ((s["fc"], b, s["fc_in"]), (s["fs"], b + 1, s["fs_in"])):
                        pe.wait_ge(sem, 16)
                        for i in range(J):
                            last = nc.tensor.matmul(m.ps[:, bank], mat[:, i, j * P:(j + 1) * P], z[:, tok0 + i],
                                                    start=i == 0, stop=i == J - 1)
                    last.then_inc(s["unit_done"], 1)
                pe.wait_ge(s["inv_in"], 32)
                outs = J if o == 0 else HC
                for j in range(J):
                    pe.wait_ge(s["y_done"], 2 * (o * J + j + 1))
                    for q in range(outs):
                        if j == 0 and o == 1:
                            pe.wait_ge(s["inv_evac"], J)
                        for e, mat in ((0, s["ic"]), (1, s["is"])):
                            first, stop = j == 0 and e == 0, j == J - 1 and e == 1
                            if o == 0:
                                last = nc.tensor.matmul(m.ps[:, q], mat[:, j, q * P:(q + 1) * P], y[:, e, j], start=first, stop=stop)
                            else:
                                last = nc.tensor.matmul(m.ps[:, q, 0:n], y[:, e, j, q * P:(q + 1) * P], mat[:, j], start=first, stop=stop)
                        if j == J - 1:
                            last.then_inc(s["inv_done"], 1)

        @block.vector
        def _(dve):
            for o in range(2):
                dve.wait_ge(h_in[o], 16)
                for j in range(J):
                    unit = o * J + j
                    b = 4 + 2 * (unit % 2)
                    dve.wait_ge(s["unit_done"], unit + 1)
                    if unit >= 2:
                        dve.wait_ge(s["y_done"], 2 * (unit - 1))
                    zr, zi, hr, hi = m.ps[:, b], m.ps[:, b + 1], h[:, o, 2 * j], h[:, o, 2 * j + 1]
                    w = prod[:, unit % 2]
                    nc.vector.tensor_tensor(w[:, 0], zr, hr, ALU.mult)
                    nc.vector.tensor_tensor(w[:, 1], zi, hi, ALU.mult)
                    nc.vector.tensor_tensor(w[:, 2], zr, hi, ALU.mult)
                    nc.vector.tensor_tensor(w[:, 3], zi, h[:, o, 2 * J] if j == 0 else hr, ALU.mult).then_inc(s["t_done"], 1)
                for q in range(J if o == 0 else HC):
                    dve.wait_ge(s["inv_done"], J * o + q + 1)
                    if o == 0:
                        x = m.x1[:, tok0 + q]
                        nc.vector.tensor_tensor(x, m.ps[:, q], x, ALU.mult).then_inc(s["inv_evac"], 1)
                    else:
                        nc.vector.tensor_tensor(m.yh[:, q, at:at + n], m.ps[:, q, 0:n], m.x2[:, q, at:at + n],
                                                ALU.mult).then_inc(s["inv_evac"], 1)

        @block.gpsimd
        def _(pool):
            for k in range(2 * J):
                o, j = divmod(k, J)
                pool.wait_ge(s["t_done"], k + 1)
                if o:
                    pool.wait_ge(s["inv_done"], J)
                w = prod[:, k % 2]
                nc.gpsimd.tensor_tensor(y[:, 0, j], w[:, 0], w[:, 1], ALU.subtract).then_inc(s["y_done"], 1)
                nc.gpsimd.tensor_tensor(y[:, 1, j], w[:, 2], w[:, 3], ALU.add).then_inc(s["y_done"], 1)


def qkv_stage(nc, m, l, w_in, w_ukv, consts, streams_q):
    both = spans(True)
    NU = QC + KVC + 1
    src = w_in[l].rearrange("(c p) n -> p c n", p=P)
    with stage(nc, f"qkv{l}", ["w_in", "wkr_in", "wv_in", "rope_in", "zeroed", "swapped", "mm_done", "raw_done", "sq_done",
                               "sum_done", "dve", "root_done", "rope_done", "norm_done", "v_done", "v_evac"],
               [("w", [P, KC, QL + KVL]), ("wkr", [P, KC, P]), ("wv", [P, KVC, HEADS, VD]), ("raw", [P, QC + KVC, TOK]),
                ("sq", [P, 2, TOK]), ("r", [P, 2, TOK]), ("var", [P, 2, TOK]), ("t", [P, 2, SEQ]), ("g", [P, QC])]) as (block, s):
        def streams(i):
            return streams_q if i < QC else both

        @block.sync
        def _(sp):
            sp.dma_start(s["w"][:], src[:, :, Q0:KR0]).then_inc(s["w_in"], 16)
            sp.wait_ge(s["zeroed"], 1)
            sp.dma_start(s["wkr"][:, :, NOPE:QK], src[:, :, KR0:G0]).then_inc(s["wkr_in"], 16)
            sp.dma_start(m.rope[:], consts["rope"]).then_inc(s["rope_in"], 16)
            for c in range(KVC):
                v_cols = w_ukv[l, c * P:(c + 1) * P].rearrange("p (h k) -> p h k", h=HEADS)[:, :, NOPE:NOPE + VD]
                sp.dma_start(s["wv"][:, c], v_cols).then_inc(s["wv_in"], 16)

        @block.gpsimd
        def _(pool):
            nc.gpsimd.memset(s["wkr"][:], 0.0).then_inc(s["zeroed"], 1)
            pool.wait_ge(s["wkr_in"], 16)
            raw = s["wkr"][:, :, NOPE:QK].rearrange("p c (a h k) -> p c a h k", a=2, h=2)
            swap = s["wkr"][:, :, QK:P].rearrange("p c (a h k) -> p c a h k", a=2, h=2)
            for h in range(2):
                for a in range(2):
                    nc.gpsimd.tensor_copy(swap[:, :, a, h], raw[:, :, a, 1 - h]).then_inc(s["swapped"], 1)

        @block.tensor
        def _(pe):
            def sums(i):
                pe.wait_ge(s["sq_done"], i + 1)
                k, c, last_c = (0, i, QC - 1) if i < QC else (1, i - QC, KVC - 1)
                for t, at, n in streams(i):
                    last = nc.tensor.matmul(m.ps[:, 4 + 2 * k + t, 0:n], m.ones[:], s["sq"][:, i % 2, at:at + n],
                                            start=c == 0, stop=c == last_c)
                last.then_inc(s["sum_done"], 1)

            pe.wait_ge(s["w_in"], 16)
            for i in range(NU):
                if i >= 2:
                    pe.wait_ge(s["sq_done"], i - 1)
                    pe.wait_ge(s["raw_done"], i - 1)
                if i == NU - 1:
                    pe.wait_ge(s["swapped"], 4)
                for t, at, n in streams(i):
                    for c in range(KC):
                        lhs = s["w"][:, c, i * P:(i + 1) * P] if i < NU - 1 else s["wkr"][:, c]
                        last = nc.tensor.matmul(m.ps[:, 2 * (i % 2) + t, 0:n], lhs, m.u[:, c, at:at + n],
                                                start=c == 0, stop=c == KC - 1)
                last.then_inc(s["mm_done"], 1)
                if i >= 1:
                    sums(i - 1)
            pe.wait_ge(s["wv_in"], 16 * KVC)
            pe.wait_ge(s["norm_done"], QC + KVC)
            for j in range(TT):
                if j >= 2:
                    pe.wait_ge(s["v_evac"], j - 1)
                for c in range(KVC):
                    last = nc.tensor.matmul(m.ps[:, j % 2], m.kvn[:, c, j * P:(j + 1) * P], s["wv"][:, c],
                                            start=c == 0, stop=c == KVC - 1)
                last.then_inc(s["v_done"], 1)

        @block.scalar
        def _(act):
            nc.scalar.mul(s["g"][:], m.cols[:, l, R_QG:R_QG + QC], SCALE)
            for i in range(NU - 1):
                act.wait_ge(s["mm_done"], i + 1)
                for t, at, n in streams(i):
                    last = nc.scalar.activation(s["raw"][:, i, at:at + n], m.ps[:, 2 * (i % 2) + t, 0:n], ACT.Copy)
                last.then_inc(s["raw_done"], 1)
                if i >= 2:
                    act.wait_ge(s["sum_done"], i - 1)
                for t, at, n in streams(i):
                    last = nc.scalar.activation(s["sq"][:, i % 2, at:at + n], m.ps[:, 2 * (i % 2) + t, 0:n], ACT.Square)
                last.then_inc(s["sq_done"], 1)
            act.wait_ge(s["dve"], 1)
            nc.scalar.activation(s["r"][:], s["var"][:], ACT.Sqrt).then_inc(s["root_done"], 1)
            for j in range(TT):
                act.wait_ge(s["v_done"], j + 1)
                nc.scalar.activation(m.vt[:, j], m.ps[:, j % 2], ACT.Copy).then_inc(s["v_evac"], 1)

        @block.vector
        def _(dve):
            link = Chain(dve, s["dve"])
            last = None
            if len(streams_q) == 1:
                nc.vector.memset(s["var"][:, 0, SEQ:TOK], 1.0)
            dve.wait_ge(s["sum_done"], QC + KVC)
            for k, width in ((0, QL), (1, KVL)):
                for t, at, n in (streams_q, both)[k]:
                    last = nc.vector.tensor_scalar(s["var"][:, k, at:at + n], m.ps[:, 4 + 2 * k + t, 0:n], 1.0 / width, EPS,
                                                   ALU.mult, ALU.add)
            link(last)
            dve.wait_ge(s["root_done"], 1)
            refined_rsqrt(nc, link, s["r"][:], s["var"][:], s["sq"][:])
            for i in range(QC + KVC):
                n = sum(n for _, _, n in streams(i))
                k, out, g = (0, m.qn[:, i, 0:n], s["g"][:, i:i + 1]) if i < QC else \
                    (1, m.kvn[:, i - QC, 0:n], m.cols[:, l, R_KVG + i - QC:R_KVG + i - QC + 1])
                nc.vector.scalar_tensor_tensor(out, s["raw"][:, i, 0:n], g, s["r"][:, k, 0:n], ALU.mult,
                                               ALU.mult).then_inc(s["norm_done"], 1)
            b = 2 * ((NU - 1) % 2)
            dve.wait_ge(s["mm_done"], NU)
            dve.wait_ge(s["rope_in"], 16)
            nc.vector.tensor_tensor(s["t"][NOPE:QK, 0], m.ps[NOPE:QK, b], m.rope[NOPE:QK], ALU.mult)
            link(nc.vector.tensor_tensor(s["t"][NOPE:QK, 1], m.ps[QK:P, b], m.rope[QK:P], ALU.mult))
            for h in range(2):
                nc.vector.tensor_tensor(m.key[NOPE:QK, h, 0:SEQ], s["t"][NOPE:QK, 0], s["t"][NOPE:QK, 1], ALU.add)
                nc.vector.tensor_copy(m.key[NOPE:QK, h, SEQ:TOK], m.ps[NOPE:QK, b + 1, 0:CTX])


def attention_stage(nc, m, l, w_uq, w_ukv, streams_q):
    n_q = sum(n for _, _, n in streams_q)
    units = [(j, 0, TOK) for j in range(XT)] + [(XT + j, SEQ, CTX) for j in range((n_q - SEQ) // P)]
    NU = 2 * len(units)
    NT = n_q // P
    ctx_q = len(streams_q) > 1
    wq_src = w_uq[l].rearrange("(c p) (h k) -> p c h k", p=P, k=QK)
    wk_src = w_ukv[l].rearrange("(c p) (h k) -> p c h k", p=P, k=NOPE + VD)
    work = [(h, *u) for h in range(2) for u in units]
    with stage(nc, f"attn{l}", ["w0", "w1", "swapped", "turns", "proj_done", "q_done", "dve", "rot_done", "qk_done",
                                "s_done", "max_done", "exp_done", "tr_done", "ta_done", "tv_done", "pv_done", "o_done",
                                "back", "back_evac"],
               [("wq", [P, 2, QC, P]), ("wk", [P, 2, KVC, NOPE]), ("t", [P, 2, SEQ]), ("qrot", [P, 2, SEQ]),
                ("q", [P, 2, TOK]), ("p", [P, 2, TOK]), ("pt", [P, 2, TT, P]), ("nm", [P, 2]), ("sum", [P, 4]),
                ("rs", [P, 2]), ("otok", [P, TT, HEADS * VD])]) as (block, s):
        loaded = [s["w0"], s["w1"]]

        def act_share(nk):
            return 4 if nk == TOK else nk // P // 2

        def proj_bank(h):
            return 4 if h == 0 else 0

        @block.sync
        def _(sp):
            with sp.Fori(0, HEADS // 2) as i:
                for h in range(2):
                    sp.wait_ge(s["proj_done"], i * 4 + (2 * h + 2))
                    sp.dma_start(s["wq"][:, h, :, 0:QK], wq_src[:, :, i * 2 + h]).then_inc(loaded[h], 16)
                    sp.dma_start(s["wk"][:, h], wk_src[:, :, i * 2 + h, 0:NOPE]).then_inc(loaded[h], 16)

        @block.gpsimd
        def _(pool):
            with pool.Fori(0, HEADS // 2) as i:
                for h in range(2):
                    pool.wait_ge(loaded[h], i * 32 + 32)
                    pool.sem_inc(s["turns"], 1)
                    raw = s["wq"][:, h, :, NOPE:QK].rearrange("p c (a h k) -> p c a h k", a=2, h=2)
                    swap = s["wq"][:, h, :, QK:P].rearrange("p c (a h k) -> p c a h k", a=2, h=2)
                    for b in range(2):
                        for a in range(2):
                            nc.gpsimd.tensor_copy(swap[:, :, a, b], raw[:, :, a, 1 - b]).then_inc(s["swapped"], 1)

        @block.tensor
        def _(pe):
            pe.sem_inc(s["proj_done"], 4)
            pe.sem_inc(s["tr_done"], 2)
            pe.sem_inc(s["pv_done"], 2)

            def project(i, h):
                pe.wait_ge(loaded[h], i * 32 + 32)
                pe.wait_ge(s["swapped"], i * 8 + (4 * h + 4))
                b = proj_bank(h)
                for bank, off, n, at, wide in ((b, 0, SEQ, 0, True), (b + 1, 0, SEQ, 0, False),
                                               (b + 2, 0, CTX, SEQ, True), (b + 2, CTX, CTX, SEQ, False)):
                    if wide and at and not ctx_q:
                        continue
                    w, z, k = (s["wq"], m.qn, QC) if wide else (s["wk"], m.kvn, KVC)
                    out = m.ps[0:P if wide else NOPE, bank, off:off + n]
                    for c in range(k):
                        last = nc.tensor.matmul(out, w[:, h, c], z[:, c, at:at + n], start=c == 0, stop=c == k - 1)
                    if wide and not at:
                        last.then_inc(s["proj_done"], 1)
                last.then_inc(s["proj_done"], 1)

            def scores(i, u):
                h, j, k0, nk = work[u]
                pe.wait_ge(s["exp_done"], i * NU + (u + 1))
                b = 2 * (u % 2)
                if j < XT:
                    nc.tensor.matmul(m.ps[:, b], s["qrot"][0:QK, h, j * P:(j + 1) * P], m.key[0:QK, h, 0:SEQ], start=True, stop=True)
                off = 1 if j < XT else 0
                nc.tensor.matmul(m.ps[:, b + off, 0:CTX], s["q"][0:QK, h, j * P:(j + 1) * P], m.key[0:QK, h, SEQ:TOK],
                                 start=True, stop=True).then_inc(s["s_done"], 1)

            def transposes(i, u):
                _, _, _, nk = work[u]
                pe.wait_ge(s["exp_done"], i * NU + (u + 3))
                pe.wait_ge(s["ta_done"], i * NU + (u + 1))
                pe.wait_ge(s["tv_done"], i * NU + (u + 1))
                na = act_share(nk)
                for k in range(nk // P):
                    kb = k if k < na else k - na
                    last = nc.tensor.transpose(m.ps[:, 4 if k < na else 5, kb * P:(kb + 1) * P],
                                               s["p"][:, u % 2, k * P:(k + 1) * P], m.ident[:])
                last.then_inc(s["tr_done"], 1)

            def values(i, u):
                h, j, k0, nk = work[u]
                pe.wait_ge(s["ta_done"], i * NU + (u + 2))
                pe.wait_ge(s["tv_done"], i * NU + (u + 2))
                pe.wait_ge(s["o_done"], i * NU + (u + 1))
                for k in range(nk // P):
                    last = nc.tensor.matmul(m.ps[:, 6 + u % 2, 0:VD], s["pt"][:, u % 2, k],
                                            m.vt[:, k0 // P + k, bass.ds((i * 2 + h) * VD, VD)], start=k == 0, stop=k == nk // P - 1)
                last.then_inc(s["pv_done"], 1)

            with pe.Fori(0, HEADS // 2) as i:
                pe.wait_ge(s["exp_done"], i * NU + 2)
                pe.wait_ge(s["ta_done"], i * NU + 1)
                pe.wait_ge(s["tv_done"], i * NU + 1)
                pe.wait_ge(s["o_done"], i * NU + 2)
                for h in range(2):
                    project(i, h)
                pe.wait_ge(s["q_done"], i * 2 + 2)
                pe.wait_ge(s["qk_done"], i * 2 + 2)
                for u in range(NU + 2):
                    if u < NU:
                        scores(i, u)
                    if 1 <= u <= NU:
                        transposes(i, u - 1)
                    if u >= 2:
                        values(i, u - 2)
            pe.wait_ge(s["o_done"], HEADS // 2 * NU + 2)
            for j in range(NT):
                if j >= 2:
                    pe.wait_ge(s["back_evac"], j - 1)
                for c in range(HC):
                    last = nc.tensor.transpose(m.ps[:, j % 2, c * P:(c + 1) * P], s["otok"][:, j, c * P:(c + 1) * P], m.ident[:])
                last.then_inc(s["back"], 1)

        @block.scalar
        def _(act):
            act.sem_inc(s["exp_done"], 2)
            act.sem_inc(s["ta_done"], 1)

            def copy_projected(i, h):
                b = proj_bank(h)
                act.wait_ge(s["proj_done"], i * 4 + (2 * h + 6))
                if h == 0:
                    act.wait_ge(s["pv_done"], i * NU + 2)
                nc.scalar.activation(m.key[0:NOPE, h, 0:SEQ], m.ps[0:NOPE, b + 1], ACT.Copy)
                if ctx_q:
                    nc.scalar.activation(s["q"][0:QK, h, SEQ:TOK], m.ps[0:QK, b + 2, 0:CTX], ACT.Copy)
                nc.scalar.activation(m.key[0:NOPE, h, SEQ:TOK], m.ps[0:NOPE, b + 2, CTX:2 * CTX], ACT.Copy)
                act.wait_ge(s["rot_done"], i * 2 + (h + 1))
                nc.scalar.activation(s["q"][0:QK, h, 0:SEQ], m.ps[0:QK, b], ACT.Copy).then_inc(s["qk_done"], 1)

            def exponential(i, u):
                h, j, k0, nk = work[u]
                act.wait_ge(s["max_done"], i * NU + (u + 1))
                act.wait_ge(s["tr_done"], i * NU + (u + 1))
                b = 2 * (u % 2)
                nc.scalar.activation(s["p"][:, u % 2, 0:nk], m.ps[:, b:b + 2].rearrange("p b k -> p (b k)")[:, 0:nk], ACT.Exp,
                                     bias=s["nm"][:, u % 2:u % 2 + 1], accum_out=s["sum"][:, u % 4:u % 4 + 1]).then_inc(s["exp_done"], 1)

            def copy_transposed(i, u):
                _, _, _, nk = work[u]
                act.wait_ge(s["tr_done"], i * NU + (u + 3))
                act.wait_ge(s["pv_done"], i * NU + (u + 1))
                n = act_share(nk)
                nc.scalar.activation(s["pt"][:, u % 2, 0:n], m.ps[:, 4, 0:n * P].rearrange("p (k q) -> p k q", q=P),
                                     ACT.Copy).then_inc(s["ta_done"], 1)

            with act.Fori(0, HEADS // 2) as i:
                for h in range(2):
                    copy_projected(i, h)
                for u in range(NU + 1):
                    if u < NU:
                        exponential(i, u)
                    if u >= 1:
                        copy_transposed(i, u - 1)

        @block.vector
        def _(dve):
            dve.sem_inc(s["tv_done"], 1)
            dve.sem_inc(s["o_done"], 2)

            def rotate(i, h):
                b = proj_bank(h)
                dve.wait_ge(s["proj_done"], i * 4 + (2 * h + 5))
                if h == 0:
                    dve.wait_ge(s["pv_done"], i * NU + 2)
                nc.vector.tensor_tensor(s["t"][NOPE:QK, 0], m.ps[NOPE:QK, b], m.rope[NOPE:QK], ALU.mult)
                nc.vector.tensor_tensor(s["t"][NOPE:QK, 1], m.ps[QK:P, b], m.rope[QK:P], ALU.mult)
                nc.vector.tensor_copy(s["qrot"][0:NOPE, h], m.ps[0:NOPE, b]).then_inc(s["rot_done"], 1)
                dve.wait_ge(s["rot_done"], i * 2 + (h + 1))
                nc.vector.tensor_tensor(s["qrot"][NOPE:QK, h], s["t"][NOPE:QK, 0], s["t"][NOPE:QK, 1], ALU.add).then_inc(s["q_done"], 1)
                dve.wait_ge(s["q_done"], i * 2 + (h + 1))

            def maximum(i, u):
                h, j, k0, nk = work[u]
                dve.wait_ge(s["s_done"], i * NU + (u + 1))
                dve.wait_ge(s["exp_done"], i * NU + (u + 1))
                b = 2 * (u % 2)
                nc.vector.tensor_reduce(s["nm"][:, u % 2:u % 2 + 1], m.ps[:, b:b + 2].rearrange("p b k -> p (b k)")[:, 0:nk],
                                        axis=AX.X, op=ALU.max, negate=True).then_inc(s["max_done"], 1)

            def copy_transposed(i, u):
                _, _, _, nk = work[u]
                dve.wait_ge(s["tr_done"], i * NU + (u + 3))
                dve.wait_ge(s["pv_done"], i * NU + (u + 1))
                na, n = act_share(nk), nk // P - act_share(nk)
                nc.vector.tensor_copy(s["pt"][:, u % 2, na:na + n],
                                      m.ps[:, 5, 0:n * P].rearrange("p (k q) -> p k q", q=P)).then_inc(s["tv_done"], 1)

            def output(i, u):
                h, j, k0, nk = work[u]
                r = s["rs"][:, u % 2:u % 2 + 1]
                dve.wait_ge(s["o_done"], i * NU + (u + 1))
                nc.vector.reciprocal(r, s["sum"][:, u % 4:u % 4 + 1]).then_inc(s["dve"], 1)
                dve.wait_ge(s["dve"], i * NU + (u + 1))
                dve.wait_ge(s["pv_done"], i * NU + (u + 3))
                nc.vector.tensor_scalar_mul(s["otok"][:, j, bass.ds((i * 2 + h) * VD, VD)], m.ps[:, 6 + u % 2, 0:VD],
                                            r).then_inc(s["o_done"], 1)

            with dve.Fori(0, HEADS // 2) as i:
                for h in range(2):
                    rotate(i, h)
                for u in range(NU + 2):
                    if u < NU:
                        maximum(i, u)
                    if 1 <= u <= NU:
                        copy_transposed(i, u - 1)
                    if u >= 2:
                        output(i, u - 2)
            for j in range(NT):
                dve.wait_ge(s["back"], j + 1)
                nc.vector.tensor_copy(m.ya[:, :, j * P:(j + 1) * P],
                                      m.ps[:, j % 2].rearrange("p (c t) -> p c t", c=HC)).then_inc(s["back_evac"], 1)


def merge_stage(nc, m, l, w_in, w_hy_o, w_mla_o, streams):
    NS = len(streams)
    KW = 2 * KC + 2 * HC
    w_src = w_in[l].rearrange("(c p) n -> p c n", p=P)
    hy_src = w_hy_o[l].rearrange("(c p) n -> p c n", p=P)
    mla_src = w_mla_o[l].rearrange("(c p) n -> p c n", p=P)
    with stage(nc, f"merge{l}", ["w0", "w1", "mm_done", "sig_done", "prod_done", "mix_done"],
               [("w", [P, 2, KW, P]), ("sig", [P, 2, 2, SEQ]), ("t", [P, 2, 2, SEQ])]) as (block, s):
        loaded = [s["w0"], s["w1"]]

        @block.sync
        def _(sp):
            with sp.Fori(0, KC // 2) as i:
                for b in range(2):
                    sp.wait_ge(s["mm_done"], i * (2 * NS) + (b + 1) * NS)
                    for at, n, src, col in ((0, KC, w_src, G0), (KC, KC, w_src, G0 + D), (2 * KC, HC, hy_src, 0),
                                            (2 * KC + HC, HC, mla_src, 0)):
                        sp.dma_start(s["w"][:, b, at:at + n], src[:, :, bass.ds(i * (2 * P) + (b * P + col), P)]).then_inc(loaded[b], 16)

        @block.tensor
        def _(pe):
            pe.sem_inc(s["mm_done"], 2 * NS)
            with pe.Fori(0, KC // 2) as i:
                for b in range(2):
                    pe.wait_ge(loaded[b], i * 64 + 64)
                    for t, at, n in streams:
                        k = b * NS + t
                        pe.wait_ge(s["prod_done"], i * (2 * NS) + (k + 1))
                        q = 4 * (k % 2)
                        for bank, w_at, z, kn in ((q, 0, m.u, KC), (q + 1, KC, m.u, KC), (q + 2, 2 * KC, m.yh, HC),
                                                  (q + 3, 2 * KC + HC, m.ya, HC)):
                            for c in range(kn):
                                last = nc.tensor.matmul(m.ps[:, bank, 0:n], s["w"][:, b, w_at + c], z[:, c, at:at + n],
                                                        start=c == 0, stop=c == kn - 1)
                        last.then_inc(s["mm_done"], 1)

        @block.scalar
        def _(act):
            with act.Fori(0, KC // 2) as i:
                for b in range(2):
                    for t, at, n in streams:
                        k = b * NS + t
                        act.wait_ge(s["mm_done"], i * (2 * NS) + (k + 1 + 2 * NS))
                        act.wait_ge(s["prod_done"], i * (2 * NS) + (k + 1))
                        nc.scalar.activation(s["sig"][:, k % 2, :, 0:n], m.ps[:, 4 * (k % 2):4 * (k % 2) + 2, 0:n],
                                             ACT.Sigmoid).then_inc(s["sig_done"], 1)

        @block.vector
        def _(dve):
            dve.sem_inc(s["prod_done"], 2)
            with dve.Fori(0, KC // 2) as i:
                for b in range(2):
                    for t, at, n in streams:
                        k = b * NS + t
                        dve.wait_ge(s["sig_done"], i * (2 * NS) + (k + 1))
                        dve.wait_ge(s["mix_done"], i * (2 * NS) + (k + 1))
                        nc.vector.tensor_tensor(s["t"][:, k % 2, :, 0:n], m.ps[:, 4 * (k % 2) + 2:4 * (k % 2) + 4, 0:n],
                                                s["sig"][:, k % 2, :, 0:n], ALU.mult).then_inc(s["prod_done"], 1)

        @block.gpsimd
        def _(pool):
            pool.sem_inc(s["mix_done"], 2)
            with pool.Fori(0, KC // 2) as i:
                for b in range(2):
                    for t, at, n in streams:
                        k = b * NS + t
                        pool.wait_ge(s["prod_done"], i * (2 * NS) + (k + 3))
                        nc.gpsimd.tensor_tensor(m.mix[:, bass.ds(i * 2 + b, 1), at:at + n].rearrange("p a n -> p (a n)"),
                                                s["t"][:, k % 2, 0, 0:n], s["t"][:, k % 2, 1, 0:n], ALU.add).then_inc(s["mix_done"], 1)


def out_stage(nc, m, l, w_out, streams):
    src = w_out[l].rearrange("(c p) n -> p c n", p=P)
    with stage(nc, f"out{l}", ["w0", "w1", "w_used", "mm_done", "evac"], [("w", [P, 2, KC, 4 * P])]) as (block, s):
        loaded = [s["w0"], s["w1"]]

        @block.sync
        def _(sp):
            for g in range(2):
                sp.dma_start(s["w"][:, g], src[:, :, g * 4 * P:(g + 1) * 4 * P]).then_inc(loaded[g], 16)

        @block.tensor
        def _(pe):
            for k in range(KC):
                if k % 4 == 0:
                    pe.wait_ge(loaded[k // 4], 16)
                if k >= 2:
                    pe.wait_ge(s["evac"], k - 1)
                for t, at, n in streams:
                    for c in range(KC):
                        last = nc.tensor.matmul(m.ps[:, 2 * (k % 2) + t, 0:n], s["w"][:, k // 4, c, (k % 4) * P:(k % 4 + 1) * P],
                                                m.mix[:, c, at:at + n], start=c == 0, stop=c == KC - 1)
                last.then_inc(s["mm_done"], 1)

        @block.vector
        def _(dve):
            for k in range(KC):
                dve.wait_ge(s["mm_done"], k + 1)
                for t, at, n in streams:
                    r = m.resid[:, k, at:at + n]
                    last = nc.vector.scalar_tensor_tensor(r, m.ps[:, 2 * (k % 2) + t, 0:n], m.mod[:, l, t, 2 * KC + k:2 * KC + k + 1],
                                                          r, ALU.mult, ALU.add)
                last.then_inc(s["evac"], 1)


class Memory:
    pass


def chip_memory(nc, ctx):
    def sb(name, shape, dtype=F32):
        return ctx.enter_context(nc.sbuf_tensor(name, shape, dtype))

    m = Memory()
    m.resid = sb("resid", [P, KC, TOK])
    m.ident = sb("ident", [P, P])
    m.ones = sb("ones", [P, P])
    m.cols = sb("cols", [P, DEPTH, R_ALL])
    m.gcols = sb("gcols", [P, RG_ALL])
    m.sil = sb("sil", [P, KC, 32])
    m.mod = sb("mod", [P, DEPTH, 2, N_MOD * KC])
    m.gain = sb("gain", [P, DEPTH, 2, 2, KC])
    m.weight = sb("weight", [P, 2, TT])
    m.table = sb("table", [P, NE + overflow_blocks(TOK)], I32)
    m.over = sb("over", [P, 1 + overflow_blocks(TOK)], I32)
    m.ps = ctx.enter_context(nc.psum_tensor("ps", [P, 8, 512], F32))
    return m


def mixers(nc, m, l, a, consts, dram):
    last = l == DEPTH - 1
    streams = spans(not last)

    def buffer(scope, name, shape):
        return scope.enter_context(nc.sbuf_tensor(f"{name}{l}", shape, F32))

    with ExitStack() as whole:
        m.u = buffer(whole, "u", [P, KC, TOK])
        norm_stage(nc, m, f"norm1_{l}", m.u, spans(True), lambda t, c: m.gain[:, l, t, 0, c:c + 1],
                   lambda t, c: m.mod[:, l, t, c:c + 1])
        m.yh = buffer(whole, "yh", [P, HC, TOK])
        with ExitStack() as part:
            m.v = buffer(part, "v", [P, TT, HW])
            m.x1 = buffer(part, "x1", [P, TT, HW])
            m.x2 = buffer(part, "x2", [P, HC, TOK])
            hyena_in_stage(nc, m, l, a["w_in"], streams)
            for t, _, _ in streams:
                conv_stage(nc, m, l, t, consts, dram)
        m.ya = buffer(whole, "ya", [P, HC, TOK])
        with ExitStack() as part:
            m.qn = buffer(part, "qn", [P, QC, TOK])
            m.kvn = buffer(part, "kvn", [P, KVC, TOK])
            m.key = buffer(part, "key", [P, 2, TOK])
            m.vt = buffer(part, "vt", [P, TT, HEADS * VD])
            m.rope = buffer(part, "rope", [P, SEQ])
            qkv_stage(nc, m, l, a["w_in"], a["w_ukv"], consts, streams)
            attention_stage(nc, m, l, a["w_uq"], a["w_ukv"], streams)
        m.mix = buffer(whole, "mix", [P, KC, TOK])
        merge_stage(nc, m, l, a["w_in"], a["w_hy_o"], a["w_mla_o"], streams)
        out_stage(nc, m, l, a["w_out"], streams)


def table_rows(a):
    def rows(v):
        return v.rearrange("(r p) -> r p", p=P)

    per_layer = [((R_G1, KC, rows(a["norm1_g"][l])), (R_G2, KC, rows(a["norm2_g"][l])), (R_ADA, N_MOD * KC, rows(a["b_ada"][l])),
                  (R_QG, QC, rows(a["q_norm_g"][l])), (R_KVG, KVC, rows(a["kv_norm_g"][l])),
                  (R_SCW, 9 * HC, a["sc_w"][l].rearrange("k (r p) -> (k r) p", p=P)), (R_SCB, 3 * HC, rows(a["sc_b"][l])))
                 for l in range(DEPTH)]
    return per_layer, ((RG_C, KC, rows(a["c"][0])), (RG_CC, KC, rows(a["c_ctx"])), (RG_F, KC, rows(a["final_g"])))


A_ALL = 2 * TOK
NO_ROW = A_ALL


def overflow_blocks(n_tok):
    return 2 * n_tok // SLOTS


def router_stage(nc, m, l, a, consts, streams, dram):
    n_tok = sum(n for _, _, n in streams)
    NT = n_tok // P
    NOV = overflow_blocks(n_tok)
    NB = NE + NOV
    QM = (n_tok - 1) // SLOTS
    R = NG + NE
    LOW = -3.0e38
    sems = ["consts_in", "wr_in", "bias_in", "tr_done", "lg_done", "tr_evac_a", "tr_evac_v", "lg_evac", "u_out0", "u_out1", "dve",
            "exps", "hot_done", "rank_done", "filled", "fill_out", "dest_done", "sc_out", "table_in"]
    bufs = [("wr", [P, KC, R]), ("bias", [P, R]), ("lg", [P, NT, R]), ("utok", [P, 2, D]), ("triu", [P, P]), ("iota", [P, 96]),
            ("gb", [P, NT, NG]), ("c", [P, NT, NG]), ("hot_g", [P, NT, NG]), ("e", [P, NT, NG]), ("leg", [P, NT, EG]),
            ("beg", [P, NT, EG]), ("val", [P, NT, EG]), ("hot1", [P, NT, EG]), ("hot2", [P, NT, EG]), ("big", [P, NT, NE]),
            ("sel", [P, 2, NT, NE]), ("both", [P, NT, NE]), ("rank", [P, NT, NE]), ("cnt", [P, NE]), ("ovf", [P, NE]),
            ("incl", [P, NE]), ("base", [P, NE]), ("one", [P, NE]), ("r", [P, 16, NT]), ("ex", [P, 2, NT]),
            ("q", [P, 2, NT]), ("pos", [P, 2, NT]), ("eid", [P, 2, NT]), ("ob", [P, 2, NT]), ("z", [P, 2, NT]), ("dest", [P, 2, NT]),
            ("dest_i", [P, 2, NT], I32), ("num", [P, 2, NT]), ("num_i", [P, 2, NT], I32), ("fill", [SLOTS, NB], I32),
            ("cmp", [P, NOV, NE]), ("oe", [P, NOV])]
    table = dram["table"][l]
    with stage(nc, f"route{l}", sems, bufs) as (block, s):
        u_out = [s["u_out0"], s["u_out1"]]

        @block.sync
        def _(sp):
            sp.dma_start(s["wr"][:, :, 0:NG], a["w_router_g"][l].rearrange("(c p) n -> p c n", p=P)).then_inc(s["wr_in"], 16)
            sp.dma_start(s["wr"][:, :, NG:R], a["w_router_e"][l].rearrange("(c p) n -> p c n", p=P)).then_inc(s["wr_in"], 16)
            sp.dma_start(s["bias"][:, 0:NG], a["b_router_g"][l].partition_broadcast(P)).then_inc(s["bias_in"], 16)
            sp.dma_start(s["bias"][:, NG:R], a["b_router_e"][l].partition_broadcast(P)).then_inc(s["bias_in"], 16)
            sp.dma_start(s["triu"][:], consts["triu"]).then_inc(s["consts_in"], 16)
            sp.dma_start(s["iota"][:], consts["iota"]).then_inc(s["consts_in"], 16)
            sp.wait_ge(s["filled"], 1)
            sp.dma_start(table.rearrange("(s b) o -> s (b o)", b=NB), s["fill"][:]).then_inc(s["fill_out"], 16)
            for j in range(NT):
                sp.wait_ge(s["tr_evac_a"], j + 1)
                sp.wait_ge(s["tr_evac_v"], j + 1)
                for k in range(2):
                    sp.dma_start(dram["u"][k * TOK + j * P:k * TOK + (j + 1) * P], s["utok"][:, j % 2]).then_inc(u_out[j % 2], 16)
            sp.wait_ge(s["sc_out"], 16 * 2 * NT)
            sp.dma_start(m.table[0:SLOTS, 0:NB], table.rearrange("(s b) o -> s (b o)", b=NB)).then_inc(s["table_in"], 16)
            for k in range(2):
                sp.wait_ge(u_out[k], 16 * NT)
            sp.wait_ge(s["table_in"], 16)

        @block.gpsimd
        def _(pool):
            nc.gpsimd.memset(s["fill"][:], NO_ROW).then_inc(s["filled"], 1)
            pool.wait_ge(s["fill_out"], 16)
            pool.wait_ge(s["dest_done"], 2)
            for k in range(2):
                for j in range(NT):
                    nc.gpsimd.indirect_dma_start(out=table, out_offset=bass.IndirectOffsetOnAxis(ap=s["dest_i"][:, k, j:j + 1], axis=0),
                                                 in_=s["num_i"][:, k, j:j + 1], in_offset=None,
                                                 bounds_check=SLOTS * NB - 1, oob_is_err=False).then_inc(s["sc_out"], 16)
            pool.wait_ge(s["sc_out"], 16 * 2 * NT)

        @block.tensor
        def _(pe):
            pe.wait_ge(s["wr_in"], 32)
            for j in range(NT):
                if j >= 2:
                    pe.wait_ge(s["tr_evac_a"], j - 1)
                    pe.wait_ge(s["tr_evac_v"], j - 1)
                b = 2 * (j % 2)
                for c in range(KC):
                    last = nc.tensor.transpose(m.ps[:, b + c // 4, (c % 4) * P:(c % 4 + 1) * P], m.u[:, c, j * P:(j + 1) * P], m.ident[:])
                last.then_inc(s["tr_done"], 1)
                if j >= 2:
                    pe.wait_ge(s["lg_evac"], j - 1)
                for c in range(KC):
                    last = nc.tensor.matmul(m.ps[:, 4 + j % 2, 0:R], m.u[:, c, j * P:(j + 1) * P], s["wr"][:, c], start=c == 0, stop=c == KC - 1)
                last.then_inc(s["lg_done"], 1)
            pe.wait_ge(s["consts_in"], 32)
            pe.wait_ge(s["hot_done"], 1)
            for j in range(NT):
                for i in range(j + 1):
                    nc.tensor.matmul(m.ps[:, 6, j * NE:(j + 1) * NE], m.ones[:] if i < j else s["triu"][:], s["both"][:, i],
                                     start=i == 0, stop=i == j)
            for i in range(NT):
                last = nc.tensor.matmul(m.ps[:, 7, 0:NE], m.ones[:], s["both"][:, i], start=i == 0, stop=i == NT - 1)
            last.then_inc(s["rank_done"], 1)

        @block.scalar
        def _(act):
            for j in range(NT):
                act.wait_ge(s["tr_done"], j + 1)
                if j >= 2:
                    act.wait_ge(u_out[j % 2], 32 * (j // 2))
                nc.scalar.activation(s["utok"][:, j % 2, 0:512], m.ps[:, 2 * (j % 2)], ACT.Copy).then_inc(s["tr_evac_a"], 1)
            act.wait_ge(s["exps"], 1)
            nc.scalar.activation(s["e"][:], s["e"][:], ACT.Exp).then_inc(s["exps"], 1)
            act.wait_ge(s["exps"], 3)
            nc.scalar.activation(s["ex"][:], s["ex"][:], ACT.Exp).then_inc(s["exps"], 1)

        @block.vector
        def _(dve):
            link = Chain(dve, s["dve"])
            for j in range(NT):
                dve.wait_ge(s["tr_done"], j + 1)
                if j >= 2:
                    dve.wait_ge(u_out[j % 2], 32 * (j // 2))
                nc.vector.tensor_copy(s["utok"][:, j % 2, 512:D], m.ps[:, 2 * (j % 2) + 1]).then_inc(s["tr_evac_v"], 1)
                dve.wait_ge(s["lg_done"], j + 1)
                nc.vector.tensor_copy(s["lg"][:, j], m.ps[:, 4 + j % 2, 0:R]).then_inc(s["lg_evac"], 1)
            dve.wait_ge(s["lg_evac"], NT)
            dve.wait_ge(s["bias_in"], 32)
            dve.wait_ge(s["consts_in"], 32)

            def over(ap, *shape):
                return ap.broadcast_to([P, *shape])

            def row(k):
                return s["r"][:, k]

            iota8 = over(s["iota"][:, None, 0:NG], NT, NG)

            def first_max(val, hot, k):
                link(nc.vector.tensor_reduce(row(k), val, axis=AX.X, op=ALU.max))
                link(nc.vector.tensor_tensor(s["c"][:], val, over(row(k)[:, :, None], NT, NG), ALU.is_equal))
                link(nc.vector.scalar_tensor_tensor(s["c"][:], s["c"][:], -64.0, iota8, ALU.mult, ALU.add))
                link(nc.vector.tensor_reduce(row(k), s["c"][:], axis=AX.X, op=ALU.min))
                link(nc.vector.tensor_tensor(hot, s["c"][:], over(row(k)[:, :, None], NT, NG), ALU.is_equal))

            def picked(out, val, hot):
                link(nc.vector.tensor_tensor(s["c"][:], val, hot, ALU.mult))
                link(nc.vector.tensor_reduce(out, s["c"][:], axis=AX.X, op=ALU.add))

            lg_g = s["lg"][:, :, 0:NG]
            link(nc.vector.tensor_tensor(s["gb"][:], lg_g, over(s["bias"][:, None, 0:NG], NT, NG), ALU.add))
            first_max(s["gb"][:], s["hot_g"][:], 0)
            link(nc.vector.tensor_reduce(row(1), lg_g, axis=AX.X, op=ALU.max))
            nc.vector.tensor_tensor(s["e"][:], lg_g, over(row(1)[:, :, None], NT, NG), ALU.subtract).then_inc(s["exps"], 1)
            dve.wait_ge(s["exps"], 2)
            link(nc.vector.tensor_reduce(row(2), s["e"][:], axis=AX.X, op=ALU.add))
            picked(row(3), s["e"][:], s["hot_g"][:])
            hot_over = over(s["hot_g"][:, :, :, None], NT, NG, EG)
            big4 = s["big"][:].rearrange("p t (g j) -> p t g j", g=NG)
            for src, dst in ((s["lg"][:, :, NG:R].rearrange("p t (g j) -> p t g j", g=NG), s["leg"]),
                             (over(s["bias"][:, NG:R].rearrange("p (t g j) -> p t g j", t=1, g=NG), NT, NG, EG), s["beg"])):
                link(nc.vector.tensor_tensor(big4, src, hot_over, ALU.mult))
                link(nc.vector.tensor_reduce(dst[:], s["big"][:].rearrange("p t (g j) -> p t j g", g=NG), axis=AX.X, op=ALU.add))
            link(nc.vector.tensor_tensor(s["val"][:], s["leg"][:], s["beg"][:], ALU.add))
            first_max(s["val"][:], s["hot1"][:], 4)
            link(nc.vector.scalar_tensor_tensor(s["val"][:], s["hot1"][:], LOW, s["val"][:], ALU.mult, ALU.add))
            first_max(s["val"][:], s["hot2"][:], 5)
            picked(s["ex"][:, 0], s["leg"][:], s["hot1"][:])
            picked(s["ex"][:, 1], s["leg"][:], s["hot2"][:])
            link(nc.vector.tensor_tensor(row(6), s["ex"][:, 0], s["ex"][:, 1], ALU.max))
            nc.vector.tensor_tensor(s["ex"][:], s["ex"][:], over(row(6)[:, None, :], 2, NT), ALU.subtract).then_inc(s["exps"], 1)
            for k, hot in enumerate((s["hot1"], s["hot2"])):
                last = nc.vector.tensor_tensor(s["sel"][:, k].rearrange("p t (g j) -> p t g j", g=NG), hot_over,
                                               over(hot[:, :, None, :], NT, NG, EG), ALU.mult)
            link(last)
            nc.vector.tensor_tensor(s["both"][:], s["sel"][:, 0], s["sel"][:, 1], ALU.add).then_inc(s["hot_done"], 1)
            dve.wait_ge(s["exps"], 4)
            link(nc.vector.tensor_tensor(row(7), s["ex"][:, 0], s["ex"][:, 1], ALU.add))
            link(nc.vector.tensor_tensor(row(7), row(7), row(2), ALU.mult))
            link(nc.vector.reciprocal(row(8), row(7)))
            link(nc.vector.tensor_tensor(row(8), row(8), row(3), ALU.mult))
            nc.vector.tensor_tensor(m.weight[:, :, 0:NT], s["ex"][:], over(row(8)[:, None, :], 2, NT), ALU.mult)
            dve.wait_ge(s["rank_done"], 1)
            nc.vector.tensor_copy(s["rank"][:], m.ps[:, 6, 0:NT * NE].rearrange("p (t e) -> p t e", e=NE))
            nc.vector.memset(s["one"][:], 1.0)
            link(nc.vector.tensor_copy(s["cnt"][:], m.ps[:, 7, 0:NE]))
            link(nc.vector.tensor_scalar(s["ovf"][:], s["cnt"][:], float(SLOTS), None, ALU.is_gt))
            for q in range(2, QM + 1):
                link(nc.vector.scalar_tensor_tensor(s["ovf"][:], s["cnt"][:], float(q * SLOTS), s["ovf"][:], ALU.is_gt, ALU.add))
            link(nc.vector.tensor_tensor_scan(s["incl"][:], s["one"][:], s["ovf"][:], 0.0, ALU.mult, ALU.add))
            link(nc.vector.tensor_tensor(s["base"][:], s["incl"][:], s["ovf"][:], ALU.subtract))
            for k in range(2):
                for vals, out in ((s["rank"][:], s["pos"]), (over(s["iota"][:, None, 0:NE], NT, NE), s["eid"]), (over(s["base"][:, None, :], NT, NE), s["ob"])):
                    link(nc.vector.tensor_tensor(s["big"][:], s["sel"][:, k], vals, ALU.mult))
                    link(nc.vector.tensor_reduce(out[:, k], s["big"][:], axis=AX.X, op=ALU.add))
            link(nc.vector.tensor_scalar(s["q"][:], s["pos"][:], float(SLOTS), None, ALU.is_ge))
            link(nc.vector.tensor_copy(s["z"][:], s["q"][:]))
            for q in range(2, QM + 1):
                link(nc.vector.scalar_tensor_tensor(s["q"][:], s["pos"][:], float(q * SLOTS), s["q"][:], ALU.is_ge, ALU.add))
            link(nc.vector.scalar_tensor_tensor(s["ob"][:], s["ob"][:], float(NE - 1), s["q"][:], ALU.add, ALU.add))
            link(nc.vector.tensor_tensor(s["ob"][:], s["ob"][:], s["eid"][:], ALU.subtract))
            link(nc.vector.tensor_tensor(s["ob"][:], s["ob"][:], s["z"][:], ALU.mult))
            link(nc.vector.tensor_tensor(s["ob"][:], s["ob"][:], s["eid"][:], ALU.add))
            link(nc.vector.scalar_tensor_tensor(s["pos"][:], s["q"][:], -float(SLOTS), s["pos"][:], ALU.mult, ALU.add))
            link(nc.vector.scalar_tensor_tensor(s["dest"][:], s["pos"][:], float(NB), s["ob"][:], ALU.mult, ALU.add))
            nc.vector.tensor_copy(s["dest_i"][:], s["dest"][:]).then_inc(s["dest_done"], 1)
            for k in range(2):
                for j in range(NT):
                    last = nc.vector.tensor_scalar_add(s["num"][:, k, j:j + 1], s["iota"][:, 88:89], float(k * TOK + j * P))
            link(last)
            nc.vector.tensor_copy(s["num_i"][:], s["num"][:]).then_inc(s["dest_done"], 1)
            link(nc.vector.tensor_tensor(s["cmp"][:], over(s["incl"][:, None, :], NOV, NE),
                                         over(s["iota"][:, 64:64 + NOV][:, :, None], NOV, NE), ALU.is_le))
            link(nc.vector.tensor_reduce(s["oe"][:], s["cmp"][:], axis=AX.X, op=ALU.add))
            link(nc.vector.tensor_scalar(s["oe"][:], s["oe"][:], float(NE - 1), None, ALU.min))
            nc.vector.tensor_copy(m.over[:, 1:1 + NOV], s["oe"][:])
            nc.vector.tensor_copy(m.over[:, 0:1], s["incl"][:, NE - 1:NE])


def gate_up(nc, ps, xt, wgu):
    for c in range(KC):
        for k in range(2):
            last = nc.tensor.matmul(ps[k * SLOTS:(k + 1) * SLOTS, 0:DE], xt[:, c], wgu[:, k, c], start=c == 0, stop=c == KC - 1)
    return last


def down_both(nc, ps, ht, wd):
    for c in range(2):
        for k in range(2):
            last = nc.tensor.matmul(ps[k * SLOTS:(k + 1) * SLOTS, 0:512], ht[:, c], wd[:, c, k * 512:(k + 1) * 512],
                                    start=c == 0, stop=c == 1)
    return last


def strided_transposes(nc, ps, src, n, ident):
    for c in range(n):
        last = nc.tensor.transpose(ps[:, c * SLOTS:(c + 1) * SLOTS], src.rearrange("p (q c) -> p c q", c=n)[:, c], ident[0:SLOTS, 0:SLOTS])
    return last


def load_expert(eng, a, l, e, wgu, wd, sem):
    for k, name in enumerate(("w_gate_e", "w_up_e")):
        eng.dma_start(wgu[:, k], a[name][l, bass.ds(e, 1)].rearrange("o (p c) n -> p (o c) n", p=P)).then_inc(sem, 16)
    eng.dma_start(wd, a["w_down_e"][l, bass.ds(e, 1)].rearrange("o (p c) n -> p (o c) n", p=P)).then_inc(sem, 16)


def moe_stage(nc, m, l, a, dram, ring):
    wgu, wd, loaded = ring
    sems = ["g0", "g1", "g2", "g3", "s0", "s1", "zeroed", "gu_done", "xt_done", "ht_done", "down_done",
            "silu_done", "x_evac", "ya", "h_done", "ht_evac", "yb", "turns"]
    bufs = [("xg", [SLOTS, 4, D]), ("xt", [P, 2, KC, SLOTS]), ("sg", [P, 2, DE]), ("h", [SLOTS, 2, DE]), ("ht", [P, 2, 2, SLOTS]),
            ("y", [SLOTS, 2, D])]
    with stage(nc, f"moe{l}", sems, bufs) as (block, s):
        gathered, scattered = [s["g0"], s["g1"], s["g2"], s["g3"]], [s["s0"], s["s1"]]
        xg, xt, sg, h, ht, y = s["xg"], s["xt"], s["sg"], s["h"], s["ht"], s["y"]

        def wait(eng, sem, n):
            if not isinstance(n, int) or n > 0:
                eng.wait_ge(sem, n)

        def rounds(eng, body):
            for b in range(RU):
                body(b, b, 0)
            with eng.Fori(1, NE // RU - 1) as i:
                for b in range(RU):
                    body(i * RU + b, b, i)
            for b in range(RU):
                body(NE - RU + b, b, NE // RU - 1)

        def inner(j):
            return not isinstance(j, int)

        @block.sync
        def _(sp):
            def load(j, b, r):
                if inner(j) or j >= RU:
                    wait(sp, s["down_done"], j - (RU - 1))
                    load_expert(sp, a, l, j, wgu[:, b], wd[:, b], loaded[b])

            rounds(sp, load)

        @block.gpsimd
        def _(pool):
            nc.gpsimd.memset(xg[:], 0.0).then_inc(s["zeroed"], 1)
            pool.wait_ge(s["zeroed"], 1)

            def gather(j):
                if j >= 4:
                    pool.wait_ge(s["xt_done"], j - 3)
                nc.gpsimd.indirect_dma_start(out=xg[:, j % 4], out_offset=None, in_=dram["u"],
                                             in_offset=bass.IndirectOffsetOnAxis(ap=m.table[0:SLOTS, j:j + 1], axis=0),
                                             bounds_check=A_ALL - 1, oob_is_err=False).then_inc(gathered[j % 4], 16)

            def scatter(j):
                pool.wait_ge(s["ya"], j + 1)
                pool.wait_ge(s["yb"], j + 1)
                nc.gpsimd.indirect_dma_start(out=dram["y"], out_offset=bass.IndirectOffsetOnAxis(ap=m.table[0:SLOTS, j:j + 1], axis=0),
                                             in_=y[:, j % 2], in_offset=None,
                                             bounds_check=A_ALL - 1, oob_is_err=False).then_inc(scattered[j % 2], 16)

            for j in range(NE + 3):
                if j < NE:
                    gather(j)
                if j >= 3:
                    scatter(j - 3)
            for b in range(2):
                pool.wait_ge(scattered[b], 16 * (NE // 2))

        @block.tensor
        def _(pe):
            def x_transposes(j, b, r):
                wait(pe, gathered[b], r * 16 + 16)
                wait(pe, s["x_evac"], j - 1)
                pe.sem_inc(s["turns"], 1)
                strided_transposes(nc, m.ps[:, 2 + b % 2], xg[:, b], KC, m.ident).then_inc(s["xt_done"], 1)

            def down(j, b):
                wait(pe, s["ht_evac"], j + 1)
                wait(pe, s["ya"], j - 1)
                wait(pe, s["yb"], j - 1)
                down_both(nc, m.ps[:, 5 + b % 2], ht[:, b % 2], wd[:, b]).then_inc(s["down_done"], 1)

            def body(j, b, r):
                wait(pe, loaded[b], r * 48 + 48)
                wait(pe, s["x_evac"], j + 1)
                wait(pe, s["h_done"], j - 1)
                gate_up(nc, m.ps[:, b % 2], xt[:, b % 2], wgu[:, b]).then_inc(s["gu_done"], 1)
                if inner(j) or j + 1 < NE:
                    x_transposes(j + 1, (b + 1) % RU, r + (b + 1) // RU)
                if inner(j) or j >= 1:
                    down(j - 1, (b - 1) % RU)
                wait(pe, s["h_done"], j + 1)
                wait(pe, s["ht_evac"], j)
                pe.sem_inc(s["turns"], 1)
                strided_transposes(nc, m.ps[:, 4], h[:, b % 2], 2, m.ident).then_inc(s["ht_done"], 1)

            x_transposes(0, 0, 0)
            rounds(pe, body)
            down(NE - 1, RU - 1)

        def copy_y(eng, sem, copy, half):
            def run(j, b):
                wait(eng, s["down_done"], j + 1)
                if inner(j):
                    eng.wait_ge(scattered[b % 2], (j - (b % 2)) * 8)
                else:
                    wait(eng, scattered[b % 2], 16 * (j // 2))
                copy(y[:, b % 2, half * 512:(half + 1) * 512], m.ps[half * SLOTS:(half + 1) * SLOTS, 5 + b % 2]).then_inc(sem, 1)
            return run

        @block.scalar
        def _(act):
            def copy(out, in_):
                return nc.scalar.activation(out, in_, ACT.Copy)

            y_half = copy_y(act, s["ya"], copy, 0)

            def x_copy(j, b):
                wait(act, s["xt_done"], j + 1)
                wait(act, s["gu_done"], j - 1)
                copy(xt[:, b % 2], m.ps[:, 2 + b % 2].rearrange("p (c q) -> p c q", c=KC)).then_inc(s["x_evac"], 1)

            def body(j, b, r):
                wait(act, s["gu_done"], j + 1)
                wait(act, s["h_done"], j - 1)
                nc.scalar.activation(sg[SLOTS:2 * SLOTS, b % 2], m.ps[0:SLOTS, b % 2, 0:DE], ACT.Silu).then_inc(s["silu_done"], 1)
                if inner(j) or j + 1 < NE:
                    x_copy(j + 1, b + 1)
                if inner(j) or j >= 1:
                    y_half(j - 1, (b - 1) % RU)

            x_copy(0, 0)
            rounds(act, body)
            y_half(NE - 1, RU - 1)

        @block.vector
        def _(dve):
            y_half = copy_y(dve, s["yb"], nc.vector.tensor_copy, 1)

            def body(j, b, r):
                wait(dve, s["silu_done"], j + 1)
                wait(dve, s["ht_done"], j - 1)
                nc.vector.tensor_tensor(h[:, b % 2], m.ps[SLOTS:2 * SLOTS, b % 2, 0:DE], sg[SLOTS:2 * SLOTS, b % 2],
                                        ALU.mult).then_inc(s["h_done"], 1)
                if inner(j) or j >= 1:
                    y_half(j - 1, (b - 1) % RU)
                wait(dve, s["ht_done"], j + 1)
                wait(dve, s["down_done"], j - 1)
                nc.vector.tensor_copy(ht[:, b % 2], m.ps[:, 4, 0:2 * SLOTS].rearrange("p (c q) -> p c q", c=2)).then_inc(s["ht_evac"], 1)

            rounds(dve, body)
            y_half(NE - 1, RU - 1)


def overflow_stage(nc, m, l, a, dram, n_tok):
    NOV = overflow_blocks(n_tok)
    sems = ["w_in", "idx_done", "g_in", "sc_out", "pe_done", "x_evac", "silu_done", "h_done", "ht_evac", "y_evac", "zeroed", "turns",
            "block_done"]
    bufs = [("wgu", [P, 2, KC, DE]), ("wd", [P, 2, D]), ("xg", [SLOTS, D]), ("xt", [P, KC, SLOTS]), ("sg", [P, DE]),
            ("h", [SLOTS, DE]), ("ht", [P, 2, SLOTS]), ("y", [SLOTS, D]), ("idx", [SLOTS, 1], I32)]
    with stage(nc, f"over{l}", sems, bufs) as (block, s):
        def blocks(eng, body):
            n = eng.value_load(m.over[0:1, 0:1], min_val=0, max_val=NOV)
            with eng.Fori(0, NOV) as i:
                with eng.If(i < n):
                    body(i)

        @block.sync
        def _(sp):
            sp.sem_inc(s["pe_done"], 4)

            def body(i):
                e = sp.value_load(m.over[0:1, bass.ds(i + 1, 1)], min_val=0, max_val=NE - 1)
                sp.wait_ge(s["pe_done"], i * 4 + 4)
                load_expert(sp, a, l, e, s["wgu"], s["wd"][:], s["w_in"])

            blocks(sp, body)

        @block.gpsimd
        def _(pool):
            nc.gpsimd.memset(s["xg"][:], 0.0).then_inc(s["zeroed"], 1)
            pool.wait_ge(s["zeroed"], 1)

            def body(i):
                at = bass.IndirectOffsetOnAxis(ap=s["idx"][:, 0:1], axis=0)
                pool.wait_ge(s["idx_done"], i + 1)
                pool.sem_inc(s["turns"], 1)
                nc.gpsimd.indirect_dma_start(out=s["xg"][:], out_offset=None, in_=dram["u"], in_offset=at,
                                             bounds_check=A_ALL - 1, oob_is_err=False).then_inc(s["g_in"], 16)
                pool.wait_ge(s["y_evac"], i + 1)
                pool.sem_inc(s["turns"], 1)
                nc.gpsimd.indirect_dma_start(out=dram["y"], out_offset=at, in_=s["y"][:], in_offset=None,
                                             bounds_check=A_ALL - 1, oob_is_err=False).then_inc(s["sc_out"], 16)
                pool.wait_ge(s["sc_out"], i * 16 + 16)
                pool.sem_inc(s["block_done"], 1)

            pool.sem_inc(s["block_done"], 1)
            blocks(pool, body)

        @block.tensor
        def _(pe):
            def body(i):
                pe.wait_ge(s["g_in"], i * 16 + 16)
                pe.sem_inc(s["turns"], 1)
                strided_transposes(nc, m.ps[:, 0], s["xg"][:], KC, m.ident).then_inc(s["pe_done"], 1)
                pe.wait_ge(s["w_in"], i * 48 + 48)
                pe.wait_ge(s["x_evac"], i + 1)
                gate_up(nc, m.ps[:, 1], s["xt"], s["wgu"]).then_inc(s["pe_done"], 1)
                pe.wait_ge(s["h_done"], i + 1)
                pe.sem_inc(s["turns"], 1)
                strided_transposes(nc, m.ps[:, 2], s["h"][:], 2, m.ident).then_inc(s["pe_done"], 1)
                pe.wait_ge(s["ht_evac"], i + 1)
                down_both(nc, m.ps[:, 3], s["ht"], s["wd"]).then_inc(s["pe_done"], 1)

            blocks(pe, body)

        @block.scalar
        def _(act):
            def body(i):
                act.wait_ge(s["pe_done"], i * 4 + 6)
                nc.scalar.activation(s["sg"][SLOTS:2 * SLOTS], m.ps[0:SLOTS, 1, 0:DE], ACT.Silu).then_inc(s["silu_done"], 1)

            blocks(act, body)

        @block.vector
        def _(dve):
            def body(i):
                dve.wait_ge(s["block_done"], i + 1)
                nc.vector.tensor_scalar(s["idx"][:], m.table[0:SLOTS, bass.ds(i + NE, 1)], 0.0, None, ALU.add).then_inc(s["idx_done"], 1)
                dve.wait_ge(s["pe_done"], i * 4 + 5)
                nc.vector.tensor_copy(s["xt"][:], m.ps[:, 0].rearrange("p (c q) -> p c q", c=KC)).then_inc(s["x_evac"], 1)
                dve.wait_ge(s["silu_done"], i + 1)
                nc.vector.tensor_tensor(s["h"][:], m.ps[SLOTS:2 * SLOTS, 1, 0:DE], s["sg"][SLOTS:2 * SLOTS], ALU.mult).then_inc(s["h_done"], 1)
                dve.wait_ge(s["pe_done"], i * 4 + 7)
                nc.vector.tensor_copy(s["ht"][:], m.ps[:, 2, 0:2 * SLOTS].rearrange("p (c q) -> p c q", c=2)).then_inc(s["ht_evac"], 1)
                dve.wait_ge(s["pe_done"], i * 4 + 8)
                nc.vector.tensor_copy(s["y"][:, 0:512], m.ps[0:SLOTS, 3])
                nc.vector.tensor_copy(s["y"][:, 512:D], m.ps[SLOTS:2 * SLOTS, 3]).then_inc(s["y_evac"], 1)

            blocks(dve, body)


def combine_stage(nc, m, l, dram, streams):
    work = [(t, at // P + j) for t, at, n in streams for j in range(n // P)]
    with stage(nc, f"comb{l}", ["y0", "y1", "y2", "y3", "half_done", "sum_done", "tr_done", "evac"],
               [("y", [P, 4, 2, D]), ("c", [P, 2, D])]) as (block, s):
        loaded = [s["y0"], s["y1"], s["y2"], s["y3"]]

        @block.sync
        def _(sp):
            for j, (t, tile) in enumerate(work):
                if j >= 4:
                    sp.wait_ge(s["sum_done"], j - 3)
                for k in range(2):
                    at = k * TOK + tile * P
                    sp.dma_start(s["y"][:, j % 4, k], dram["y"][at:at + P]).then_inc(loaded[j % 4], 16)

        @block.scalar
        def _(act):
            for j, (t, tile) in enumerate(work):
                act.wait_ge(loaded[j % 4], 32 * (j // 4 + 1))
                if j >= 2:
                    act.wait_ge(s["tr_done"], j - 1)
                nc.scalar.mul(s["c"][:, j % 2], s["y"][:, j % 4, 0], m.weight[:, 0, tile:tile + 1]).then_inc(s["half_done"], 1)

        @block.tensor
        def _(pe):
            for j, (t, tile) in enumerate(work):
                pe.wait_ge(s["sum_done"], j + 1)
                if j >= 2:
                    pe.wait_ge(s["evac"], j - 1)
                for c in range(KC):
                    last = nc.tensor.transpose(m.ps[:, 2 * (j % 2) + c // 4, (c % 4) * P:(c % 4 + 1) * P], s["c"][:, j % 2, c * P:(c + 1) * P], m.ident[:])
                last.then_inc(s["tr_done"], 1)

        @block.vector
        def _(dve):
            def add(j):
                t, tile = work[j]
                dve.wait_ge(s["tr_done"], j + 1)
                for c in range(KC):
                    r = m.resid[:, c, tile * P:(tile + 1) * P]
                    last = nc.vector.scalar_tensor_tensor(r, m.ps[:, 2 * (j % 2) + c // 4, (c % 4) * P:(c % 4 + 1) * P],
                                                          m.mod[:, l, t, 5 * KC + c:5 * KC + c + 1], r, ALU.mult, ALU.add)
                last.then_inc(s["evac"], 1)

            for j, (t, tile) in enumerate(work):
                dve.wait_ge(s["half_done"], j + 1)
                nc.vector.scalar_tensor_tensor(s["c"][:, j % 2], s["y"][:, j % 4, 1], m.weight[:, 1, tile:tile + 1], s["c"][:, j % 2],
                                               ALU.mult, ALU.add).then_inc(s["sum_done"], 1)
                if j >= 1:
                    add(j - 1)
            add(len(work) - 1)


def store_stage(nc, m, out):
    with stage(nc, "store", ["tr_done", "evac", "out0", "out1"], [("o", [P, 2, D])]) as (block, s):
        @block.tensor
        def _(pe):
            for j in range(XT):
                if j >= 2:
                    pe.wait_ge(s["evac"], j - 1)
                for c in range(KC):
                    last = nc.tensor.transpose(m.ps[:, 2 * (j % 2) + c // 4, (c % 4) * P:(c % 4 + 1) * P], m.u[:, c, j * P:(j + 1) * P], m.ident[:])
                last.then_inc(s["tr_done"], 1)

        @block.vector
        def _(dve):
            for j in range(XT):
                dve.wait_ge(s["tr_done"], j + 1)
                if j >= 2:
                    dve.wait_ge((s["out0"], s["out1"])[j % 2], 16 * (j // 2))
                nc.vector.tensor_copy(s["o"][:, j % 2], m.ps[:, 2 * (j % 2):2 * (j % 2) + 2].rearrange("p b k -> p (b k)")).then_inc(s["evac"], 1)

        @block.sync
        def _(sp):
            for j in range(XT):
                sp.wait_ge(s["evac"], j + 1)
                sp.dma_start(out[0, j * P:(j + 1) * P], s["o"][:, j % 2]).then_inc((s["out0"], s["out1"])[j % 2], 16)
            for k in range(2):
                sp.wait_ge((s["out0"], s["out1"])[k], 16 * (XT // 2))


def experts(nc, m, l, a, consts, dram):
    streams = spans(l < DEPTH - 1)
    n_tok = sum(n for _, _, n in streams)
    with ExitStack() as whole:
        wgu = whole.enter_context(nc.sbuf_tensor(f"wgu{l}", [P, RU, 2, KC, DE], F32))
        wd = whole.enter_context(nc.sbuf_tensor(f"wd{l}", [P, RU, 2, D], F32))
        ring = wgu, wd, [nc.alloc_semaphore(f"expert_in{l}_{b}") for b in range(RU)]

        def first_round(sp):
            for b in range(RU):
                load_expert(sp, a, l, b, wgu[:, b], wd[:, b], ring[2][b])

        with nc.sbuf_tensor(f"u2_{l}", [P, KC, TOK], F32) as u:
            m.u = u
            norm_stage(nc, m, f"norm2_{l}", m.u, streams, lambda t, c: m.gain[:, l, t, 1, c:c + 1],
                       lambda t, c: m.mod[:, l, t, 3 * KC + c:3 * KC + c + 1], first_round)
            router_stage(nc, m, l, a, consts, streams, dram)
        moe_stage(nc, m, l, a, dram, ring)
    overflow_stage(nc, m, l, a, dram, n_tok)
    combine_stage(nc, m, l, dram, streams)


def trunk(nc, a, consts, out):
    with ExitStack() as ctx:
        m = chip_memory(nc, ctx)
        dram = {"u": nc.dram_tensor("rows_in", [A_ALL, D], F32).ap(), "y": nc.dram_tensor("rows_out", [A_ALL, D], F32).ap(),
                "table": [nc.dram_tensor(f"slots{l}", [SLOTS * (NE + overflow_blocks(TOK if l < DEPTH - 1 else SEQ)), 1],
                                         I32).ap() for l in range(DEPTH)],
                "h": [[nc.dram_tensor(f"transfer{l}_{t}", [2, P, transfer_planes(t), HW], F32).ap() for t in range(2)]
                      for l in range(DEPTH)]}
        per_layer, shared = table_rows(a)
        load_stage(nc, m, a["x"], a["ctx"], per_layer, shared, consts)
        prepare_stage(nc, m, a, consts, dram)
        for l in range(DEPTH):
            mixers(nc, m, l, a, consts, dram)
            experts(nc, m, l, a, consts, dram)
        with nc.sbuf_tensor("u_out", [P, KC, TOK], F32) as u:
            m.u = u
            norm_stage(nc, m, "norm_out", m.u, spans(False), lambda t, c: m.gcols[:, RG_F + c:RG_F + c + 1], None)
            store_stage(nc, m, out)


NAMES = ["x", "c", "ctx", "c_ctx", "w_ada", "b_ada", "norm1_g", "w_in", "q_norm_g", "kv_norm_g", "w_uq", "w_ukv", "sc_w", "sc_b",
         "flt_w1", "flt_b1", "flt_freq", "flt_w2", "flt_b2", "flt_w3", "flt_bias", "w_hy_o", "w_mla_o", "w_out", "norm2_g",
         "w_router_g", "b_router_g", "w_router_e", "b_router_e", "w_gate_e", "w_up_e", "w_down_e", "final_g"]


def kernel(**inputs):
    import concourse.bacc as bacc
    from concourse.bass_utils import run_bass_kernel_spmd

    nc = bacc.Bacc("TRN2", target_bir_lowering=False, num_devices=1)
    arrays, a, consts = {}, {}, {}
    for name in NAMES:
        arrays[f"in_{name}"] = np.ascontiguousarray(inputs[name])
        a[name] = nc.dram_tensor(f"in_{name}", arrays[f"in_{name}"].shape, F32, kind="ExternalInput").ap()
    for name, value in layout_constants().items():
        arrays[f"const_{name}"] = value
        consts[name] = nc.dram_tensor(f"const_{name}", value.shape, F32, kind="ExternalInput").ap()
    out = nc.dram_tensor("out", (1, SEQ, D), F32, kind="ExternalOutput").ap()
    trunk(nc, a, consts, out)
    r = run_bass_kernel_spmd(nc, [arrays], core_ids=[0])
    return r.results[0]["out"]
```

```python
import math
from contextlib import ExitStack, contextmanager

import concourse.bass as bass
from concourse import mybir
import numpy as np

F32 = mybir.dt.float32
I32 = mybir.dt.int32
ACT = mybir.ActivationFunctionType
ALU = mybir.AluOpType
AX = mybir.AxisListType

P = 128
D = 1024
KC = D // P
SEQ, CTX = 512, 256
TOK = SEQ + CTX
XT, CT = SEQ // P, CTX // P
TT = TOK // P
DEPTH = 2
EPS = 1e-6
N_MOD = 6
GRID_W = 64

HW = 512
HC = HW // P
BANDS, EMB, FFN = 16, 33, 64
HY_COLS = 3 * HW
DECAY_FAST, DECAY_SLOW, DECAY_TARGET = 0.3, 1.5, 1e-2

HEADS, NOPE, ROPE, VD = 8, 64, 32, 64
QK = NOPE + ROPE
QL, KVL = 384, 256
QC, KVC = QL // P, KVL // P
PAIRS = ROPE // 4
SCALE = QK ** -0.5
Q0 = HY_COLS
KR0 = Q0 + QL + KVL
G0 = KR0 + ROPE
IN_COLS = G0 + 2 * D

NG, EG = 8, 8
NE = NG * EG
DE = 256
SLOTS = 64
RU = 4

R_G1, R_G2, R_ADA, R_QG, R_KVG, R_SCW, R_SCB = 0, 8, 16, 64, 67, 69, 105
R_ALL = 117
RG_C, RG_CC, RG_F, RG_ALL = 0, 8, 16, 24


def layout_constants():
    out = {"ident": np.eye(P, dtype=np.float32), "ones": np.ones((P, P), np.float32)}
    f = np.float32
    deltas = np.abs(np.linspace(math.log(DECAY_TARGET) / DECAY_FAST, math.log(DECAY_TARGET) / DECAY_SLOW,
                                HW).astype(f))
    for name, n in (("x", SEQ), ("c", CTX)):
        half = np.arange(n // 2)
        mats = [fun(np.pi / (2 * n) * ((2 * half[:, None] + parity) * (2 * half[None, :] + 1) % (4 * n)))
                for fun, parity in ((np.cos, 0), (np.sin, 1), (np.cos, 1), (np.sin, 0))]
        out[f"dft_{name}"] = np.stack(mats).astype(f)
        out[f"idft_{name}"] = np.stack([mat.T / n for mat in mats]).astype(f)
        order = np.concatenate([np.arange(0, n, 2), np.arange(1, n, 2)])
        t = np.linspace(0.0, 1.0, n).astype(f)[:, None]
        w = (f(2.0 * math.pi) * np.arange(n, dtype=f)[:, None] / f(n)).astype(f)
        bands = np.linspace(1e-4, BANDS - 1, BANDS).astype(f)[None, :]
        bw = (bands * w).astype(f)
        out[f"feat_{name}"] = np.ascontiguousarray(np.concatenate([t, np.cos(bw), -np.sin(bw)], axis=1)[order].T.astype(f))
        out[f"decay_{name}"] = np.exp(-t * deltas[None, :])[order].astype(f)
    rows = SEQ // GRID_W
    r, col = np.meshgrid(np.arange(rows), np.arange(GRID_W), indexing="ij")
    pos = np.stack([r.reshape(-1), col.reshape(-1)], axis=-1).astype(f)
    inv = (f(10000.0) ** (-np.arange(PAIRS, dtype=f) / f(PAIRS))).astype(f)
    ang = pos[:, :, None] * inv
    cs, sn = np.cos(ang).astype(f), np.sin(ang).astype(f)
    rope = np.zeros((P, SEQ), f)
    for a in range(2):
        for h in range(2):
            at = a * 2 * PAIRS + h * PAIRS
            rope[NOPE + at:NOPE + at + PAIRS] = cs[:, a].T
            rope[QK + at:QK + at + PAIRS] = (sn if h else -sn)[:, a].T
    out["rope"] = rope
    out["triu"] = np.triu(np.ones((P, P), f), 1)
    iota = np.zeros((P, 96), f)
    iota[:, 0:64] = np.arange(64)
    iota[:, 64:88] = np.arange(24)
    iota[:, 88] = np.arange(P)
    out["iota"] = iota
    return out


@contextmanager
def stage(nc, name, signals, buffers=()):
    with ExitStack() as ctx:
        mine = {n: ctx.enter_context(nc.sbuf_tensor(f"{name}_{n}", shape, dt[0] if dt else F32))
                for n, shape, *dt in buffers}
        sems = {n: nc.alloc_semaphore(f"{name}_{n}") for n in signals}
        with nc.Block() as block:
            yield block, {**mine, **sems}
        nc.clear_and_free_semaphores(list(sems.values()))
        nc.all_engine_barrier()


class Chain:

    def __init__(self, eng, sem, start=0):
        self.eng, self.sem, self.n = eng, sem, start

    def __call__(self, ins):
        self.n = self.n + 1
        ins.then_inc(self.sem, 1)
        self.eng.wait_ge(self.sem, self.n)


def refined_rsqrt(nc, link, root, var, tmp):
    link(nc.vector.reciprocal(root, root))
    link(nc.vector.tensor_tensor(tmp, root, root, ALU.mult))
    link(nc.vector.scalar_tensor_tensor(tmp, tmp, -0.5, var, ALU.mult, ALU.mult))
    link(nc.vector.scalar_tensor_tensor(root, tmp, 1.5, root, ALU.add, ALU.mult))


def spans(with_ctx):
    return ((0, 0, SEQ), (1, SEQ, CTX)) if with_ctx else ((0, 0, SEQ),)


def load_stage(nc, m, x, ctx, rows_l, rows_g, consts, then):
    with stage(nc, "load", ["tokens_in", "rows_in", "consts_in", "pe_done", "evac", "silu_done", "sil_zeroed"],
               [("tok", [P, TT, D]), ("rows", [P, DEPTH + 1, P])]) as (block, s):
        @block.sync
        def _(sp):
            sp.dma_start(m.ident[:], consts["ident"]).then_inc(s["consts_in"], 16)
            sp.dma_start(m.ones[:], consts["ones"]).then_inc(s["consts_in"], 16)
            for l in range(DEPTH):
                for at, n, src in rows_l[l]:
                    sp.dma_start(s["rows"][at:at + n, l], src).then_inc(s["rows_in"], 16)
            for at, n, src in rows_g:
                sp.dma_start(s["rows"][at:at + n, DEPTH], src).then_inc(s["rows_in"], 16)
            for t in range(TT):
                src = x[0, t * P:(t + 1) * P] if t < XT else ctx[0, (t - XT) * P:(t - XT + 1) * P]
                sp.dma_start(s["tok"][:, t], src).then_inc(s["tokens_in"], 16)
            then(sp)

        @block.tensor
        def _(pe):
            pe.wait_ge(s["consts_in"], 32)
            pe.wait_ge(s["rows_in"], 16 * (sum(len(r) for r in rows_l) + len(rows_g)))
            for l in range(DEPTH + 1):
                n = R_ALL if l < DEPTH else RG_ALL
                last = nc.tensor.transpose(m.ps[:, 7, l * P:l * P + n], s["rows"][0:n, l], m.ident[0:n, 0:n])
            last.then_inc(s["pe_done"], 1)
            pe.wait_ge(s["tokens_in"], 16 * TT)
            for t in range(TT):
                for half in range(2):
                    n = 2 * t + half
                    if n >= 4:
                        pe.wait_ge(s["evac"], n - 3)
                    for c in range(4):
                        k = half * 4 + c
                        last = nc.tensor.transpose(m.ps[:, n % 4, c * P:(c + 1) * P], s["tok"][:, t, k * P:(k + 1) * P],
                                                   m.ident[:])
                    last.then_inc(s["pe_done"], 1)

        @block.vector
        def _(dve):
            nc.vector.memset(m.sil[:], 0.0).then_inc(s["sil_zeroed"], 1)
            for n in range(2 * TT):
                t, half = n // 2, n % 2
                dve.wait_ge(s["pe_done"], n + 2)
                nc.vector.tensor_copy(m.resid[:, half * 4:half * 4 + 4, t * P:(t + 1) * P],
                                      m.ps[:, n % 4].rearrange("p (c t) -> p c t", c=4)).then_inc(s["evac"], 1)

        @block.scalar
        def _(act):
            act.wait_ge(s["pe_done"], 1)
            for l in range(DEPTH):
                nc.scalar.activation(m.cols[:, l, 0:R_ALL], m.ps[:, 7, l * P:l * P + R_ALL], ACT.Copy)
            nc.scalar.activation(m.gcols[:, 0:RG_ALL], m.ps[:, 7, DEPTH * P:DEPTH * P + RG_ALL],
                                 ACT.Copy).then_inc(s["silu_done"], 1)
            act.wait_ge(s["sil_zeroed"], 1)
            nc.scalar.activation(m.sil[:, :, 0:2], m.ps[:, 7, DEPTH * P:DEPTH * P + 2 * KC].rearrange("p (s c) -> p c s", s=2),
                                 ACT.Silu)


TWO_PI = 2.0 * math.pi
TWO_PI_HI = 6.28125
ROUND = 1.5 * 2.0 ** 23
PI_BELOW = 3.1415925


PARITY = (0, 1, 1, 0)


ADA_RING, ADA_COLS = 4, 512
SMALL_LOADS = DEPTH * 7 + 2


def of_layer(l):
    return slice(l * FFN, (l + 1) * FFN)


def prepare_buffers(nc, scope):
    shapes = {"w": [P, ADA_RING, KC, ADA_COLS], "feat0": [EMB, SEQ], "feat1": [EMB, CTX], "w1": [EMB, DEPTH, FFN], "w2": [P, FFN],
              "w3": [P, 4 * HW], "vec": [P, 3], "bias": [1, DEPTH, 2, HW]}
    early = {name: scope.enter_context(nc.sbuf_tensor(f"prep_{name}", shape, F32)) for name, shape in shapes.items()}
    for name in ("small_in", *(f"ada{k}_in" for k in range(ADA_RING))):
        early[name] = nc.alloc_semaphore(f"prep_{name}")
    return early


def ada_load(sp, a, early, g):
    l, blk = divmod(g, N_MOD * D // ADA_COLS)
    src = a["w_ada"].rearrange("l (c p) n -> l p c n", p=P)[l, :, :, blk * ADA_COLS:(blk + 1) * ADA_COLS]
    sp.dma_start(early["w"][:, g % ADA_RING], src).then_inc(early[f"ada{g % ADA_RING}_in"], 16)


def prepare_loads(sp, a, consts, early):
    for t, tag in ((0, "x"), (1, "c")):
        sp.dma_start(early[f"feat{t}"][:], consts[f"feat_{tag}"]).then_inc(early["small_in"], 16)
    for l in range(DEPTH):
        at = of_layer(l)
        for dst, src in ((early["w1"][:, l], a["flt_w1"][l]), (early["w2"][at], a["flt_w2"][l]), (early["w3"][at], a["flt_w3"][l]),
                         (early["vec"][at, 0:1], a["flt_b1"][l][:, None]), (early["vec"][at, 1:2], a["flt_freq"][l][:, None]),
                         (early["vec"][at, 2:3], a["flt_b2"][l][:, None]), (early["bias"][0:1, l], a["flt_bias"][l][None])):
            sp.dma_start(dst, src).then_inc(early["small_in"], 16)
    for g in range(ADA_RING):
        ada_load(sp, a, early, g)


def prepare_stage(nc, m, a, consts, dram, early):
    RING, COLS = ADA_RING, ADA_COLS
    per = COLS // P
    BLOCKS = N_MOD * D // COLS
    sets = [(l, t) for l in range(DEPTH) for t, _, _ in spans(l < DEPTH - 1)]
    items = [(i, l, t, o) for i, (l, t) in enumerate(sets) for o in range(2)]
    NI = len(items)
    rest = DEPTH * BLOCKS - RING
    starts = [0, RING // 2] + [RING + rest * i // (NI + 1) for i in range(NI + 2)]
    slots = [range(first, past) for first, past in zip(starts, starts[1:])]
    tiles = [(SEQ, CTX)[t] // P for _, _, t, _ in items]
    before = [sum(tiles[:k]) for k in range(NI + 1)]
    units = [(k, j) for k in range(NI) for j in range(tiles[k] // 2)]
    sems = ["sel_done", "mats_in", "mlp_done", "sines", "dve", "h3_done", "f_done", "sq_done", "sum_done",
            "var_done", "root_done", "inverse_done", "scaled", "edge", "sum_taps", "difference", "cos_done", "sin_done", "cos_folded", "sin_folded", "other_done", "h0_out", "h1_out",
            "rows_done", "rows_evac", "cols_done", "mod_done"]
    bufs = [("dft0", [P, 4, XT // 2, SEQ // 2]), ("dft1", [P, 4, CT // 2, CTX // 2]),
            ("decay0", [P, XT, HW]), ("decay1", [P, CT, HW]), 
            ("h", [P, TOK]), ("rows", [P, 2, COLS]), ("sel", [P, 2]),
            ("f", [P, 2, 2, XT, HW]), ("sq", [P, 2, HW]), ("var", [P, 2, HW]), ("rn", [P, 2, HW]), ("out", [P, 2, 2, 2, HW]), ("other", [P, 2, HW])]
    with stage(nc, "prep", sems, bufs) as (block, s):
        s = {**s, **early}
        loaded, h_out = [s[f"ada{k}_in"] for k in range(RING)], [s["h0_out"], s["h1_out"]]
        f, sq, var, rn, out = s["f"], s["sq"], s["var"], s["rn"], s["out"]
        angle, turn = (b[:].rearrange("p e n -> p (e n)")[:, 0:TOK] for b in (var, sq))

        def ada_wait(eng, g):
            if g >= 0:
                eng.wait_ge(s["mod_done"], g + 1)

        @block.sync
        def _(sp):
            for t, tag in ((0, "x"), (1, "c")):
                sp.dma_start(s[f"decay{t}"][:], consts[f"decay_{tag}"].rearrange("(j p) k -> p j k", p=P)).then_inc(s["mats_in"], 16)
                sp.dma_start(s[f"dft{t}"][:], consts[f"dft_{tag}"].rearrange("e (j p) k -> p e j k", p=P)).then_inc(s["mats_in"], 16)
            for g in range(RING, DEPTH * BLOCKS):
                sp.wait_ge(s["rows_done"], g - RING + 1)
                ada_load(sp, a, early, g)

        @block.tensor
        def _(pe):
            def ada(g):
                pe.wait_ge(loaded[g % RING], 16 * (g // RING + 1))
                ada_wait(pe, g - 2)
                for c in range(KC // 4):
                    for q in range(4):
                        k = q * KC // 4 + c
                        last = nc.tensor.matmul(m.ps[32 * q:32 * q + 32, g % 2], m.sil[:, k], s["w"][:, g % RING, k],
                                                start=c == 0, stop=c == KC // 4 - 1)
                last.then_inc(s["rows_done"], 1)

            def ada_columns(g):
                pe.wait_ge(s["rows_evac"], g + 1)
                if g == 0:
                    pe.wait_ge(s["sel_done"], 1)
                for j in range(per):
                    last = nc.tensor.matmul(m.ps[:, g % 2, 2 * j:2 * j + 2], s["rows"][:, g % 2, j * P:(j + 1) * P], s["sel"][:],
                                            start=True, stop=True)
                last.then_inc(s["cols_done"], 1)

            def adas(slot):
                for g in slots[slot]:
                    ada(g)
                    if g > slots[slot][0]:
                        ada_columns(g - 1)
                ada_columns(slots[slot][-1])

            def taps(k):
                i, l, t, o = items[k]
                J = tiles[k]
                ada_wait(pe, slots[k + 2][0] - 1)
                for q in range(2 * J + 1):
                    if q < 2 * J:
                        e, j = divmod(q, J)
                        if q >= 2:
                            pe.wait_ge(s["f_done"], 2 * before[k] + q - 1)
                        nc.tensor.matmul(m.ps[:, q % 2], s["h"][of_layer(l), t * SEQ + j * P:t * SEQ + (j + 1) * P],
                                         s["w3"][of_layer(l), (2 * o + e) * HW:(2 * o + e + 1) * HW],
                                         start=True, stop=True).then_inc(s["h3_done"], 1)
                    if q >= 1:
                        e, j = divmod(q - 1, J)
                        pe.wait_ge(s["sq_done"], 2 * before[k] + q)
                        if q == 1 and k:
                            pe.wait_ge(s["var_done"], k)
                        nc.tensor.matmul(m.ps[:, 2 + e], m.ones[:], sq[:, (q - 1) % 2], start=j == 0,
                                         stop=j == J - 1).then_inc(s["sum_done"], 1)

            def transform(k):
                i, l, t, o = items[k]
                J, dft = tiles[k] // 2, s[f"dft{t}"]
                pe.wait_ge(s["sum_taps"], k + 1)
                pe.wait_ge(s["difference"], k + 1)
                for j in range(J):
                    unit = units.index((k, j))
                    for is_sin, done, folded in ((0, "cos_done", "cos_folded"), (1, "sin_done", "sin_folded")):
                        if unit >= 1:
                            pe.wait_ge(s[folded], unit)
                        for e in ((1, 3) if is_sin else (0, 2)):
                            for x in range(J):
                                last = nc.tensor.matmul(m.ps[:, 4 + e], dft[:, e, x, j * P:(j + 1) * P],
                                                        f[:, k % 2, is_sin, PARITY[e] * J + x], start=x == 0, stop=x == J - 1)
                        last.then_inc(s[done], 1)

            pe.wait_ge(s["small_in"], 16 * SMALL_LOADS)
            for k in range(2):
                if k:
                    pe.wait_ge(s["sines"], 1)
                for l in range(DEPTH):
                    for t, at, n in spans(True):
                        last = nc.tensor.matmul(m.ps[of_layer(l), 4 + 2 * k + t, 0:n], s["w2"][of_layer(l)] if k else s["w1"][:, l],
                                                s["h"][of_layer(l), at:at + n] if k else s[f"feat{t}"][:], start=True, stop=True)
                last.then_inc(s["mlp_done"], 1)
                adas(k)
            pe.wait_ge(s["sines"], 2)
            taps(0)
            adas(2)
            for k in range(NI):
                if k + 1 < NI:
                    taps(k + 1)
                if k < NI - 1:
                    transform(k)
                adas(k + 3)
            transform(NI - 1)

        @block.scalar
        def _(act):
            def squares(k):
                J = tiles[k]
                for q in range(2 * J):
                    e, j = divmod(q, J)
                    act.wait_ge(s["f_done"], 2 * before[k] + q + 1)
                    if 2 * before[k] + q >= 2:
                        act.wait_ge(s["sum_done"], 2 * before[k] + q - 1)
                    nc.scalar.activation(sq[:, q % 2], f[:, k % 2, e, j], ACT.Square).then_inc(s["sq_done"], 1)

            def root(k):
                act.wait_ge(s["var_done"], k + 1)
                if k:
                    act.wait_ge(s["scaled"], k)
                nc.scalar.activation(rn[:], var[:], ACT.Sqrt).then_inc(s["root_done"], 1)

            def store(k):
                i, l, t, o = items[k]
                for unit, (item, j) in enumerate(units):
                    if item == k:
                        for part, done, folded in ((0, "cos_done", "cos_folded"), (1, "sin_done", "sin_folded")):
                            act.wait_ge(s[done], unit + 1)
                            if unit >= 1:
                                act.wait_ge(s[folded], unit)
                            nc.scalar.activation(s["other"][:, part], m.ps[:, 6 + part], ACT.Copy).then_inc(s["other_done"], 1)
                        act.wait_ge(s["cos_folded"], unit + 1)
                        act.wait_ge(s["sin_folded"], unit + 1)
                        act.dma_start(dram["h"][l][t][o, :, :, j], out[:, unit % 2]).then_inc(h_out[unit % 2], 16)

            def evacuate(g):
                act.wait_ge(s["rows_done"], g + 1)
                if g >= 2:
                    act.wait_ge(s["cols_done"], g - 1)
                nc.scalar.activation(s["rows"][:, g % 2], m.ps[:, g % 2], ACT.Copy).then_inc(s["rows_evac"], 1)

            def columns(g):
                l, blk = divmod(g, BLOCKS)
                act.wait_ge(s["cols_done"], g + 1)
                nc.scalar.activation(m.mod[:, l, :, blk * per:(blk + 1) * per], m.ps[:, g % 2, 0:2 * per].rearrange("p (j s) -> p s j", s=2),
                                     ACT.Copy).then_inc(s["mod_done"], 1)

            def evacuate_slot(i):
                for g in slots[i]:
                    evacuate(g)
                    if g > slots[i][0]:
                        columns(g - 1)
                columns(slots[i][-1])

            for k in range(2):
                evacuate_slot(k)
                act.wait_ge(s["dve"], 6 * (k + 1))
                if k:
                    act.wait_ge(s["mlp_done"], 2)
                nc.scalar.activation(s["h"][:], angle, ACT.Sin).then_inc(s["sines"], 1)
            squares(0)
            root(0)
            evacuate_slot(2)
            for k in range(NI):
                if k + 1 < NI:
                    squares(k + 1)
                if k + 1 < NI:
                    store(k)
                    root(k + 1)
                evacuate_slot(k + 3)
            store(NI - 1)
            for r in range(2):
                act.wait_ge(h_out[r], 16 * (len(units) // 2))

        @block.gpsimd
        def _(pool):
            for k, (i, l, t, o) in enumerate(items):
                g, J = f[:, k % 2], tiles[k]
                pool.wait_ge(s["inverse_done"], k + 1)
                for e in range(2):
                    last = nc.gpsimd.tensor_tensor(g[:, e, 0:J], g[:, e, 0:J], rn[:, e:e + 1].broadcast_to([P, J, HW]), ALU.mult)
                last.then_inc(s["scaled"], 1)
                pool.wait_ge(s["scaled"], k + 1)
                nc.gpsimd.memset(g[0:1, 1, 0], 0.0)
                nc.gpsimd.tensor_tensor(g[0:1, 0, 0], g[0:1, 0, 0], s["bias"][0:1, l, o], ALU.add).then_inc(s["edge"], 1)
                pool.wait_ge(s["edge"], k + 1)
                nc.gpsimd.tensor_tensor(g[:, 0, 0:J], g[:, 0, 0:J], g[:, 1, 0:J], ALU.add).then_inc(s["sum_taps"], 1)

        @block.vector
        def _(dve):
            link = Chain(dve, s["dve"])

            def decayed(k):
                i, l, t, o = items[k]
                J = tiles[k]
                if k >= 2:
                    n = sum(item <= k - 2 for item, _ in units)
                    dve.wait_ge(s["cos_done"], n)
                    dve.wait_ge(s["sin_done"], n)
                for q in range(2 * J):
                    e, j = divmod(q, J)
                    dve.wait_ge(s["h3_done"], 2 * before[k] + q + 1)
                    nc.vector.tensor_tensor(f[:, k % 2, e, j], m.ps[:, q % 2], s[f"decay{t}"][:, j], ALU.mult).then_inc(s["f_done"], 1)

            def inverse_norm(k):
                dve.wait_ge(s["sum_done"], 2 * before[k + 1])
                nc.vector.tensor_scalar_add(var[:], m.ps[:, 2:4], EPS).then_inc(s["var_done"], 1)
                dve.wait_ge(s["root_done"], k + 1)
                refined_rsqrt(nc, link, rn[:], var[:], sq[:])
                dve.sem_inc(s["inverse_done"], 1)

            def difference(k):
                g, J = f[:, k % 2], tiles[k]
                dve.wait_ge(s["sum_taps"], k + 1)
                nc.vector.scalar_tensor_tensor(g[:, 1, 0:J], g[:, 1, 0:J], -2.0, g[:, 0, 0:J], ALU.mult, ALU.add).then_inc(s["difference"], 1)

            def fold(k):
                for unit, (item, j) in enumerate(units):
                    if item != k:
                        continue
                    if unit >= 2:
                        dve.wait_ge(h_out[unit % 2], 16 * (unit // 2))
                    for part, done, folded in ((0, "cos_done", "cos_folded"), (1, "sin_done", "sin_folded")):
                        dve.wait_ge(s[done], unit + 1)
                        dve.wait_ge(s["other_done"], 2 * unit + part + 1)
                        nc.vector.tensor_tensor(out[:, unit % 2, 0, part], m.ps[:, 4 + part], s["other"][:, part], ALU.add)
                        nc.vector.tensor_tensor(out[:, unit % 2, 1, part], m.ps[:, 4 + part], s["other"][:, part],
                                                ALU.subtract).then_inc(s[folded], 1)

            nc.vector.tensor_reduce(s["sel"][:], m.ident.rearrange("p (q r) -> p r q", q=4)[:, 0:2], AX.X,
                                    ALU.add).then_inc(s["sel_done"], 1)
            dve.wait_ge(s["small_in"], 16 * SMALL_LOADS)
            x, kk = angle, turn
            for k in range(2):
                dve.wait_ge(s["mlp_done"], k + 1)
                link(nc.vector.tensor_scalar(x, m.ps[:, 4 + 2 * k:6 + 2 * k].rearrange("p b n -> p (b n)")[:, 0:TOK],
                                             s["vec"][:, 2 * k:2 * k + 1], s["vec"][:, 1:2], ALU.add, ALU.mult))
                link(nc.vector.tensor_scalar(kk, x, 1.0 / TWO_PI, ROUND, ALU.mult, ALU.add))
                link(nc.vector.tensor_scalar_sub(kk, kk, ROUND))
                link(nc.vector.scalar_tensor_tensor(x, kk, -TWO_PI_HI, x, ALU.mult, ALU.add))
                link(nc.vector.scalar_tensor_tensor(x, kk, -(TWO_PI - TWO_PI_HI), x, ALU.mult, ALU.add))
                link(nc.vector.tensor_scalar(x, x, PI_BELOW, -PI_BELOW, ALU.min, ALU.max))
                dve.wait_ge(s["sines"], k + 1)
            dve.wait_ge(s["mats_in"], 16 * 4)
            decayed(0)
            for k in range(NI + 1):
                if k >= 1:
                    if k < NI:
                        decayed(k)
                    difference(k - 1)
                    fold(k - 1)
                if k < NI:
                    inverse_norm(k)
            dve.wait_ge(s["mod_done"], DEPTH * BLOCKS)
            for l in range(DEPTH):
                for t in range(2):
                    last = nc.vector.tensor_tensor(m.mod[:, l, t], m.mod[:, l, t], m.cols[:, l, R_ADA:R_ADA + N_MOD * KC], ALU.add)
            link(last)
            for l in range(DEPTH):
                for t in range(2):
                    for k, (part, row) in enumerate(((1, R_G1), (4, R_G2))):
                        nc.vector.scalar_tensor_tensor(m.gain[:, l, t, k], m.mod[:, l, t, part * KC:(part + 1) * KC],
                                                       1.0, m.cols[:, l, row:row + KC], ALU.add, ALU.mult)


def norm_stage(nc, m, name, out, streams, gains, shifts, prefetch=None):
    n_tok = sum(n for _, _, n in streams)
    NT = n_tok // P
    with stage(nc, name, ["sq_done", "sum_done", "chain", "root_done", "diag_done", "rows_done", "scaled"],
               [("sq", [P, 2, TOK]), ("rstd", [P, NT]), ("var", [P, NT]), ("tmp", [P, NT]), ("diag", [P, NT, P])]) as (block, s):
        if prefetch:
            block.sync(prefetch)
        r, var = s["rstd"][:], s["var"][:]

        @block.scalar
        def _(act):
            for c in range(KC):
                if c >= 2:
                    act.wait_ge(s["sum_done"], c - 1)
                nc.scalar.activation(s["sq"][:, c % 2, 0:n_tok], m.resid[:, c, 0:n_tok], ACT.Square).then_inc(s["sq_done"], 1)
            act.wait_ge(s["chain"], 1)
            nc.scalar.activation(r, var, ACT.Sqrt).then_inc(s["root_done"], 1)
            for c in range(0, KC, 2):
                act.wait_ge(s["scaled"], c + 1)
                for t, at, n in streams:
                    o = out[:, c, at:at + n]
                    if shifts is None:
                        nc.scalar.activation(o, o, ACT.Identity, scale=gains(t, c))
                    else:
                        nc.scalar.activation(o, o, ACT.Identity, scale=gains(t, c), bias=shifts(t, c))

        @block.gpsimd
        def _(pool):
            for c in range(1, KC, 2):
                pool.wait_ge(s["scaled"], c + 1)
                for t, at, n in streams:
                    o = out[:, c, at:at + n]
                    if shifts is None:
                        nc.gpsimd.tensor_scalar(o, o, gains(t, c), None, ALU.mult)
                    else:
                        nc.gpsimd.tensor_scalar(o, o, gains(t, c), shifts(t, c), ALU.mult, ALU.add)

        @block.tensor
        def _(pe):
            for c in range(KC):
                pe.wait_ge(s["sq_done"], c + 1)
                for j in range(NT):
                    last = nc.tensor.matmul(m.ps[:, j, 0:1], s["sq"][:, c % 2, j * P:(j + 1) * P], m.ones[:, 0:1],
                                            start=c == 0, stop=c == KC - 1)
                last.then_inc(s["sum_done"], 1)
            for j in range(NT):
                pe.wait_ge(s["diag_done"], j + 1)
                last = nc.tensor.matmul(m.ps[:, 6 + j // 4, (j % 4) * P:(j % 4 + 1) * P], m.ones[:], s["diag"][:, j], start=True, stop=True)
            last.then_inc(s["rows_done"], 1)

        @block.vector
        def _(dve):
            link = Chain(dve, s["chain"])
            dve.wait_ge(s["sum_done"], KC)
            link(nc.vector.tensor_scalar(var, m.ps[:, 0:NT, 0], 1.0 / D, EPS, ALU.mult, ALU.add))
            dve.wait_ge(s["root_done"], 1)
            refined_rsqrt(nc, link, r, var, s["tmp"][:])
            for j in range(NT):
                nc.vector.tensor_scalar_mul(s["diag"][:, j], m.ident[:], r[:, j:j + 1]).then_inc(s["diag_done"], 1)
            dve.wait_ge(s["rows_done"], 1)
            rows = m.ps[:, 6:8].rearrange("p b n -> p (b n)")[:, 0:n_tok]
            for c in range(KC):
                nc.vector.tensor_tensor(out[:, c, 0:n_tok], rows, m.resid[:, c, 0:n_tok], ALU.mult).then_inc(s["scaled"], 1)


def hyena_in_loads(w_in, l, early, g):
    w, loaded = early

    def run(sp):
        sp.dma_start(w[:, g % 2], w_in[l].rearrange("(c p) n -> p c n", p=P)[:, :, g * HW:(g + 1) * HW]).then_inc(loaded[g % 2], 16)
    return run


def hyena_in_stage(nc, m, l, w_in, streams, early, then):
    n_tok = sum(n for _, _, n in streams)
    tiles = n_tok // P
    NT = 3 * HC
    PAD = TOK + 4
    first = {0: 1, 1: SEQ + 3}
    w, loaded = early
    with stage(nc, f"hyin{l}", ["mm_done", "p_done", "mid_done", "conv_done", "zeroed", "taps",
                                "tr_done", "tr_evac"],
               [("p", [P, 2, PAD]), ("conv", [P, 2, TOK])]) as (block, s):
        def col(row, i):
            return m.cols[:, l, row + i:row + i + 1]

        @block.sync
        def _(sp):
            sp.wait_ge(s["mm_done"], HC)
            hyena_in_loads(w_in, l, early, 2)(sp)
            then(sp)

        @block.tensor
        def _(pe):
            def transposes(i):
                pe.wait_ge(s["conv_done"], i + 1)
                if i >= 1:
                    pe.wait_ge(s["tr_evac"], 2 * i)
                for t, at, n in streams:
                    by_parity = s["conv"][:, i % 2, at:at + n].rearrange("p (x r q) -> p q x r", r=P, q=2)
                    for j in range(n // P):
                        parity, x = divmod(j, n // P // 2)
                        last = nc.tensor.transpose(m.ps[:, 4 + t, j * P:(j + 1) * P], by_parity[:, parity, x], m.ident[:])
                last.then_inc(s["tr_done"], 1)

            for i in range(NT):
                if i % HC == 0:
                    g = i // HC
                    pe.wait_ge(loaded[g % 2], 16 * (g // 2 + 1))
                if i >= 2:
                    pe.wait_ge(s["p_done"], i - 1)
                    pe.wait_ge(s["mid_done"], i - 1)
                for t, at, n in streams:
                    for c in range(KC):
                        last = nc.tensor.matmul(m.ps[:, 2 * (i % 2) + t, 0:n], w[:, (i // HC) % 2, c, (i % HC) * P:(i % HC + 1) * P],
                                                m.u[:, c, at:at + n], start=c == 0, stop=c == KC - 1)
                last.then_inc(s["mm_done"], 1)
                if 1 <= i <= 2 * HC:
                    transposes(i - 1)

        @block.scalar
        def _(act):
            act.wait_ge(s["zeroed"], 1)
            for i in range(NT):
                if 2 <= i <= 2 * HC + 1:
                    k = i - 2
                    act.wait_ge(s["tr_done"], k + 1)
                    dst = m.v if k < HC else m.x1
                    for half in range(2):
                        a, b = 4 * half, min(4 * half + 4, tiles)
                        if a < b:
                            ins = nc.scalar.activation(dst[:, a:b, (k % HC) * P:(k % HC + 1) * P],
                                                       m.ps[:, 4 + half, 0:(b - a) * P].rearrange("p (j c) -> p j c", c=P),
                                                       ACT.Copy)
                            ins.then_inc(s["tr_evac"], 1 if tiles > 4 else 2)
                act.wait_ge(s["mm_done"], i + 1)
                if i >= 2:
                    act.wait_ge(s["conv_done"], i - 1)
                for t, at, n in streams:
                    last = nc.scalar.activation(s["p"][:, i % 2, first[t]:first[t] + n], m.ps[:, 2 * (i % 2) + t, 0:n], ACT.Copy)
                last.then_inc(s["p_done"], 1)
                dst = s["conv"][:, i % 2] if i < 2 * HC else m.x2[:, i - 2 * HC]
                if 2 <= i < 2 * HC:
                    act.wait_ge(s["tr_done"], i - 1)
                for t, at, n in streams:
                    last = nc.scalar.activation(dst[:, at:at + n], m.ps[:, 2 * (i % 2) + t, 0:n], ACT.Identity,
                                                scale=col(R_SCW + NT, i), bias=col(R_SCB, i))
                last.then_inc(s["mid_done"], 1)

        @block.vector
        def _(dve):
            nc.vector.memset(s["p"][:], 0.0).then_inc(s["zeroed"], 1)
            for i in range(NT):
                dst = s["conv"][:, i % 2] if i < 2 * HC else m.x2[:, i - 2 * HC]
                dve.wait_ge(s["mid_done"], i + 1)
                dve.wait_ge(s["p_done"], i + 1)
                for k, tap in enumerate((0, 2)):
                    for t, at, n in streams:
                        f = first[t] + tap - 1
                        last = nc.vector.scalar_tensor_tensor(dst[:, at:at + n], s["p"][:, i % 2, f:f + n],
                                                              col(R_SCW + tap * NT, i), dst[:, at:at + n],
                                                              ALU.mult, ALU.add)
                    if k == 0:
                        last.then_inc(s["taps"], 1)
                        dve.wait_ge(s["taps"], i + 1)
                last.then_inc(s["conv_done"], 1)


def conv_shape(name):
    n = (SEQ, CTX)[int(name[-1])]
    return [P, 2, n // P // 2, 2, HW] if name[0] == "h" else [P, 4, n // P // 2, n // 2]


def conv_load(sp, early, name, l, o, consts, dram):
    buf, loaded = early[name]
    kind, t = name[:-1], int(name[-1])
    src = dram["h"][l][t][o] if kind == "h" else consts[f"{kind}_{'xc'[t]}"].rearrange("e (j p) k -> p e j k", p=P)
    sp.dma_start(buf[:], src).then_inc(loaded, 16)


def conv_stage(nc, m, l, streams, consts, dram, early, then):
    HALF = HW // 2
    jobs = [(t, at, n, o, half) for o in range(2) for t, at, n in streams for half in range(2)]
    NJ = len(jobs)
    order0 = {(t, half): i for i, (t, _, _, o, half) in enumerate(jobs) if o == 0}
    sems = ["dft1_in", "idft0_in", "idft1_in", "h1_in", "fwd_done", "other_done", "z_done", "u_done", "sine_done", "dve", "y_done", "inv_done", "evac"]
    own = [name for t, _, _ in streams for name in (f"dft{t}", f"h{t}", f"idft{t}") if name not in early]
    bufs = [(name, conv_shape(name)) for name in own]
    chunks = XT // 2
    bufs += [("other", [P, chunks, 2 * HALF]), ("t", [P, 2, chunks, 2, HALF]),
             ("u", [P, 2, chunks, 2, HALF]), ("y", [P, 2, 2, chunks, 2, HALF])]
    with stage(nc, f"conv{l}", sems, bufs) as (block, s):
        data = {**early, **{name: (s[name], s[f"{name}_in"]) for name in own}}

        @block.sync
        def _(sp):
            for name in own:
                conv_load(sp, data, name, l, 0, consts, dram)
            for t, _, _ in streams:
                sp.wait_ge(s["dve"], 2 * order0[t, 1] + 1)
                conv_load(sp, data, f"h{t}", l, 1, consts, dram)
            then(sp)

        @block.tensor
        def _(pe):
            def forward(i):
                t, at, n, o, half = jobs[i]
                J, tok0, cols = n // P // 2, at // P, slice(half * HALF, (half + 1) * HALF)
                src = m.x1 if o else m.v
                dft, loaded = data[f"dft{t}"]
                pe.wait_ge(loaded, 16)
                if o:
                    pe.wait_ge(s["evac"], order0[t, half] + 1)
                if i >= 1:
                    pe.wait_ge(s["z_done"], i)
                for j in range(J):
                    for e in range(4):
                        for x in range(J):
                            last = nc.tensor.matmul(m.ps[:, 2 * j + e // 2, (e % 2) * HALF:(e % 2 + 1) * HALF],
                                                    dft[:, e, x, j * P:(j + 1) * P],
                                                    src[:, tok0 + PARITY[e] * J + x, cols], start=x == 0, stop=x == J - 1)
                last.then_inc(s["fwd_done"], 1)

            def inverse(i):
                t, at, n, o, half = jobs[i]
                J, y = n // P // 2, s["y"][:, i % 2]
                mat, loaded = data[f"idft{t}"]
                pe.wait_ge(loaded, 16)
                pe.wait_ge(s["y_done"], i + 1)
                if i >= 2:
                    pe.wait_ge(s["evac"], i - 1)
                b = 4 + 2 * (i % 2)
                for q in range(2 * J if o == 0 else 2):
                    for parity in (range(2) if o else (q // J,)):
                        parts = ((0, 0), (1, 3)) if parity == 0 else ((0, 2), (1, 1))
                        k = 0
                        for part, e in parts:
                            for x in range(J):
                                if o == 0:
                                    out, lhs, rhs = (m.ps[:, b + q // 2, (q % 2) * HALF:(q % 2 + 1) * HALF],
                                                     mat[:, e, x, (q % J) * P:(q % J + 1) * P], y[:, parity, x, part])
                                else:
                                    out, lhs, rhs = (m.ps[:, b + q, parity * n // 2:(parity + 1) * n // 2],
                                                     y[:, parity, x, part, q * P:(q + 1) * P], mat[:, e, x])
                                last = nc.tensor.matmul(out, lhs, rhs, start=k == 0, stop=k == 2 * J - 1)
                                k += 1
                last.then_inc(s["inv_done"], 1)

            for i in range(NJ):
                forward(i)
                if i >= 1:
                    inverse(i - 1)
            inverse(NJ - 1)

        @block.scalar
        def _(act):
            for i, (t, at, n, o, half) in enumerate(jobs):
                J = n // P // 2
                act.wait_ge(s["fwd_done"], i + 1)
                if i >= 1:
                    act.wait_ge(s["z_done"], i)
                nc.scalar.activation(s["other"][:, 0:J], m.ps[:, 1:2 * J:2], ACT.Copy).then_inc(s["other_done"], 1)

        @block.gpsimd
        def _(pool):
            for i, (t, at, n, o, half) in enumerate(jobs):
                J = n // P // 2
                pool.wait_ge(s["u_done"], i + 1)
                u = s["u"][:, :, 0:J]
                nc.gpsimd.tensor_tensor(u[:, :, :, 0], u[:, :, :, 0], u[:, :, :, 1], ALU.add).then_inc(s["sine_done"], 1)

        @block.vector
        def _(dve):
            link = Chain(dve, s["dve"])

            def products(i):
                t, at, n, o, half = jobs[i]
                J = n // P // 2
                w, u = s["t"][:, :, 0:J], s["u"][:, :, 0:J]
                z = s["y"][:, i % 2, :, 0:J]
                transfer, loaded = data[f"h{t}"]
                h = transfer[:, :, :, :, half * HALF:(half + 1) * HALF]
                dve.wait_ge(s["fwd_done"], i + 1)
                dve.wait_ge(s["other_done"], i + 1)
                if i >= 2:
                    dve.wait_ge(s["inv_done"], i - 1)
                first, other = m.ps[:, 0:2 * J:2], s["other"][:, 0:J]
                nc.vector.tensor_tensor(z[:, 0].rearrange("p j c n -> p j (c n)"), first, other, ALU.add)
                nc.vector.tensor_tensor(z[:, 1].rearrange("p j c n -> p j (c n)"), first, other, ALU.subtract).then_inc(s["z_done"], 1)
                dve.wait_ge(s["z_done"], i + 1)
                dve.wait_ge(loaded, 16 * (o + 1))
                nc.vector.tensor_tensor(u[:, :, :, 0], z[:, :, :, 0], h[:, :, :, 1], ALU.mult)
                nc.vector.tensor_tensor(u[:, :, :, 1], z[:, :, :, 1], h[:, :, :, 0], ALU.mult).then_inc(s["u_done"], 1)
                for c in range(2):
                    last = nc.vector.tensor_tensor(w[:, :, :, c], z[:, :, :, c], h[:, :, :, c], ALU.mult)
                link(last)

            def sums(i):
                t, at, n, o, half = jobs[i]
                J = n // P // 2
                w, u, y = s["t"][:, :, 0:J], s["u"][:, :, 0:J], s["y"][:, i % 2, :, 0:J]
                link(nc.vector.tensor_tensor(w[:, :, :, 0], w[:, :, :, 0], w[:, :, :, 1], ALU.subtract))
                nc.vector.tensor_tensor(y[:, 0, :, 0], w[:, 0, :, 0], w[:, 1, :, 0], ALU.add)
                nc.vector.tensor_tensor(y[:, 1, :, 0], w[:, 0, :, 0], w[:, 1, :, 0], ALU.subtract)
                dve.wait_ge(s["sine_done"], i + 1)
                nc.vector.tensor_tensor(y[:, 0, :, 1], u[:, 0, :, 0], u[:, 1, :, 0], ALU.subtract)
                nc.vector.tensor_tensor(y[:, 1, :, 1], u[:, 0, :, 0], u[:, 1, :, 0], ALU.add).then_inc(s["y_done"], 1)
                dve.wait_ge(s["y_done"], i + 1)

            def gate(i):
                t, at, n, o, half = jobs[i]
                dve.wait_ge(s["inv_done"], i + 1)
                b = 4 + 2 * (i % 2)
                if o == 0:
                    x = m.x1[:, at // P:(at + n) // P, half * HALF:(half + 1) * HALF]
                    got = m.ps[:, b:b + n // P // 2].rearrange("p b (q c) -> p (b q) c", q=2)
                    nc.vector.tensor_tensor(x, got, x, ALU.mult).then_inc(s["evac"], 1)
                else:
                    for c in range(2):
                        out, x = (z[:, 2 * half + c, at:at + n].rearrange("p (x q) -> p q x", q=2) for z in (m.yh, m.x2))
                        last = nc.vector.tensor_tensor(out, m.ps[:, b + c, 0:n].rearrange("p (q x) -> p q x", q=2), x, ALU.mult)
                    last.then_inc(s["evac"], 1)

            for i in range(NJ):
                products(i)
                if i >= 1:
                    gate(i - 1)
                sums(i)
            gate(NJ - 1)


def qkv_stage(nc, m, l, w_in, w_ukv, consts, streams_q, early, then):
    both = spans(True)
    NU = QC + KVC + 1
    tiles_of = [sum(n for _, _, n in streams_q) // P, TT]
    turns = [(k, j) for k in (1, 0) for j in range(tiles_of[k])]
    src = w_in[l].rearrange("(c p) n -> p c n", p=P)
    w, w_loaded = early
    with stage(nc, f"qkv{l}", ["wkr_in", "wv_in", "rope_in", "zeroed", "swapped", "mm_done", "raw_done", "sq_done",
                               "sum_done", "dve", "root_done", "diag_done", "rows_done", "norm_done", "v_done", "v_evac"],
               [("wkr", [P, KC, P]), ("wv", [P, KVC, HEADS, VD]), ("raw", [P, QC + KVC, TOK]),
                ("sq", [P, QC + KVC, TOK]), ("r", [P, sum(tiles_of)]), ("var", [P, sum(tiles_of)]), ("tmp", [P, sum(tiles_of)]),
                ("diag", [P, sum(tiles_of), P]), ("t", [P, 2, SEQ]), ("g", [P, QC])]) as (block, s):
        def streams(i):
            return streams_q if i < QC else both

        @block.sync
        def _(sp):
            sp.wait_ge(s["zeroed"], 1)
            sp.dma_start(s["wkr"][:, :, NOPE:QK], src[:, :, KR0:G0]).then_inc(s["wkr_in"], 16)
            sp.dma_start(m.rope[:], consts["rope"]).then_inc(s["rope_in"], 16)
            for c in range(KVC):
                v_cols = w_ukv[l, c * P:(c + 1) * P].rearrange("p (h k) -> p h k", h=HEADS)[:, :, NOPE:NOPE + VD]
                sp.dma_start(s["wv"][:, c], v_cols).then_inc(s["wv_in"], 16)
            then(sp)

        @block.gpsimd
        def _(pool):
            nc.gpsimd.memset(s["wkr"][:], 0.0).then_inc(s["zeroed"], 1)
            pool.wait_ge(s["wkr_in"], 16)
            raw = s["wkr"][:, :, NOPE:QK].rearrange("p c (a h k) -> p c a h k", a=2, h=2)
            swap = s["wkr"][:, :, QK:P].rearrange("p c (a h k) -> p c a h k", a=2, h=2)
            for h in range(2):
                for a in range(2):
                    nc.gpsimd.tensor_copy(swap[:, :, a, h], raw[:, :, a, 1 - h]).then_inc(s["swapped"], 1)

        @block.tensor
        def _(pe):
            def sums(k):
                first, past = ((0, QC), (QC, QC + KVC))[k]
                pe.wait_ge(s["sq_done"], past)
                for j in range(tiles_of[k]):
                    for c in range(first, past):
                        last = nc.tensor.matmul(m.ps[:, 4 + k, j:j + 1], s["sq"][:, c, j * P:(j + 1) * P], m.ones[:, 0:1],
                                                start=c == first, stop=c == past - 1)
                last.then_inc(s["sum_done"], 1)

            def rows(k):
                for n, (kind, j) in enumerate(turns):
                    if kind == k:
                        pe.wait_ge(s["diag_done"], n + 1)
                        last = nc.tensor.matmul(m.ps[:, (4, 6)[k] + j // 4, (j % 4) * P:(j % 4 + 1) * P], m.ones[:], s["diag"][:, n],
                                                start=True, stop=True)
                last.then_inc(s["rows_done"], 1)

            pe.wait_ge(w_loaded, 16)
            for i in range(NU):
                if i >= 2:
                    pe.wait_ge(s["sq_done"], i - 1)
                    pe.wait_ge(s["raw_done"], i - 1)
                if i == NU - 1:
                    pe.wait_ge(s["swapped"], 4)
                for t, at, n in streams(i):
                    for c in range(KC):
                        lhs = w[:, c, i * P:(i + 1) * P] if i < NU - 1 else s["wkr"][:, c]
                        last = nc.tensor.matmul(m.ps[:, 2 * (i % 2) + t, 0:n], lhs, m.u[:, c, at:at + n],
                                                start=c == 0, stop=c == KC - 1)
                last.then_inc(s["mm_done"], 1)
                if i in (QC, QC + KVC):
                    sums(0 if i == QC else 1)
            for k in (1, 0):
                rows(k)
            pe.wait_ge(s["wv_in"], 16 * KVC)
            pe.wait_ge(s["norm_done"], KVC)
            for j in range(TT):
                if j >= 2:
                    pe.wait_ge(s["v_evac"], j - 1)
                for c in range(KVC):
                    last = nc.tensor.matmul(m.ps[:, j % 2], m.kvn[:, c, j * P:(j + 1) * P], s["wv"][:, c],
                                            start=c == 0, stop=c == KVC - 1)
                last.then_inc(s["v_done"], 1)

        @block.scalar
        def _(act):
            nc.scalar.mul(s["g"][:], m.cols[:, l, R_QG:R_QG + QC], SCALE)
            for i in range(NU - 1):
                act.wait_ge(s["mm_done"], i + 1)
                for t, at, n in streams(i):
                    last = nc.scalar.activation(s["raw"][:, i, at:at + n], m.ps[:, 2 * (i % 2) + t, 0:n], ACT.Copy)
                last.then_inc(s["raw_done"], 1)
                for t, at, n in streams(i):
                    last = nc.scalar.activation(s["sq"][:, i, at:at + n], m.ps[:, 2 * (i % 2) + t, 0:n], ACT.Square)
                last.then_inc(s["sq_done"], 1)
            act.wait_ge(s["dve"], 1)
            nc.scalar.activation(s["r"][:], s["var"][:], ACT.Sqrt).then_inc(s["root_done"], 1)
            for j in range(TT):
                act.wait_ge(s["v_done"], j + 1)
                nc.scalar.activation(m.vt[:, j], m.ps[:, j % 2], ACT.Copy).then_inc(s["v_evac"], 1)

        @block.vector
        def _(dve):
            link = Chain(dve, s["dve"])
            NQ = tiles_of[0]
            dve.wait_ge(s["sum_done"], 2)
            for k, width in ((0, QL), (1, KVL)):
                last = nc.vector.tensor_scalar(s["var"][:, k * NQ:k * NQ + tiles_of[k]], m.ps[:, 4 + k, 0:tiles_of[k]], 1.0 / width, EPS,
                                               ALU.mult, ALU.add)
            link(last)
            dve.wait_ge(s["root_done"], 1)
            refined_rsqrt(nc, link, s["r"][:], s["var"][:], s["tmp"][:])
            for n, (k, j) in enumerate(turns):
                nc.vector.tensor_scalar_mul(s["diag"][:, n], m.ident[:], s["r"][:, k * NQ + j:k * NQ + j + 1]).then_inc(s["diag_done"], 1)
            for i in (*range(QC, QC + KVC), *range(QC)):
                n = sum(n for _, _, n in streams(i))
                k, out, g = (0, m.qn[:, i, 0:n], s["g"][:, i:i + 1]) if i < QC else \
                    (1, m.kvn[:, i - QC, 0:n], m.cols[:, l, R_KVG + i - QC:R_KVG + i - QC + 1])
                dve.wait_ge(s["rows_done"], 2 - k)
                row = m.ps[:, (4, 6)[k]:(4, 6)[k] + 2].rearrange("p b n -> p (b n)")[:, 0:n]
                nc.vector.scalar_tensor_tensor(out, row, g, s["raw"][:, i, 0:n], ALU.mult, ALU.mult).then_inc(s["norm_done"], 1)
            b = 2 * ((NU - 1) % 2)
            dve.wait_ge(s["mm_done"], NU)
            dve.wait_ge(s["rope_in"], 16)
            nc.vector.tensor_tensor(s["t"][NOPE:QK, 0], m.ps[NOPE:QK, b], m.rope[NOPE:QK], ALU.mult)
            link(nc.vector.tensor_tensor(s["t"][NOPE:QK, 1], m.ps[QK:P, b], m.rope[QK:P], ALU.mult))
            for h in range(2):
                nc.vector.tensor_tensor(m.key[NOPE:QK, h, 0:SEQ], s["t"][NOPE:QK, 0], s["t"][NOPE:QK, 1], ALU.add)
                nc.vector.tensor_copy(m.key[NOPE:QK, h, SEQ:TOK], m.ps[NOPE:QK, b + 1, 0:CTX])


def attention_loads(eng, l, i, a, early):
    wq, wk, loaded = early
    wq_src = a["w_uq"][l].rearrange("(c p) (h k) -> p c h k", p=P, k=QK)
    wk_src = a["w_ukv"][l].rearrange("(c p) (h k) -> p c h k", p=P, k=NOPE + VD)

    def run(h):
        eng.dma_start(wq[:, h, :, 0:QK], wq_src[:, :, i * 2 + h]).then_inc(loaded[h], 16)
        eng.dma_start(wk[:, h], wk_src[:, :, i * 2 + h, 0:NOPE]).then_inc(loaded[h], 16)
    return run


def attention_stage(nc, m, l, a, streams_q, early, then):
    n_q = sum(n for _, _, n in streams_q)
    units = [(j, 0, TOK) for j in range(XT)] + [(XT + j, SEQ, CTX) for j in range((n_q - SEQ) // P)]
    NU = 2 * len(units)
    NT = n_q // P
    ctx_q = len(streams_q) > 1
    wq, wk, loaded = early
    work = [(h, *u) for h in range(2) for u in units]
    with stage(nc, f"attn{l}", ["swapped", "turns", "proj_done", "q_done", "dve", "rot_done", "qk_done",
                                "s_done", "max_done", "exp_done", "tr_done", "ta_done", "tv_done", "pv_done", "o_done",
                                "back", "back_evac"],
               [("t", [P, 2, SEQ]), ("qrot", [P, 2, SEQ]),
                ("q", [P, 2, TOK]), ("p", [P, 2, TOK]), ("pt", [P, 2, TT, P]), ("nm", [P, 2]), ("sum", [P, 4]),
                ("rs", [P, 2]), ("otok", [P, TT, HEADS * VD])]) as (block, s):

        def act_share(nk):
            return 4 if nk == TOK else nk // P // 2

        def proj_bank(h):
            return 4 if h == 0 else 0

        @block.sync
        def _(sp):
            with sp.Fori(1, HEADS // 2) as i:
                for h in range(2):
                    sp.wait_ge(s["proj_done"], i * 4 + (2 * h + 2))
                    attention_loads(sp, l, i, a, early)(h)
            then(sp)

        @block.gpsimd
        def _(pool):
            with pool.Fori(0, HEADS // 2) as i:
                for h in range(2):
                    pool.wait_ge(loaded[h], i * 32 + 32)
                    pool.sem_inc(s["turns"], 1)
                    raw = wq[:, h, :, NOPE:QK].rearrange("p c (a h k) -> p c a h k", a=2, h=2)
                    swap = wq[:, h, :, QK:P].rearrange("p c (a h k) -> p c a h k", a=2, h=2)
                    for b in range(2):
                        for a in range(2):
                            nc.gpsimd.tensor_copy(swap[:, :, a, b], raw[:, :, a, 1 - b]).then_inc(s["swapped"], 1)

        @block.tensor
        def _(pe):
            pe.sem_inc(s["proj_done"], 4)
            pe.sem_inc(s["tr_done"], 2)
            pe.sem_inc(s["pv_done"], 2)

            def project(i, h):
                pe.wait_ge(loaded[h], i * 32 + 32)
                pe.wait_ge(s["swapped"], i * 8 + (4 * h + 4))
                b = proj_bank(h)
                for bank, off, n, at, wide in ((b, 0, SEQ, 0, True), (b + 1, 0, SEQ, 0, False),
                                               (b + 2, 0, CTX, SEQ, True), (b + 2, CTX, CTX, SEQ, False)):
                    if wide and at and not ctx_q:
                        continue
                    w, z, k = (wq, m.qn, QC) if wide else (wk, m.kvn, KVC)
                    out = m.ps[0:P if wide else NOPE, bank, off:off + n]
                    for c in range(k):
                        last = nc.tensor.matmul(out, w[:, h, c], z[:, c, at:at + n], start=c == 0, stop=c == k - 1)
                    if wide and not at:
                        last.then_inc(s["proj_done"], 1)
                last.then_inc(s["proj_done"], 1)

            def scores(i, u):
                h, j, k0, nk = work[u]
                pe.wait_ge(s["exp_done"], i * NU + (u + 1))
                b = 2 * (u % 2)
                if j < XT:
                    nc.tensor.matmul(m.ps[:, b], s["qrot"][0:QK, h, j * P:(j + 1) * P], m.key[0:QK, h, 0:SEQ], start=True, stop=True)
                off = 1 if j < XT else 0
                nc.tensor.matmul(m.ps[:, b + off, 0:CTX], s["q"][0:QK, h, j * P:(j + 1) * P], m.key[0:QK, h, SEQ:TOK],
                                 start=True, stop=True).then_inc(s["s_done"], 1)

            def transposes(i, u):
                _, _, _, nk = work[u]
                pe.wait_ge(s["exp_done"], i * NU + (u + 3))
                pe.wait_ge(s["ta_done"], i * NU + (u + 1))
                pe.wait_ge(s["tv_done"], i * NU + (u + 1))
                na = act_share(nk)
                for k in range(nk // P):
                    kb = k if k < na else k - na
                    last = nc.tensor.transpose(m.ps[:, 4 if k < na else 5, kb * P:(kb + 1) * P],
                                               s["p"][:, u % 2, k * P:(k + 1) * P], m.ident[:])
                last.then_inc(s["tr_done"], 1)

            def values(i, u):
                h, j, k0, nk = work[u]
                pe.wait_ge(s["ta_done"], i * NU + (u + 2))
                pe.wait_ge(s["tv_done"], i * NU + (u + 2))
                pe.wait_ge(s["o_done"], i * NU + (u + 1))
                for k in range(nk // P):
                    last = nc.tensor.matmul(m.ps[:, 6 + u % 2, 0:VD], s["pt"][:, u % 2, k],
                                            m.vt[:, k0 // P + k, bass.ds((i * 2 + h) * VD, VD)], start=k == 0, stop=k == nk // P - 1)
                last.then_inc(s["pv_done"], 1)

            with pe.Fori(0, HEADS // 2) as i:
                pe.wait_ge(s["exp_done"], i * NU + 2)
                pe.wait_ge(s["ta_done"], i * NU + 1)
                pe.wait_ge(s["tv_done"], i * NU + 1)
                pe.wait_ge(s["o_done"], i * NU + 2)
                for h in range(2):
                    project(i, h)
                pe.wait_ge(s["q_done"], i * 2 + 2)
                pe.wait_ge(s["qk_done"], i * 2 + 2)
                for u in range(NU + 2):
                    if u < NU:
                        scores(i, u)
                    if 1 <= u <= NU:
                        transposes(i, u - 1)
                    if u >= 2:
                        values(i, u - 2)
            pe.wait_ge(s["o_done"], HEADS // 2 * NU + 2)
            for j in range(NT):
                if j >= 2:
                    pe.wait_ge(s["back_evac"], j - 1)
                for c in range(HC):
                    last = nc.tensor.transpose(m.ps[:, j % 2, c * P:(c + 1) * P], s["otok"][:, j, c * P:(c + 1) * P], m.ident[:])
                last.then_inc(s["back"], 1)

        @block.scalar
        def _(act):
            act.sem_inc(s["exp_done"], 2)
            act.sem_inc(s["ta_done"], 1)

            def copy_projected(i, h):
                b = proj_bank(h)
                act.wait_ge(s["proj_done"], i * 4 + (2 * h + 6))
                if h == 0:
                    act.wait_ge(s["pv_done"], i * NU + 2)
                nc.scalar.activation(m.key[0:NOPE, h, 0:SEQ], m.ps[0:NOPE, b + 1], ACT.Copy)
                if ctx_q:
                    nc.scalar.activation(s["q"][0:QK, h, SEQ:TOK], m.ps[0:QK, b + 2, 0:CTX], ACT.Copy)
                nc.scalar.activation(m.key[0:NOPE, h, SEQ:TOK], m.ps[0:NOPE, b + 2, CTX:2 * CTX], ACT.Copy)
                act.wait_ge(s["rot_done"], i * 2 + (h + 1))
                nc.scalar.activation(s["q"][0:QK, h, 0:SEQ], m.ps[0:QK, b], ACT.Copy).then_inc(s["qk_done"], 1)

            def exponential(i, u):
                h, j, k0, nk = work[u]
                act.wait_ge(s["max_done"], i * NU + (u + 1))
                act.wait_ge(s["tr_done"], i * NU + (u + 1))
                b = 2 * (u % 2)
                nc.scalar.activation(s["p"][:, u % 2, 0:nk], m.ps[:, b:b + 2].rearrange("p b k -> p (b k)")[:, 0:nk], ACT.Exp,
                                     bias=s["nm"][:, u % 2:u % 2 + 1], accum_out=s["sum"][:, u % 4:u % 4 + 1]).then_inc(s["exp_done"], 1)

            def copy_transposed(i, u):
                _, _, _, nk = work[u]
                act.wait_ge(s["tr_done"], i * NU + (u + 3))
                act.wait_ge(s["pv_done"], i * NU + (u + 1))
                n = act_share(nk)
                nc.scalar.activation(s["pt"][:, u % 2, 0:n], m.ps[:, 4, 0:n * P].rearrange("p (k q) -> p k q", q=P),
                                     ACT.Copy).then_inc(s["ta_done"], 1)

            with act.Fori(0, HEADS // 2) as i:
                for h in range(2):
                    copy_projected(i, h)
                for u in range(NU + 1):
                    if u < NU:
                        exponential(i, u)
                    if u >= 1:
                        copy_transposed(i, u - 1)

        @block.vector
        def _(dve):
            dve.sem_inc(s["tv_done"], 1)
            dve.sem_inc(s["o_done"], 2)

            def rotate(i, h):
                b = proj_bank(h)
                dve.wait_ge(s["proj_done"], i * 4 + (2 * h + 5))
                if h == 0:
                    dve.wait_ge(s["pv_done"], i * NU + 2)
                nc.vector.tensor_tensor(s["t"][NOPE:QK, 0], m.ps[NOPE:QK, b], m.rope[NOPE:QK], ALU.mult)
                nc.vector.tensor_tensor(s["t"][NOPE:QK, 1], m.ps[QK:P, b], m.rope[QK:P], ALU.mult)
                nc.vector.tensor_copy(s["qrot"][0:NOPE, h], m.ps[0:NOPE, b]).then_inc(s["rot_done"], 1)
                dve.wait_ge(s["rot_done"], i * 2 + (h + 1))
                nc.vector.tensor_tensor(s["qrot"][NOPE:QK, h], s["t"][NOPE:QK, 0], s["t"][NOPE:QK, 1], ALU.add).then_inc(s["q_done"], 1)
                dve.wait_ge(s["q_done"], i * 2 + (h + 1))

            def maximum(i, u):
                h, j, k0, nk = work[u]
                dve.wait_ge(s["s_done"], i * NU + (u + 1))
                dve.wait_ge(s["exp_done"], i * NU + (u + 1))
                b = 2 * (u % 2)
                nc.vector.tensor_reduce(s["nm"][:, u % 2:u % 2 + 1], m.ps[:, b:b + 2].rearrange("p b k -> p (b k)")[:, 0:nk],
                                        axis=AX.X, op=ALU.max, negate=True).then_inc(s["max_done"], 1)

            def copy_transposed(i, u):
                _, _, _, nk = work[u]
                dve.wait_ge(s["tr_done"], i * NU + (u + 3))
                dve.wait_ge(s["pv_done"], i * NU + (u + 1))
                na, n = act_share(nk), nk // P - act_share(nk)
                nc.vector.tensor_copy(s["pt"][:, u % 2, na:na + n],
                                      m.ps[:, 5, 0:n * P].rearrange("p (k q) -> p k q", q=P)).then_inc(s["tv_done"], 1)

            def output(i, u):
                h, j, k0, nk = work[u]
                r = s["rs"][:, u % 2:u % 2 + 1]
                dve.wait_ge(s["o_done"], i * NU + (u + 1))
                nc.vector.reciprocal(r, s["sum"][:, u % 4:u % 4 + 1]).then_inc(s["dve"], 1)
                dve.wait_ge(s["dve"], i * NU + (u + 1))
                dve.wait_ge(s["pv_done"], i * NU + (u + 3))
                nc.vector.tensor_scalar_mul(s["otok"][:, j, bass.ds((i * 2 + h) * VD, VD)], m.ps[:, 6 + u % 2, 0:VD],
                                            r).then_inc(s["o_done"], 1)

            with dve.Fori(0, HEADS // 2) as i:
                for h in range(2):
                    rotate(i, h)
                for u in range(NU + 2):
                    if u < NU:
                        maximum(i, u)
                    if 1 <= u <= NU:
                        copy_transposed(i, u - 1)
                    if u >= 2:
                        output(i, u - 2)
            for j in range(NT):
                dve.wait_ge(s["back"], j + 1)
                nc.vector.tensor_copy(m.ya[:, :, j * P:(j + 1) * P],
                                      m.ps[:, j % 2].rearrange("p (c t) -> p c t", c=HC)).then_inc(s["back_evac"], 1)


MERGE_KW = 2 * KC + 2 * HC


def merge_loads(eng, l, i, b, a, early):
    w, loaded = early
    for at, n, src, col in ((0, KC, a["w_in"], G0), (KC, KC, a["w_in"], G0 + D), (2 * KC, HC, a["w_hy_o"], 0),
                            (2 * KC + HC, HC, a["w_mla_o"], 0)):
        eng.dma_start(w[:, b, at:at + n], src[l].rearrange("(c p) n -> p c n", p=P)[:, :, bass.ds(i * (2 * P) + (b * P + col), P)]
                      ).then_inc(loaded[b], 16)


def merge_stage(nc, m, l, a, streams, early, then):
    NS = len(streams)
    w, loaded = early
    with stage(nc, f"merge{l}", ["mm_done", "sig_done", "prod_done", "mix_done"],
               [("sig", [P, 2, 2, SEQ]), ("t", [P, 2, 2, SEQ])]) as (block, s):
        @block.sync
        def _(sp):
            with sp.Fori(1, KC // 2) as i:
                for b in range(2):
                    sp.wait_ge(s["mm_done"], i * (2 * NS) + (b + 1) * NS)
                    merge_loads(sp, l, i, b, a, early)
            then(sp)

        @block.tensor
        def _(pe):
            pe.sem_inc(s["mm_done"], 2 * NS)
            with pe.Fori(0, KC // 2) as i:
                for b in range(2):
                    pe.wait_ge(loaded[b], i * 64 + 64)
                    for t, at, n in streams:
                        k = b * NS + t
                        pe.wait_ge(s["prod_done"], i * (2 * NS) + (k + 1))
                        q = 4 * (k % 2)
                        for bank, w_at, z, kn in ((q, 0, m.u, KC), (q + 1, KC, m.u, KC), (q + 2, 2 * KC, m.yh, HC),
                                                  (q + 3, 2 * KC + HC, m.ya, HC)):
                            for c in range(kn):
                                last = nc.tensor.matmul(m.ps[:, bank, 0:n], w[:, b, w_at + c], z[:, c, at:at + n],
                                                        start=c == 0, stop=c == kn - 1)
                        last.then_inc(s["mm_done"], 1)

        @block.scalar
        def _(act):
            with act.Fori(0, KC // 2) as i:
                for b in range(2):
                    for t, at, n in streams:
                        k = b * NS + t
                        act.wait_ge(s["mm_done"], i * (2 * NS) + (k + 1 + 2 * NS))
                        act.wait_ge(s["prod_done"], i * (2 * NS) + (k + 1))
                        nc.scalar.activation(s["sig"][:, k % 2, :, 0:n], m.ps[:, 4 * (k % 2):4 * (k % 2) + 2, 0:n],
                                             ACT.Sigmoid).then_inc(s["sig_done"], 1)

        @block.vector
        def _(dve):
            dve.sem_inc(s["prod_done"], 2)
            with dve.Fori(0, KC // 2) as i:
                for b in range(2):
                    for t, at, n in streams:
                        k = b * NS + t
                        dve.wait_ge(s["sig_done"], i * (2 * NS) + (k + 1))
                        dve.wait_ge(s["mix_done"], i * (2 * NS) + (k + 1))
                        nc.vector.tensor_tensor(s["t"][:, k % 2, :, 0:n], m.ps[:, 4 * (k % 2) + 2:4 * (k % 2) + 4, 0:n],
                                                s["sig"][:, k % 2, :, 0:n], ALU.mult).then_inc(s["prod_done"], 1)

        @block.gpsimd
        def _(pool):
            pool.sem_inc(s["mix_done"], 2)
            with pool.Fori(0, KC // 2) as i:
                for b in range(2):
                    for t, at, n in streams:
                        k = b * NS + t
                        pool.wait_ge(s["prod_done"], i * (2 * NS) + (k + 3))
                        nc.gpsimd.tensor_tensor(m.mix[:, bass.ds(i * 2 + b, 1), at:at + n].rearrange("p a n -> p (a n)"),
                                                s["t"][:, k % 2, 0, 0:n], s["t"][:, k % 2, 1, 0:n], ALU.add).then_inc(s["mix_done"], 1)


def out_loads(eng, l, w_out, early):
    w, loaded = early
    for g in range(2):
        eng.dma_start(w[:, g], w_out[l].rearrange("(c p) n -> p c n", p=P)[:, :, g * 4 * P:(g + 1) * 4 * P]).then_inc(loaded[g], 16)


def out_stage(nc, m, l, streams, early):
    w, loaded = early
    with stage(nc, f"out{l}", ["mm_done", "evac"]) as (block, s):
        @block.tensor
        def _(pe):
            for k in range(KC):
                if k % 4 == 0:
                    pe.wait_ge(loaded[k // 4], 16)
                if k >= 2:
                    pe.wait_ge(s["evac"], k - 1)
                for t, at, n in streams:
                    for c in range(KC):
                        last = nc.tensor.matmul(m.ps[:, 2 * (k % 2) + t, 0:n], w[:, k // 4, c, (k % 4) * P:(k % 4 + 1) * P],
                                                m.mix[:, c, at:at + n], start=c == 0, stop=c == KC - 1)
                last.then_inc(s["mm_done"], 1)

        @block.vector
        def _(dve):
            for k in range(KC):
                dve.wait_ge(s["mm_done"], k + 1)
                for t, at, n in streams:
                    r = m.resid[:, k, at:at + n]
                    last = nc.vector.scalar_tensor_tensor(r, m.ps[:, 2 * (k % 2) + t, 0:n], m.mod[:, l, t, 2 * KC + k:2 * KC + k + 1],
                                                          r, ALU.mult, ALU.add)
                last.then_inc(s["evac"], 1)


class Memory:
    pass


def chip_memory(nc, ctx):
    def sb(name, shape, dtype=F32):
        return ctx.enter_context(nc.sbuf_tensor(name, shape, dtype))

    m = Memory()
    m.resid = sb("resid", [P, KC, TOK])
    m.ident = sb("ident", [P, P])
    m.ones = sb("ones", [P, P])
    m.cols = sb("cols", [P, DEPTH, R_ALL])
    m.gcols = sb("gcols", [P, RG_ALL])
    m.sil = sb("sil", [P, KC, 32])
    m.mod = sb("mod", [P, DEPTH, 2, N_MOD * KC])
    m.gain = sb("gain", [P, DEPTH, 2, 2, KC])
    m.weight = sb("weight", [P, 2, TT])
    m.table = sb("table", [P, NE + overflow_blocks(TOK)], I32)
    m.over = sb("over", [P, 1 + overflow_blocks(TOK)], I32)
    m.ps = ctx.enter_context(nc.psum_tensor("ps", [P, 8, 512], F32))
    return m


def mixers(nc, m, l, a, consts, dram):
    last = l == DEPTH - 1
    streams = spans(not last)

    def buffer(scope, name, shape):
        return scope.enter_context(nc.sbuf_tensor(f"{name}{l}", shape, F32))

    def signals(name, n):
        return [nc.alloc_semaphore(f"{name}{l}_{k}") for k in range(n)]

    with ExitStack() as whole:
        m.u = buffer(whole, "u", [P, KC, TOK])
        m.yh = buffer(whole, "yh", [P, HC, TOK])
        qkv_early = buffer(whole, "w_qkv", [P, KC, QL + KVL]), signals("w_qkv_in", 1)[0]
        with ExitStack() as part:
            m.v = buffer(part, "v", [P, TT, HW])
            m.x1 = buffer(part, "x1", [P, TT, HW])
            m.x2 = buffer(part, "x2", [P, HC, TOK])
            conv_early = {name: (buffer(part, name, conv_shape(name)), signals(f"{name}_in", 1)[0]) for name in ("dft0", "h0")}
            with ExitStack() as first:
                hyena_early = buffer(first, "w_hy", [P, 2, KC, HW]), signals("w_hy_in", 2)

                def hyena_loads(sp):
                    for g in range(2):
                        hyena_in_loads(a["w_in"], l, hyena_early, g)(sp)

                def conv_loads(sp):
                    for name in conv_early:
                        conv_load(sp, conv_early, name, l, 0, consts, dram)

                def qkv_loads(sp):
                    w, loaded = qkv_early
                    sp.dma_start(w[:], a["w_in"][l].rearrange("(c p) n -> p c n", p=P)[:, :, Q0:KR0]).then_inc(loaded, 16)

                norm_stage(nc, m, f"norm1_{l}", m.u, spans(True), lambda t, c: m.gain[:, l, t, 0, c:c + 1],
                           lambda t, c: m.mod[:, l, t, c:c + 1], hyena_loads)
                hyena_in_stage(nc, m, l, a["w_in"], streams, hyena_early, conv_loads)
            conv_stage(nc, m, l, streams, consts, dram, conv_early, qkv_loads)
        m.ya = buffer(whole, "ya", [P, HC, TOK])
        merge_early = buffer(whole, "w_merge", [P, 2, MERGE_KW, P]), signals("w_merge_in", 2)
        with ExitStack() as part:
            m.qn = buffer(part, "qn", [P, QC, TOK])
            m.kvn = buffer(part, "kvn", [P, KVC, TOK])
            m.key = buffer(part, "key", [P, 2, TOK])
            m.vt = buffer(part, "vt", [P, TT, HEADS * VD])
            m.rope = buffer(part, "rope", [P, SEQ])
            heads_early = buffer(part, "wq", [P, 2, QC, P]), buffer(part, "wk", [P, 2, KVC, NOPE]), signals("heads_in", 2)

            def first_heads(sp):
                for h in range(2):
                    attention_loads(sp, l, 0, a, heads_early)(h)

            def first_merge(sp):
                for b in range(2):
                    merge_loads(sp, l, 0, b, a, merge_early)

            qkv_stage(nc, m, l, a["w_in"], a["w_ukv"], consts, streams, qkv_early, first_heads)
            attention_stage(nc, m, l, a, streams, heads_early, first_merge)
        m.mix = buffer(whole, "mix", [P, KC, TOK])
        out_early = buffer(whole, "w_out", [P, 2, KC, 4 * P]), signals("w_out_in", 2)
        merge_stage(nc, m, l, a, streams, merge_early, lambda sp: out_loads(sp, l, a["w_out"], out_early))
        out_stage(nc, m, l, streams, out_early)


def table_rows(a):
    def rows(v):
        return v.rearrange("(r p) -> r p", p=P)

    per_layer = [((R_G1, KC, rows(a["norm1_g"][l])), (R_G2, KC, rows(a["norm2_g"][l])), (R_ADA, N_MOD * KC, rows(a["b_ada"][l])),
                  (R_QG, QC, rows(a["q_norm_g"][l])), (R_KVG, KVC, rows(a["kv_norm_g"][l])),
                  (R_SCW, 9 * HC, a["sc_w"][l].rearrange("k (r p) -> (k r) p", p=P)), (R_SCB, 3 * HC, rows(a["sc_b"][l])))
                 for l in range(DEPTH)]
    return per_layer, ((RG_C, KC, rows(a["c"][0])), (RG_CC, KC, rows(a["c_ctx"])), (RG_F, KC, rows(a["final_g"])))


A_ALL = 2 * TOK
NO_ROW = A_ALL


def overflow_blocks(n_tok):
    return 2 * n_tok // SLOTS


def router_stage(nc, m, l, a, consts, streams, dram):
    n_tok = sum(n for _, _, n in streams)
    NT = n_tok // P
    NOV = overflow_blocks(n_tok)
    NB = NE + NOV
    QM = (n_tok - 1) // SLOTS
    R = NG + NE
    LOW = -3.0e38
    sems = ["consts_in", "wr_in", "bias_in", "tr_done", "lg_done", "tr_evac_a", "tr_evac_v", "lg_evac", "u_out0", "u_out1", "dve",
            "exps", "hot_done", "rank_done", "filled", "fill_out", "dest_done", "sc_out", "table_in"]
    bufs = [("wr", [P, KC, R]), ("bias", [P, R]), ("lg", [P, NT, R]), ("utok", [P, 2, D]), ("triu", [P, P]), ("iota", [P, 96]),
            ("gb", [P, NT, NG]), ("c", [P, NT, NG]), ("hot_g", [P, NT, NG]), ("e", [P, NT, NG]), ("leg", [P, NT, EG]),
            ("beg", [P, NT, EG]), ("val", [P, NT, EG]), ("hot1", [P, NT, EG]), ("hot2", [P, NT, EG]), ("big", [P, NT, NE]),
            ("sel", [P, 2, NT, NE]), ("both", [P, NT, NE]), ("before", [P, NT + 1, NE]), ("rank", [P, NT, NE]), ("cnt", [P, NE]), ("ovf", [P, NE]),
            ("incl", [P, NE]), ("base", [P, NE]), ("one", [P, NE]), ("r", [P, 16, NT]), ("ex", [P, 2, NT]),
            ("q", [P, 2, NT]), ("pos", [P, 2, NT]), ("eid", [P, 2, NT]), ("ob", [P, 2, NT]), ("z", [P, 2, NT]), ("dest", [P, 2, NT]),
            ("dest_i", [P, 2, NT], I32), ("num", [P, 2, NT]), ("num_i", [P, 2, NT], I32), ("fill", [SLOTS, NB], I32),
            ("cmp", [P, NOV, NE]), ("oe", [P, NOV])]
    table = dram["table"][l]
    with stage(nc, f"route{l}", sems, bufs) as (block, s):
        u_out = [s["u_out0"], s["u_out1"]]

        @block.sync
        def _(sp):
            sp.dma_start(s["wr"][:, :, 0:NG], a["w_router_g"][l].rearrange("(c p) n -> p c n", p=P)).then_inc(s["wr_in"], 16)
            sp.dma_start(s["wr"][:, :, NG:R], a["w_router_e"][l].rearrange("(c p) n -> p c n", p=P)).then_inc(s["wr_in"], 16)
            sp.dma_start(s["bias"][:, 0:NG], a["b_router_g"][l].partition_broadcast(P)).then_inc(s["bias_in"], 16)
            sp.dma_start(s["bias"][:, NG:R], a["b_router_e"][l].partition_broadcast(P)).then_inc(s["bias_in"], 16)
            sp.dma_start(s["triu"][:], consts["triu"]).then_inc(s["consts_in"], 16)
            sp.dma_start(s["iota"][:], consts["iota"]).then_inc(s["consts_in"], 16)
            sp.wait_ge(s["filled"], 1)
            sp.dma_start(table.rearrange("(s b) o -> s (b o)", b=NB), s["fill"][:]).then_inc(s["fill_out"], 16)
            for j in range(NT):
                sp.wait_ge(s["tr_evac_a"], j + 1)
                sp.wait_ge(s["tr_evac_v"], j + 1)
                for k in range(2):
                    sp.dma_start(dram["u"][k * TOK + j * P:k * TOK + (j + 1) * P], s["utok"][:, j % 2]).then_inc(u_out[j % 2], 16)
            sp.wait_ge(s["sc_out"], 16 * 2 * NT)
            sp.dma_start(m.table[0:SLOTS, 0:NB], table.rearrange("(s b) o -> s (b o)", b=NB)).then_inc(s["table_in"], 16)
            for k in range(2):
                sp.wait_ge(u_out[k], 16 * NT)
            sp.wait_ge(s["table_in"], 16)

        @block.gpsimd
        def _(pool):
            nc.gpsimd.memset(s["fill"][:], NO_ROW).then_inc(s["filled"], 1)
            pool.wait_ge(s["fill_out"], 16)
            pool.wait_ge(s["dest_done"], 2)
            for k in range(2):
                for j in range(NT):
                    nc.gpsimd.indirect_dma_start(out=table, out_offset=bass.IndirectOffsetOnAxis(ap=s["dest_i"][:, k, j:j + 1], axis=0),
                                                 in_=s["num_i"][:, k, j:j + 1], in_offset=None,
                                                 bounds_check=SLOTS * NB - 1, oob_is_err=False).then_inc(s["sc_out"], 16)
            pool.wait_ge(s["sc_out"], 16 * 2 * NT)

        @block.tensor
        def _(pe):
            pe.wait_ge(s["wr_in"], 32)
            for j in range(NT):
                if j >= 2:
                    pe.wait_ge(s["tr_evac_a"], j - 1)
                    pe.wait_ge(s["tr_evac_v"], j - 1)
                b = 2 * (j % 2)
                for c in range(KC):
                    last = nc.tensor.transpose(m.ps[:, b + c // 4, (c % 4) * P:(c % 4 + 1) * P], m.u[:, c, j * P:(j + 1) * P], m.ident[:])
                last.then_inc(s["tr_done"], 1)
                if j >= 2:
                    pe.wait_ge(s["lg_evac"], j - 1)
                for c in range(KC):
                    last = nc.tensor.matmul(m.ps[:, 4 + j % 2, 0:R], m.u[:, c, j * P:(j + 1) * P], s["wr"][:, c], start=c == 0, stop=c == KC - 1)
                last.then_inc(s["lg_done"], 1)
            pe.wait_ge(s["consts_in"], 32)
            pe.wait_ge(s["hot_done"], 1)
            nc.tensor.matmul(m.ps[:, 6, 0:NT * NE], s["triu"][:], s["both"][:].rearrange("p t e -> p (t e)"), start=True, stop=False)
            nc.tensor.matmul(m.ps[:, 6, 0:NT * NE], m.ones[:], s["before"][:, 0:NT].rearrange("p t e -> p (t e)"), start=False, stop=True)
            last = nc.tensor.matmul(m.ps[:, 7, 0:NE], m.ones[:], s["before"][:, NT], start=True, stop=True)
            last.then_inc(s["rank_done"], 1)

        @block.scalar
        def _(act):
            for j in range(NT):
                act.wait_ge(s["tr_done"], j + 1)
                if j >= 2:
                    act.wait_ge(u_out[j % 2], 32 * (j // 2))
                nc.scalar.activation(s["utok"][:, j % 2, 0:512], m.ps[:, 2 * (j % 2)], ACT.Copy).then_inc(s["tr_evac_a"], 1)
            act.wait_ge(s["exps"], 1)
            nc.scalar.activation(s["e"][:], s["e"][:], ACT.Exp).then_inc(s["exps"], 1)
            act.wait_ge(s["exps"], 3)
            nc.scalar.activation(s["ex"][:], s["ex"][:], ACT.Exp).then_inc(s["exps"], 1)

        @block.vector
        def _(dve):
            link = Chain(dve, s["dve"])
            nc.vector.memset(s["before"][:, 0], 0.0)
            for j in range(NT):
                dve.wait_ge(s["tr_done"], j + 1)
                if j >= 2:
                    dve.wait_ge(u_out[j % 2], 32 * (j // 2))
                nc.vector.tensor_copy(s["utok"][:, j % 2, 512:D], m.ps[:, 2 * (j % 2) + 1]).then_inc(s["tr_evac_v"], 1)
                dve.wait_ge(s["lg_done"], j + 1)
                nc.vector.tensor_copy(s["lg"][:, j], m.ps[:, 4 + j % 2, 0:R]).then_inc(s["lg_evac"], 1)
            dve.wait_ge(s["lg_evac"], NT)
            dve.wait_ge(s["bias_in"], 32)
            dve.wait_ge(s["consts_in"], 32)

            def over(ap, *shape):
                return ap.broadcast_to([P, *shape])

            def row(k):
                return s["r"][:, k]

            iota8 = over(s["iota"][:, None, 0:NG], NT, NG)

            def first_max(val, hot, k):
                link(nc.vector.tensor_reduce(row(k), val, axis=AX.X, op=ALU.max))
                link(nc.vector.tensor_tensor(s["c"][:], val, over(row(k)[:, :, None], NT, NG), ALU.is_equal))
                link(nc.vector.scalar_tensor_tensor(s["c"][:], s["c"][:], -64.0, iota8, ALU.mult, ALU.add))
                link(nc.vector.tensor_reduce(row(k), s["c"][:], axis=AX.X, op=ALU.min))
                link(nc.vector.tensor_tensor(hot, s["c"][:], over(row(k)[:, :, None], NT, NG), ALU.is_equal))

            def picked(out, val, hot):
                link(nc.vector.tensor_tensor(s["c"][:], val, hot, ALU.mult))
                link(nc.vector.tensor_reduce(out, s["c"][:], axis=AX.X, op=ALU.add))

            lg_g = s["lg"][:, :, 0:NG]
            link(nc.vector.tensor_tensor(s["gb"][:], lg_g, over(s["bias"][:, None, 0:NG], NT, NG), ALU.add))
            first_max(s["gb"][:], s["hot_g"][:], 0)
            link(nc.vector.tensor_reduce(row(1), lg_g, axis=AX.X, op=ALU.max))
            nc.vector.tensor_tensor(s["e"][:], lg_g, over(row(1)[:, :, None], NT, NG), ALU.subtract).then_inc(s["exps"], 1)
            dve.wait_ge(s["exps"], 2)
            link(nc.vector.tensor_reduce(row(2), s["e"][:], axis=AX.X, op=ALU.add))
            picked(row(3), s["e"][:], s["hot_g"][:])
            hot_over = over(s["hot_g"][:, :, :, None], NT, NG, EG)
            big4 = s["big"][:].rearrange("p t (g j) -> p t g j", g=NG)
            for src, dst in ((s["lg"][:, :, NG:R].rearrange("p t (g j) -> p t g j", g=NG), s["leg"]),
                             (over(s["bias"][:, NG:R].rearrange("p (t g j) -> p t g j", t=1, g=NG), NT, NG, EG), s["beg"])):
                link(nc.vector.tensor_tensor(big4, src, hot_over, ALU.mult))
                link(nc.vector.tensor_reduce(dst[:], s["big"][:].rearrange("p t (g j) -> p t j g", g=NG), axis=AX.X, op=ALU.add))
            link(nc.vector.tensor_tensor(s["val"][:], s["leg"][:], s["beg"][:], ALU.add))
            first_max(s["val"][:], s["hot1"][:], 4)
            link(nc.vector.scalar_tensor_tensor(s["val"][:], s["hot1"][:], LOW, s["val"][:], ALU.mult, ALU.add))
            first_max(s["val"][:], s["hot2"][:], 5)
            picked(s["ex"][:, 0], s["leg"][:], s["hot1"][:])
            picked(s["ex"][:, 1], s["leg"][:], s["hot2"][:])
            link(nc.vector.tensor_tensor(row(6), s["ex"][:, 0], s["ex"][:, 1], ALU.max))
            nc.vector.tensor_tensor(s["ex"][:], s["ex"][:], over(row(6)[:, None, :], 2, NT), ALU.subtract).then_inc(s["exps"], 1)
            for k, hot in enumerate((s["hot1"], s["hot2"])):
                last = nc.vector.tensor_tensor(s["sel"][:, k].rearrange("p t (g j) -> p t g j", g=NG), hot_over,
                                               over(hot[:, :, None, :], NT, NG, EG), ALU.mult)
            link(last)
            link(nc.vector.tensor_tensor(s["both"][:], s["sel"][:, 0], s["sel"][:, 1], ALU.add))
            link(nc.vector.tensor_copy(s["before"][:, 1], s["both"][:, 0]))
            for j in range(1, NT):
                last = nc.vector.tensor_tensor(s["before"][:, j + 1], s["before"][:, j], s["both"][:, j], ALU.add)
                if j < NT - 1:
                    link(last)
            last.then_inc(s["hot_done"], 1)
            dve.wait_ge(s["exps"], 4)
            link(nc.vector.tensor_tensor(row(7), s["ex"][:, 0], s["ex"][:, 1], ALU.add))
            link(nc.vector.tensor_tensor(row(7), row(7), row(2), ALU.mult))
            link(nc.vector.reciprocal(row(8), row(7)))
            link(nc.vector.tensor_tensor(row(8), row(8), row(3), ALU.mult))
            nc.vector.tensor_tensor(m.weight[:, :, 0:NT], s["ex"][:], over(row(8)[:, None, :], 2, NT), ALU.mult)
            dve.wait_ge(s["rank_done"], 1)
            nc.vector.tensor_copy(s["rank"][:], m.ps[:, 6, 0:NT * NE].rearrange("p (t e) -> p t e", e=NE))
            nc.vector.memset(s["one"][:], 1.0)
            link(nc.vector.tensor_copy(s["cnt"][:], m.ps[:, 7, 0:NE]))
            link(nc.vector.tensor_scalar(s["ovf"][:], s["cnt"][:], float(SLOTS), None, ALU.is_gt))
            for q in range(2, QM + 1):
                link(nc.vector.scalar_tensor_tensor(s["ovf"][:], s["cnt"][:], float(q * SLOTS), s["ovf"][:], ALU.is_gt, ALU.add))
            link(nc.vector.tensor_tensor_scan(s["incl"][:], s["one"][:], s["ovf"][:], 0.0, ALU.mult, ALU.add))
            link(nc.vector.tensor_tensor(s["base"][:], s["incl"][:], s["ovf"][:], ALU.subtract))
            for k in range(2):
                for vals, out in ((s["rank"][:], s["pos"]), (over(s["iota"][:, None, 0:NE], NT, NE), s["eid"]), (over(s["base"][:, None, :], NT, NE), s["ob"])):
                    link(nc.vector.tensor_tensor(s["big"][:], s["sel"][:, k], vals, ALU.mult))
                    link(nc.vector.tensor_reduce(out[:, k], s["big"][:], axis=AX.X, op=ALU.add))
            link(nc.vector.tensor_scalar(s["q"][:], s["pos"][:], float(SLOTS), None, ALU.is_ge))
            link(nc.vector.tensor_copy(s["z"][:], s["q"][:]))
            for q in range(2, QM + 1):
                link(nc.vector.scalar_tensor_tensor(s["q"][:], s["pos"][:], float(q * SLOTS), s["q"][:], ALU.is_ge, ALU.add))
            link(nc.vector.scalar_tensor_tensor(s["ob"][:], s["ob"][:], float(NE - 1), s["q"][:], ALU.add, ALU.add))
            link(nc.vector.tensor_tensor(s["ob"][:], s["ob"][:], s["eid"][:], ALU.subtract))
            link(nc.vector.tensor_tensor(s["ob"][:], s["ob"][:], s["z"][:], ALU.mult))
            link(nc.vector.tensor_tensor(s["ob"][:], s["ob"][:], s["eid"][:], ALU.add))
            link(nc.vector.scalar_tensor_tensor(s["pos"][:], s["q"][:], -float(SLOTS), s["pos"][:], ALU.mult, ALU.add))
            link(nc.vector.scalar_tensor_tensor(s["dest"][:], s["pos"][:], float(NB), s["ob"][:], ALU.mult, ALU.add))
            nc.vector.tensor_copy(s["dest_i"][:], s["dest"][:]).then_inc(s["dest_done"], 1)
            for k in range(2):
                for j in range(NT):
                    last = nc.vector.tensor_scalar_add(s["num"][:, k, j:j + 1], s["iota"][:, 88:89], float(k * TOK + j * P))
            link(last)
            nc.vector.tensor_copy(s["num_i"][:], s["num"][:]).then_inc(s["dest_done"], 1)
            link(nc.vector.tensor_tensor(s["cmp"][:], over(s["incl"][:, None, :], NOV, NE),
                                         over(s["iota"][:, 64:64 + NOV][:, :, None], NOV, NE), ALU.is_le))
            link(nc.vector.tensor_reduce(s["oe"][:], s["cmp"][:], axis=AX.X, op=ALU.add))
            link(nc.vector.tensor_scalar(s["oe"][:], s["oe"][:], float(NE - 1), None, ALU.min))
            nc.vector.tensor_copy(m.over[:, 1:1 + NOV], s["oe"][:])
            nc.vector.tensor_copy(m.over[:, 0:1], s["incl"][:, NE - 1:NE])


def gate_up(nc, ps, xt, wgu):
    for c in range(KC):
        for k in range(2):
            last = nc.tensor.matmul(ps[k * SLOTS:(k + 1) * SLOTS, 0:DE], xt[:, c], wgu[:, k, c], start=c == 0, stop=c == KC - 1)
    return last


def down_both(nc, ps, ht, wd):
    for c in range(2):
        for k in range(2):
            last = nc.tensor.matmul(ps[k * SLOTS:(k + 1) * SLOTS, 0:512], ht[:, c], wd[:, c, k * 512:(k + 1) * 512],
                                    start=c == 0, stop=c == 1)
    return last


def strided_transposes(nc, ps, src, n, ident):
    for c in range(n):
        last = nc.tensor.transpose(ps[:, c * SLOTS:(c + 1) * SLOTS], src.rearrange("p (q c) -> p c q", c=n)[:, c], ident[0:SLOTS, 0:SLOTS])
    return last


def load_expert(eng, a, l, e, wgu, wd, sem):
    for k, name in enumerate(("w_gate_e", "w_up_e")):
        eng.dma_start(wgu[:, k], a[name][l, bass.ds(e, 1)].rearrange("o (p c) n -> p (o c) n", p=P)).then_inc(sem, 16)
    eng.dma_start(wd, a["w_down_e"][l, bass.ds(e, 1)].rearrange("o (p c) n -> p (o c) n", p=P)).then_inc(sem, 16)


def moe_stage(nc, m, l, a, dram, ring):
    wgu, wd, loaded = ring
    sems = ["g0", "g1", "g2", "g3", "s0", "s1", "zeroed", "gu_done", "xt_done", "ht_done", "down_done",
            "silu_done", "x_evac", "ya", "h_done", "ht_evac", "yb", "turns"]
    bufs = [("xg", [SLOTS, 4, D]), ("xt", [P, 2, KC, SLOTS]), ("sg", [P, 2, DE]), ("h", [SLOTS, 2, DE]), ("ht", [P, 2, 2, SLOTS]),
            ("y", [SLOTS, 2, D])]
    with stage(nc, f"moe{l}", sems, bufs) as (block, s):
        gathered, scattered = [s["g0"], s["g1"], s["g2"], s["g3"]], [s["s0"], s["s1"]]
        xg, xt, sg, h, ht, y = s["xg"], s["xt"], s["sg"], s["h"], s["ht"], s["y"]

        def wait(eng, sem, n):
            if not isinstance(n, int) or n > 0:
                eng.wait_ge(sem, n)

        def rounds(eng, body):
            for b in range(RU):
                body(b, b, 0)
            with eng.Fori(1, NE // RU - 1) as i:
                for b in range(RU):
                    body(i * RU + b, b, i)
            for b in range(RU):
                body(NE - RU + b, b, NE // RU - 1)

        def inner(j):
            return not isinstance(j, int)

        @block.sync
        def _(sp):
            def load(j, b, r):
                if inner(j) or j >= RU:
                    wait(sp, s["down_done"], j - (RU - 1))
                    load_expert(sp, a, l, j, wgu[:, b], wd[:, b], loaded[b])

            rounds(sp, load)

        @block.gpsimd
        def _(pool):
            def gather(j):
                if j < 4:
                    nc.gpsimd.memset(xg[:, j], 0.0).then_inc(s["zeroed"], 1)
                    pool.wait_ge(s["zeroed"], j + 1)
                if j >= 4:
                    pool.wait_ge(s["xt_done"], j - 3)
                nc.gpsimd.indirect_dma_start(out=xg[:, j % 4], out_offset=None, in_=dram["u"],
                                             in_offset=bass.IndirectOffsetOnAxis(ap=m.table[0:SLOTS, j:j + 1], axis=0),
                                             bounds_check=A_ALL - 1, oob_is_err=False).then_inc(gathered[j % 4], 16)

            def scatter(j):
                pool.wait_ge(s["ya"], j + 1)
                pool.wait_ge(s["yb"], j + 1)
                nc.gpsimd.indirect_dma_start(out=dram["y"], out_offset=bass.IndirectOffsetOnAxis(ap=m.table[0:SLOTS, j:j + 1], axis=0),
                                             in_=y[:, j % 2], in_offset=None,
                                             bounds_check=A_ALL - 1, oob_is_err=False).then_inc(scattered[j % 2], 16)

            for j in range(NE + 3):
                if j < NE:
                    gather(j)
                if j >= 3:
                    scatter(j - 3)
            for b in range(2):
                pool.wait_ge(scattered[b], 16 * (NE // 2))

        @block.tensor
        def _(pe):
            def x_transposes(j, b, r):
                wait(pe, gathered[b], r * 16 + 16)
                wait(pe, s["x_evac"], j - 1)
                pe.sem_inc(s["turns"], 1)
                strided_transposes(nc, m.ps[:, 2 + b % 2], xg[:, b], KC, m.ident).then_inc(s["xt_done"], 1)

            def down(j, b):
                wait(pe, s["ht_evac"], j + 1)
                wait(pe, s["ya"], j - 1)
                wait(pe, s["yb"], j - 1)
                down_both(nc, m.ps[:, 5 + b % 2], ht[:, b % 2], wd[:, b]).then_inc(s["down_done"], 1)

            def body(j, b, r):
                wait(pe, loaded[b], r * 48 + 48)
                wait(pe, s["x_evac"], j + 1)
                wait(pe, s["h_done"], j - 1)
                gate_up(nc, m.ps[:, b % 2], xt[:, b % 2], wgu[:, b]).then_inc(s["gu_done"], 1)
                if inner(j) or j + 1 < NE:
                    x_transposes(j + 1, (b + 1) % RU, r + (b + 1) // RU)
                if inner(j) or j >= 1:
                    down(j - 1, (b - 1) % RU)
                wait(pe, s["h_done"], j + 1)
                wait(pe, s["ht_evac"], j)
                pe.sem_inc(s["turns"], 1)
                strided_transposes(nc, m.ps[:, 4], h[:, b % 2], 2, m.ident).then_inc(s["ht_done"], 1)

            x_transposes(0, 0, 0)
            rounds(pe, body)
            down(NE - 1, RU - 1)

        def copy_y(eng, sem, copy, half):
            def run(j, b):
                wait(eng, s["down_done"], j + 1)
                if inner(j):
                    eng.wait_ge(scattered[b % 2], (j - (b % 2)) * 8)
                else:
                    wait(eng, scattered[b % 2], 16 * (j // 2))
                copy(y[:, b % 2, half * 512:(half + 1) * 512], m.ps[half * SLOTS:(half + 1) * SLOTS, 5 + b % 2]).then_inc(sem, 1)
            return run

        @block.scalar
        def _(act):
            def copy(out, in_):
                return nc.scalar.activation(out, in_, ACT.Copy)

            y_half = copy_y(act, s["ya"], copy, 0)

            def x_copy(j, b):
                wait(act, s["xt_done"], j + 1)
                wait(act, s["gu_done"], j - 1)
                copy(xt[:, b % 2], m.ps[:, 2 + b % 2].rearrange("p (c q) -> p c q", c=KC)).then_inc(s["x_evac"], 1)

            def body(j, b, r):
                wait(act, s["gu_done"], j + 1)
                wait(act, s["h_done"], j - 1)
                nc.scalar.activation(sg[SLOTS:2 * SLOTS, b % 2], m.ps[0:SLOTS, b % 2, 0:DE], ACT.Silu).then_inc(s["silu_done"], 1)
                if inner(j) or j + 1 < NE:
                    x_copy(j + 1, b + 1)
                if inner(j) or j >= 1:
                    y_half(j - 1, (b - 1) % RU)

            x_copy(0, 0)
            rounds(act, body)
            y_half(NE - 1, RU - 1)

        @block.vector
        def _(dve):
            y_half = copy_y(dve, s["yb"], nc.vector.tensor_copy, 1)

            def body(j, b, r):
                wait(dve, s["silu_done"], j + 1)
                wait(dve, s["ht_done"], j - 1)
                nc.vector.tensor_tensor(h[:, b % 2], m.ps[SLOTS:2 * SLOTS, b % 2, 0:DE], sg[SLOTS:2 * SLOTS, b % 2],
                                        ALU.mult).then_inc(s["h_done"], 1)
                if inner(j) or j >= 1:
                    y_half(j - 1, (b - 1) % RU)
                wait(dve, s["ht_done"], j + 1)
                wait(dve, s["down_done"], j - 1)
                nc.vector.tensor_copy(ht[:, b % 2], m.ps[:, 4, 0:2 * SLOTS].rearrange("p (c q) -> p c q", c=2)).then_inc(s["ht_evac"], 1)

            rounds(dve, body)
            y_half(NE - 1, RU - 1)


def overflow_stage(nc, m, l, a, dram, n_tok):
    NOV = overflow_blocks(n_tok)
    sems = ["w_in", "idx_done", "g_in", "sc_out", "pe_done", "x_evac", "silu_done", "h_done", "ht_evac", "y_evac", "zeroed", "turns",
            "block_done"]
    bufs = [("wgu", [P, 2, KC, DE]), ("wd", [P, 2, D]), ("xg", [SLOTS, D]), ("xt", [P, KC, SLOTS]), ("sg", [P, DE]),
            ("h", [SLOTS, DE]), ("ht", [P, 2, SLOTS]), ("y", [SLOTS, D]), ("idx", [SLOTS, 1], I32)]
    with stage(nc, f"over{l}", sems, bufs) as (block, s):
        def blocks(eng, body):
            n = eng.value_load(m.over[0:1, 0:1], min_val=0, max_val=NOV)
            with eng.If(n > 0):
                with eng.Fori(0, NOV) as i:
                    with eng.If(i < n):
                        body(i)

        @block.sync
        def _(sp):
            sp.sem_inc(s["pe_done"], 4)

            def body(i):
                e = sp.value_load(m.over[0:1, bass.ds(i + 1, 1)], min_val=0, max_val=NE - 1)
                sp.wait_ge(s["pe_done"], i * 4 + 4)
                load_expert(sp, a, l, e, s["wgu"], s["wd"][:], s["w_in"])

            blocks(sp, body)

        @block.gpsimd
        def _(pool):
            nc.gpsimd.memset(s["xg"][:], 0.0).then_inc(s["zeroed"], 1)
            pool.wait_ge(s["zeroed"], 1)

            def body(i):
                at = bass.IndirectOffsetOnAxis(ap=s["idx"][:, 0:1], axis=0)
                pool.wait_ge(s["idx_done"], i + 1)
                pool.sem_inc(s["turns"], 1)
                nc.gpsimd.indirect_dma_start(out=s["xg"][:], out_offset=None, in_=dram["u"], in_offset=at,
                                             bounds_check=A_ALL - 1, oob_is_err=False).then_inc(s["g_in"], 16)
                pool.wait_ge(s["y_evac"], i + 1)
                pool.sem_inc(s["turns"], 1)
                nc.gpsimd.indirect_dma_start(out=dram["y"], out_offset=at, in_=s["y"][:], in_offset=None,
                                             bounds_check=A_ALL - 1, oob_is_err=False).then_inc(s["sc_out"], 16)
                pool.wait_ge(s["sc_out"], i * 16 + 16)
                pool.sem_inc(s["block_done"], 1)

            pool.sem_inc(s["block_done"], 1)
            blocks(pool, body)

        @block.tensor
        def _(pe):
            def body(i):
                pe.wait_ge(s["g_in"], i * 16 + 16)
                pe.sem_inc(s["turns"], 1)
                strided_transposes(nc, m.ps[:, 0], s["xg"][:], KC, m.ident).then_inc(s["pe_done"], 1)
                pe.wait_ge(s["w_in"], i * 48 + 48)
                pe.wait_ge(s["x_evac"], i + 1)
                gate_up(nc, m.ps[:, 1], s["xt"], s["wgu"]).then_inc(s["pe_done"], 1)
                pe.wait_ge(s["h_done"], i + 1)
                pe.sem_inc(s["turns"], 1)
                strided_transposes(nc, m.ps[:, 2], s["h"][:], 2, m.ident).then_inc(s["pe_done"], 1)
                pe.wait_ge(s["ht_evac"], i + 1)
                down_both(nc, m.ps[:, 3], s["ht"], s["wd"]).then_inc(s["pe_done"], 1)

            blocks(pe, body)

        @block.scalar
        def _(act):
            def body(i):
                act.wait_ge(s["pe_done"], i * 4 + 6)
                nc.scalar.activation(s["sg"][SLOTS:2 * SLOTS], m.ps[0:SLOTS, 1, 0:DE], ACT.Silu).then_inc(s["silu_done"], 1)

            blocks(act, body)

        @block.vector
        def _(dve):
            def body(i):
                dve.wait_ge(s["block_done"], i + 1)
                nc.vector.tensor_scalar(s["idx"][:], m.table[0:SLOTS, bass.ds(i + NE, 1)], 0.0, None, ALU.add).then_inc(s["idx_done"], 1)
                dve.wait_ge(s["pe_done"], i * 4 + 5)
                nc.vector.tensor_copy(s["xt"][:], m.ps[:, 0].rearrange("p (c q) -> p c q", c=KC)).then_inc(s["x_evac"], 1)
                dve.wait_ge(s["silu_done"], i + 1)
                nc.vector.tensor_tensor(s["h"][:], m.ps[SLOTS:2 * SLOTS, 1, 0:DE], s["sg"][SLOTS:2 * SLOTS], ALU.mult).then_inc(s["h_done"], 1)
                dve.wait_ge(s["pe_done"], i * 4 + 7)
                nc.vector.tensor_copy(s["ht"][:], m.ps[:, 2, 0:2 * SLOTS].rearrange("p (c q) -> p c q", c=2)).then_inc(s["ht_evac"], 1)
                dve.wait_ge(s["pe_done"], i * 4 + 8)
                nc.vector.tensor_copy(s["y"][:, 0:512], m.ps[0:SLOTS, 3])
                nc.vector.tensor_copy(s["y"][:, 512:D], m.ps[SLOTS:2 * SLOTS, 3]).then_inc(s["y_evac"], 1)

            blocks(dve, body)


def combine_stage(nc, m, l, dram, streams):
    work = [(t, at // P + j) for t, at, n in streams for j in range(n // P)]
    with stage(nc, f"comb{l}", ["y0", "y1", "y2", "y3", "half_done", "sum_done", "tr_done", "evac"],
               [("y", [P, 4, 2, D]), ("c", [P, 2, D])]) as (block, s):
        loaded = [s["y0"], s["y1"], s["y2"], s["y3"]]

        @block.sync
        def _(sp):
            for j, (t, tile) in enumerate(work):
                if j >= 4:
                    sp.wait_ge(s["sum_done"], j - 3)
                for k in range(2):
                    at = k * TOK + tile * P
                    sp.dma_start(s["y"][:, j % 4, k], dram["y"][at:at + P]).then_inc(loaded[j % 4], 16)

        @block.scalar
        def _(act):
            for j, (t, tile) in enumerate(work):
                act.wait_ge(loaded[j % 4], 32 * (j // 4 + 1))
                if j >= 2:
                    act.wait_ge(s["tr_done"], j - 1)
                nc.scalar.mul(s["c"][:, j % 2], s["y"][:, j % 4, 0], m.weight[:, 0, tile:tile + 1]).then_inc(s["half_done"], 1)

        @block.tensor
        def _(pe):
            for j, (t, tile) in enumerate(work):
                pe.wait_ge(s["sum_done"], j + 1)
                if j >= 2:
                    pe.wait_ge(s["evac"], j - 1)
                for c in range(KC):
                    last = nc.tensor.transpose(m.ps[:, 2 * (j % 2) + c // 4, (c % 4) * P:(c % 4 + 1) * P], s["c"][:, j % 2, c * P:(c + 1) * P], m.ident[:])
                last.then_inc(s["tr_done"], 1)

        @block.vector
        def _(dve):
            def add(j):
                t, tile = work[j]
                dve.wait_ge(s["tr_done"], j + 1)
                for c in range(KC):
                    r = m.resid[:, c, tile * P:(tile + 1) * P]
                    last = nc.vector.scalar_tensor_tensor(r, m.ps[:, 2 * (j % 2) + c // 4, (c % 4) * P:(c % 4 + 1) * P],
                                                          m.mod[:, l, t, 5 * KC + c:5 * KC + c + 1], r, ALU.mult, ALU.add)
                last.then_inc(s["evac"], 1)

            for j, (t, tile) in enumerate(work):
                dve.wait_ge(s["half_done"], j + 1)
                nc.vector.scalar_tensor_tensor(s["c"][:, j % 2], s["y"][:, j % 4, 1], m.weight[:, 1, tile:tile + 1], s["c"][:, j % 2],
                                               ALU.mult, ALU.add).then_inc(s["sum_done"], 1)
                if j >= 1:
                    add(j - 1)
            add(len(work) - 1)


def store_stage(nc, m, out):
    with stage(nc, "store", ["tr_done", "evac", "out0", "out1"], [("o", [P, 2, D])]) as (block, s):
        @block.tensor
        def _(pe):
            for j in range(XT):
                if j >= 2:
                    pe.wait_ge(s["evac"], j - 1)
                for c in range(KC):
                    last = nc.tensor.transpose(m.ps[:, 2 * (j % 2) + c // 4, (c % 4) * P:(c % 4 + 1) * P], m.u[:, c, j * P:(j + 1) * P], m.ident[:])
                last.then_inc(s["tr_done"], 1)

        @block.vector
        def _(dve):
            for j in range(XT):
                dve.wait_ge(s["tr_done"], j + 1)
                if j >= 2:
                    dve.wait_ge((s["out0"], s["out1"])[j % 2], 16 * (j // 2))
                nc.vector.tensor_copy(s["o"][:, j % 2], m.ps[:, 2 * (j % 2):2 * (j % 2) + 2].rearrange("p b k -> p (b k)")).then_inc(s["evac"], 1)

        @block.sync
        def _(sp):
            for j in range(XT):
                sp.wait_ge(s["evac"], j + 1)
                sp.dma_start(out[0, j * P:(j + 1) * P], s["o"][:, j % 2]).then_inc((s["out0"], s["out1"])[j % 2], 16)
            for k in range(2):
                sp.wait_ge((s["out0"], s["out1"])[k], 16 * (XT // 2))


def experts(nc, m, l, a, consts, dram):
    streams = spans(l < DEPTH - 1)
    n_tok = sum(n for _, _, n in streams)
    with ExitStack() as whole:
        wgu = whole.enter_context(nc.sbuf_tensor(f"wgu{l}", [P, RU, 2, KC, DE], F32))
        wd = whole.enter_context(nc.sbuf_tensor(f"wd{l}", [P, RU, 2, D], F32))
        ring = wgu, wd, [nc.alloc_semaphore(f"expert_in{l}_{b}") for b in range(RU)]

        def first_round(sp):
            for b in range(RU):
                load_expert(sp, a, l, b, wgu[:, b], wd[:, b], ring[2][b])

        with nc.sbuf_tensor(f"u2_{l}", [P, KC, TOK], F32) as u:
            m.u = u
            norm_stage(nc, m, f"norm2_{l}", m.u, streams, lambda t, c: m.gain[:, l, t, 1, c:c + 1],
                       lambda t, c: m.mod[:, l, t, 3 * KC + c:3 * KC + c + 1], first_round)
            router_stage(nc, m, l, a, consts, streams, dram)
        moe_stage(nc, m, l, a, dram, ring)
    overflow_stage(nc, m, l, a, dram, n_tok)
    combine_stage(nc, m, l, dram, streams)


def trunk(nc, a, consts, out):
    with ExitStack() as ctx:
        m = chip_memory(nc, ctx)
        dram = {"u": nc.dram_tensor("rows_in", [A_ALL, D], F32).ap(), "y": nc.dram_tensor("rows_out", [A_ALL, D], F32).ap(),
                "table": [nc.dram_tensor(f"slots{l}", [SLOTS * (NE + overflow_blocks(TOK if l < DEPTH - 1 else SEQ)), 1],
                                         I32).ap() for l in range(DEPTH)],
                "h": [[nc.dram_tensor(f"transfer{l}_{t}", [2, P, 2, (SEQ, CTX)[t] // P // 2, 2, HW], F32).ap() for t in range(2)]
                      for l in range(DEPTH)]}
        per_layer, shared = table_rows(a)
        with ExitStack() as scope:
            early = prepare_buffers(nc, scope)
            load_stage(nc, m, a["x"], a["ctx"], per_layer, shared, consts, lambda sp: prepare_loads(sp, a, consts, early))
            prepare_stage(nc, m, a, consts, dram, early)
        for l in range(DEPTH):
            mixers(nc, m, l, a, consts, dram)
            experts(nc, m, l, a, consts, dram)
        with nc.sbuf_tensor("u_out", [P, KC, TOK], F32) as u:
            m.u = u
            norm_stage(nc, m, "norm_out", m.u, spans(False), lambda t, c: m.gcols[:, RG_F + c:RG_F + c + 1], None)
            store_stage(nc, m, out)


NAMES = ["x", "c", "ctx", "c_ctx", "w_ada", "b_ada", "norm1_g", "w_in", "q_norm_g", "kv_norm_g", "w_uq", "w_ukv", "sc_w", "sc_b",
         "flt_w1", "flt_b1", "flt_freq", "flt_w2", "flt_b2", "flt_w3", "flt_bias", "w_hy_o", "w_mla_o", "w_out", "norm2_g",
         "w_router_g", "b_router_g", "w_router_e", "b_router_e", "w_gate_e", "w_up_e", "w_down_e", "final_g"]


def kernel(**inputs):
    import concourse.bacc as bacc
    from concourse.bass_utils import run_bass_kernel_spmd

    nc = bacc.Bacc("TRN2", target_bir_lowering=False, num_devices=1)
    arrays, a, consts = {}, {}, {}
    for name in NAMES:
        arrays[f"in_{name}"] = np.ascontiguousarray(inputs[name])
        a[name] = nc.dram_tensor(f"in_{name}", arrays[f"in_{name}"].shape, F32, kind="ExternalInput").ap()
    for name, value in layout_constants().items():
        arrays[f"const_{name}"] = value
        consts[name] = nc.dram_tensor(f"const_{name}", value.shape, F32, kind="ExternalInput").ap()
    out = nc.dram_tensor("out", (1, SEQ, D), F32, kind="ExternalOutput").ap()
    trunk(nc, a, consts, out)
    r = run_bass_kernel_spmd(nc, [arrays], core_ids=[0])
    return r.results[0]["out"]
```
